# Optimizing a Trainium2 kernel written in Bass

```python
import jax, jax.numpy as jnp
from jax import lax
import numpy as np
import math
import jax
import jax.numpy as jnp

D_MODEL = 1024
BATCH = 1
SEQ = 1024
DEPTH = 2

CONV_WIDTH = D_MODEL // 2
CONV_HEADS = 8
CONV_K = 3
POOL_WIDTH = D_MODEL // 2
POOL_WINDOWS = (2, 4, 8, 16)
POOL_GROUPS = len(POOL_WINDOWS)
POOL_GROUP_DIM = POOL_WIDTH // POOL_GROUPS
MIX_WIDTH = CONV_WIDTH + POOL_WIDTH
IN_COLS = 4 * CONV_WIDTH + 2 * POOL_WIDTH
NORM_EPS = 1e-6


def rms_norm(x, g):
    xf = x.astype(jnp.float32)
    y = xf * lax.rsqrt(jnp.mean(xf * xf, axis=-1, keepdims=True) + NORM_EPS)
    return (y * g.astype(jnp.float32)).astype(x.dtype)

def causal_depthwise_conv(z, w):
    C = z.shape[-1]
    return lax.conv_general_dilated(
        z, w[:, None, :].astype(z.dtype),
        window_strides=(1,), padding=[(CONV_K - 1, 0)],
        dimension_numbers=("NWC", "WIO", "NWC"),
        feature_group_count=C)

def causal_multiscale_pool(p, w_pool, pool_scale):
    B, T, _ = p.shape
    pf = p.astype(jnp.float32)
    pos = jnp.arange(1, T + 1, dtype=jnp.float32)[None, :, None]
    outs = []
    for g, w in enumerate(POOL_WINDOWS):
        pg = pf[..., g * POOL_GROUP_DIM:(g + 1) * POOL_GROUP_DIM]
        s = jnp.cumsum(pg, axis=1)
        lag = jnp.pad(s, ((0, 0), (w, 0), (0, 0)))[:, :T]
        mean = (s - lag) / jnp.minimum(pos, float(w))
        outs.append(mean - pg)
    pooled = jnp.stack(outs, axis=2).astype(p.dtype)
    mixed = jnp.einsum("btgc,gcd->btgd", pooled, w_pool)
    return mixed.reshape(B, T, POOL_WIDTH) * pool_scale

def first_inputs(seed: int = 0) -> dict:
    key = jax.random.key(seed)
    ks = jax.random.split(key, 12)
    f32 = jnp.float32
    x = jax.random.normal(ks[0], (BATCH, SEQ, D_MODEL), f32)
    c = jax.random.normal(ks[1], (BATCH, D_MODEL), f32)
    w_ada = jax.random.normal(ks[2], (DEPTH, D_MODEL, 3 * D_MODEL), f32) * D_MODEL ** -0.5
    b_ada = 0.01 * jax.random.normal(ks[3], (DEPTH, 3 * D_MODEL), f32)
    g_pre = 1.0 + 0.02 * jax.random.normal(ks[4], (DEPTH, D_MODEL), f32)
    w_in = jax.random.normal(ks[5], (DEPTH, D_MODEL, IN_COLS), f32) * D_MODEL ** -0.5
    w_conv = jax.random.normal(ks[6], (DEPTH, CONV_K, CONV_WIDTH), f32) * CONV_K ** -0.5
    w_pool = jax.random.normal(ks[7], (DEPTH, POOL_GROUPS, POOL_GROUP_DIM, POOL_GROUP_DIM), f32) * POOL_GROUP_DIM ** -0.5
    pool_scale = 1.0 + 0.1 * jax.random.normal(ks[8], (DEPTH, POOL_WIDTH), f32)
    w_out = jax.random.normal(ks[9], (DEPTH, MIX_WIDTH, D_MODEL), f32) * MIX_WIDTH ** -0.5
    g_post = 1.0 + 0.02 * jax.random.normal(ks[10], (DEPTH, D_MODEL), f32)
    return {"x": x, "c": c, "w_ada": w_ada, "b_ada": b_ada, "g_pre": g_pre, "w_in": w_in,
            "w_conv": w_conv, "w_pool": w_pool, "pool_scale": pool_scale,
            "w_out": w_out, "g_post": g_post}

def first_block(x, c, w_ada, b_ada, g_pre, w_in, w_conv, w_pool, pool_scale, w_out, g_post):
    B, T, D = x.shape
    c_act = jax.nn.silu(c)
    cw = CONV_WIDTH
    for l in range(DEPTH):
        mod = c_act @ w_ada[l] + b_ada[l]
        shift, scale, gate = jnp.split(mod, 3, axis=-1)
        h = rms_norm(x, g_pre[l]) * (1.0 + scale[:, None, :]) + shift[:, None, :]
        proj = h @ w_in[l]
        u_a = proj[..., 0 * cw:1 * cw]
        b_a = proj[..., 1 * cw:2 * cw]
        c_a = proj[..., 2 * cw:3 * cw]
        gate_a = proj[..., 3 * cw:4 * cw]
        o = 4 * cw
        u_p = proj[..., o:o + POOL_WIDTH]
        gate_p = proj[..., o + POOL_WIDTH:o + 2 * POOL_WIDTH]
        y_a = b_a * causal_depthwise_conv(c_a * u_a, w_conv[l]) * jax.nn.silu(gate_a)
        y_p = causal_multiscale_pool(u_p, w_pool[l], pool_scale[l]) * jax.nn.silu(gate_p)
        y = jnp.concatenate([y_a, y_p], axis=-1) @ w_out[l]
        x = x + gate[:, None, :] * rms_norm(y, g_post[l])
    return x


DEPTH_2 = 1

CHUNK = 64
Q_BLOCK = 128
GMLP_BLOCK = 128

A_GROUPS = 4
A_GDIM = 64
A_WIDTH = A_GROUPS * A_GDIM
B_HEADS = 4
B_QK_DIM = 64
B_V_DIM = 2 * B_QK_DIM
B_WIDTH = B_HEADS * B_V_DIM
C_HEADS = 4
C_HEAD_DIM = 64
C_WIDTH = C_HEADS * C_HEAD_DIM
IDX_HEADS = 8
IDX_DIM = 32
TOPK_MAX = 256
MIX_WIDTH_2 = A_WIDTH + B_WIDTH + C_WIDTH

FFN_HIDDEN = -(-8 * D_MODEL // (3 * 256)) * 256

OFF_A_U = 0
OFF_A_V = OFF_A_U + A_WIDTH
OFF_B_Q = OFF_A_V + A_WIDTH
OFF_B_K = OFF_B_Q + B_HEADS * 2 * B_QK_DIM
OFF_B_V = OFF_B_K + B_HEADS * 2 * B_QK_DIM
OFF_C_Q = OFF_B_V + B_WIDTH
OFF_C_K = OFF_C_Q + C_WIDTH
OFF_C_V = OFF_C_K + C_WIDTH
OFF_I_Q = OFF_C_V + C_WIDTH
OFF_I_K = OFF_I_Q + IDX_HEADS * IDX_DIM
OFF_I_W = OFF_I_K + IDX_DIM
IN_WIDTH = OFF_I_W + IDX_HEADS

DEEPNORM_ALPHA = (2 * DEPTH_2) ** 0.25
DEEPNORM_BETA = (8 * DEPTH_2) ** -0.25
LN_EPS = 1e-5


def layer_norm(x, g, b):
    xf = x.astype(jnp.float32)
    mu = jnp.mean(xf, axis=-1, keepdims=True)
    xc = xf - mu
    var = jnp.mean(xc * xc, axis=-1, keepdims=True)
    return (xc * lax.rsqrt(var + LN_EPS) * g.astype(jnp.float32) + b.astype(jnp.float32)).astype(x.dtype)

def rms_norm_2(x, g):
    xf = x.astype(jnp.float32)
    ms = jnp.mean(xf * xf, axis=-1, keepdims=True)
    return (xf * lax.rsqrt(ms + LN_EPS) * g.astype(jnp.float32)).astype(x.dtype)

def alibi_slopes(n):
    return jnp.asarray([2.0 ** (-8.0 * (h + 1) / n) for h in range(n)], dtype=jnp.float32)

def to_blocks(a, size):
    bn, s = a.shape[:2]
    return jnp.moveaxis(a.reshape((bn, s // size, size) + a.shape[2:]), 1, 0)

def from_blocks(a):
    n, bn, t = a.shape[:3]
    return jnp.moveaxis(a, 0, 1).reshape((bn, n * t) + a.shape[3:])

def gmlp_mixer(u, v, w_s, b_s, ln_g, ln_b):
    bn, s, _ = u.shape
    nblk = s // GMLP_BLOCK
    u = jax.nn.gelu(u)
    v = jax.nn.gelu(v).reshape(bn, nblk, GMLP_BLOCK, A_GROUPS, A_GDIM)
    v = layer_norm(v, ln_g, ln_b)
    pos_chunk = jnp.arange(GMLP_BLOCK) // CHUNK
    mask = pos_chunk[None, :] <= pos_chunk[:, None]
    w = jnp.where(mask[None], w_s, jnp.zeros_like(w_s))
    sg = jnp.einsum('gts,bnsgc->bntgc', w, v) + b_s.T[None, None, :, :, None]
    return u * sg.reshape(bn, s, A_WIDTH)

def diff_attention(q, k, v, lam, lam_init, subln_g):
    bn, s = q.shape[:2]
    nblk = s // Q_BLOCK
    scale = B_QK_DIM ** -0.5
    slopes = alibi_slopes(B_HEADS)
    kpos = jnp.arange(s)
    kchunk = kpos // CHUNK

    def block(args):
        qblk, i = args
        qpos = i * Q_BLOCK + jnp.arange(Q_BLOCK)
        allowed = kchunk[None, :] <= (qpos // CHUNK)[:, None]
        dist = jnp.abs(qpos[:, None] - kpos[None, :]).astype(jnp.float32)
        bias = -slopes[:, None, None] * dist[None]
        logits = jnp.einsum('bthmd,bshmd->bhmts', qblk, k).astype(jnp.float32) * scale
        logits = logits + bias[None, :, None]
        logits = jnp.where(allowed[None, None, None], logits, -jnp.inf)
        p = jax.nn.softmax(logits, axis=-1)
        attn = p[:, :, 0] - lam * p[:, :, 1]
        return jnp.einsum('bhts,bshe->bthe', attn.astype(v.dtype), v)

    o = from_blocks(lax.map(block, (to_blocks(q, Q_BLOCK), jnp.arange(nblk))))
    o = rms_norm_2(o, subln_g) * (1.0 - lam_init)
    return o.reshape(bn, s, B_WIDTH)

def dsa_attention(q, k, v, qi, ki, wi):
    bn, s = q.shape[:2]
    nblk = s // Q_BLOCK
    topk = min(TOPK_MAX, s // 4)
    scale = C_HEAD_DIM ** -0.5
    idx_scale = (IDX_HEADS ** -0.5) * (IDX_DIM ** -0.5)
    slopes = alibi_slopes(C_HEADS)
    kchunk = jnp.arange(s) // CHUNK

    def block(args):
        qblk, qiblk, wiblk, i = args
        qpos = i * Q_BLOCK + jnp.arange(Q_BLOCK)
        qchunk = qpos // CHUNK
        allowed = kchunk[None, :] <= qchunk[:, None]
        idx_logits = jnp.einsum('bthd,bsd->bths', qiblk, ki).astype(jnp.float32)
        score = jnp.einsum('bth,bths->bts', wiblk.astype(jnp.float32) * idx_scale, jax.nn.relu(idx_logits))
        score = jnp.where(allowed[None], score, -jnp.inf)
        _, sel = lax.top_k(score, topk)
        sel_ok = (sel // CHUNK) <= qchunk[None, :, None]
        k_sel = jax.vmap(lambda kb, ib: kb[ib])(k, sel)
        v_sel = jax.vmap(lambda vb, ib: vb[ib])(v, sel)
        logits = jnp.einsum('bthd,btkhd->bhtk', qblk, k_sel).astype(jnp.float32) * scale
        dist = jnp.abs(qpos[None, :, None] - sel).astype(jnp.float32)
        logits = logits - slopes[None, :, None, None] * dist[:, None]
        logits = jnp.where(sel_ok[:, None], logits, -jnp.inf)
        p = jax.nn.softmax(logits, axis=-1)
        return jnp.einsum('bhtk,btkhd->bthd', p.astype(v_sel.dtype), v_sel)

    xs = (to_blocks(q, Q_BLOCK), to_blocks(qi, Q_BLOCK), to_blocks(wi, Q_BLOCK), jnp.arange(nblk))
    o = from_blocks(lax.map(block, xs))
    return o.reshape(bn, s, C_WIDTH)

def hybrid_layer(x, layer_idx, w_in, w_s, b_s, a_ln_g, a_ln_b, lam_q1, lam_k1, lam_q2, lam_k2,
                 subln_g, w_out, ln1_g, ln1_b, w_gu, w_down, ln2_g, ln2_b):
    bn, s, _ = x.shape
    h = jnp.einsum('bsd,de->bse', x, w_in)
    a_u = h[..., OFF_A_U:OFF_A_V]
    a_v = h[..., OFF_A_V:OFF_B_Q]
    b_q = h[..., OFF_B_Q:OFF_B_K].reshape(bn, s, B_HEADS, 2, B_QK_DIM)
    b_k = h[..., OFF_B_K:OFF_B_V].reshape(bn, s, B_HEADS, 2, B_QK_DIM)
    b_v = h[..., OFF_B_V:OFF_C_Q].reshape(bn, s, B_HEADS, B_V_DIM)
    c_q = h[..., OFF_C_Q:OFF_C_K].reshape(bn, s, C_HEADS, C_HEAD_DIM)
    c_k = h[..., OFF_C_K:OFF_C_V].reshape(bn, s, C_HEADS, C_HEAD_DIM)
    c_v = h[..., OFF_C_V:OFF_I_Q].reshape(bn, s, C_HEADS, C_HEAD_DIM)
    i_q = h[..., OFF_I_Q:OFF_I_K].reshape(bn, s, IDX_HEADS, IDX_DIM)
    i_k = h[..., OFF_I_K:OFF_I_W]
    i_w = h[..., OFF_I_W:IN_WIDTH]

    out_a = gmlp_mixer(a_u, a_v, w_s, b_s, a_ln_g, a_ln_b)

    lam_init = 0.8 - 0.6 * math.exp(-0.3 * layer_idx)
    lam = (jnp.exp(jnp.sum(lam_q1.astype(jnp.float32) * lam_k1.astype(jnp.float32)))
           - jnp.exp(jnp.sum(lam_q2.astype(jnp.float32) * lam_k2.astype(jnp.float32))) + lam_init)
    out_b = diff_attention(b_q, b_k, b_v, lam, lam_init, subln_g)

    out_c = dsa_attention(c_q, c_k, c_v, i_q, i_k, i_w)

    mix = jnp.concatenate([out_a, out_b, out_c], axis=-1)
    x = layer_norm(DEEPNORM_ALPHA * x + jnp.einsum('bse,ed->bsd', mix, w_out), ln1_g, ln1_b)

    gu = jnp.einsum('bsd,df->bsf', x, w_gu)
    gate, up = gu[..., :FFN_HIDDEN], gu[..., FFN_HIDDEN:]
    ffn = jnp.einsum('bsf,fd->bsd', jax.nn.silu(gate) * up, w_down)
    return layer_norm(DEEPNORM_ALPHA * x + ffn, ln2_g, ln2_b)

def second_inputs(seed: int = 0) -> dict:
    key = jax.random.key(seed)
    ks = jax.random.split(key, 20)
    f32 = jnp.float32
    nrm = lambda k, shape: jax.random.normal(k, shape, dtype=f32)
    return {
        'x': nrm(ks[0], (BATCH, SEQ, D_MODEL)),
        'w_in': nrm(ks[1], (DEPTH_2, D_MODEL, IN_WIDTH)) * D_MODEL ** -0.5,
        'gmlp_w_s': nrm(ks[2], (DEPTH_2, A_GROUPS, GMLP_BLOCK, GMLP_BLOCK)) * GMLP_BLOCK ** -0.5,
        'gmlp_b_s': 1.0 + 0.1 * nrm(ks[3], (DEPTH_2, A_GROUPS, GMLP_BLOCK)),
        'gmlp_ln_g': 1.0 + 0.05 * nrm(ks[4], (DEPTH_2, A_GROUPS, A_GDIM)),
        'gmlp_ln_b': 0.02 * nrm(ks[5], (DEPTH_2, A_GROUPS, A_GDIM)),
        'lam_q1': 0.1 * nrm(ks[6], (DEPTH_2, B_QK_DIM)),
        'lam_k1': 0.1 * nrm(ks[7], (DEPTH_2, B_QK_DIM)),
        'lam_q2': 0.1 * nrm(ks[8], (DEPTH_2, B_QK_DIM)),
        'lam_k2': 0.1 * nrm(ks[9], (DEPTH_2, B_QK_DIM)),
        'diff_subln_g': 1.0 + 0.05 * nrm(ks[10], (DEPTH_2, B_V_DIM)),
        'w_out': nrm(ks[11], (DEPTH_2, MIX_WIDTH_2, D_MODEL)) * MIX_WIDTH_2 ** -0.5 * DEEPNORM_BETA,
        'ln1_g': 1.0 + 0.05 * nrm(ks[12], (DEPTH_2, D_MODEL)),
        'ln1_b': 0.02 * nrm(ks[13], (DEPTH_2, D_MODEL)),
        'w_gu': nrm(ks[14], (DEPTH_2, D_MODEL, 2 * FFN_HIDDEN)) * D_MODEL ** -0.5,
        'w_down': nrm(ks[15], (DEPTH_2, FFN_HIDDEN, D_MODEL)) * FFN_HIDDEN ** -0.5 * DEEPNORM_BETA,
        'ln2_g': 1.0 + 0.05 * nrm(ks[16], (DEPTH_2, D_MODEL)),
        'ln2_b': 0.02 * nrm(ks[17], (DEPTH_2, D_MODEL)),
    }

def second_block(x, w_in, gmlp_w_s, gmlp_b_s, gmlp_ln_g, gmlp_ln_b, lam_q1, lam_k1, lam_q2, lam_k2,
              diff_subln_g, w_out, ln1_g, ln1_b, w_gu, w_down, ln2_g, ln2_b):
    for l in range(DEPTH_2):
        x = hybrid_layer(x, l, w_in[l], gmlp_w_s[l], gmlp_b_s[l], gmlp_ln_g[l], gmlp_ln_b[l],
                         lam_q1[l], lam_k1[l], lam_q2[l], lam_k2[l], diff_subln_g[l], w_out[l],
                         ln1_g[l], ln1_b[l], w_gu[l], w_down[l], ln2_g[l], ln2_b[l])
    return x


def setup_inputs(seed=0):
    out = dict(first_inputs(seed))
    for name, value in second_inputs(seed + 1).items():
        if name != "x":
            out[name + "_2"] = value
    return out


def reference(
    x, c, w_ada, b_ada, g_pre, w_in, w_conv, w_pool, pool_scale, w_out, g_post, w_in_2,
    gmlp_w_s_2, gmlp_b_s_2, gmlp_ln_g_2, gmlp_ln_b_2, lam_q1_2, lam_k1_2, lam_q2_2, lam_k2_2,
    diff_subln_g_2, w_out_2, ln1_g_2, ln1_b_2, w_gu_2, w_down_2, ln2_g_2, ln2_b_2,
):
    x = first_block(
        x, c, w_ada, b_ada, g_pre, w_in, w_conv, w_pool, pool_scale, w_out, g_post,
    )
    return second_block(
        x, w_in_2, gmlp_w_s_2, gmlp_b_s_2, gmlp_ln_g_2, gmlp_ln_b_2, lam_q1_2, lam_k1_2,
        lam_q2_2, lam_k2_2, diff_subln_g_2, w_out_2, ln1_g_2, ln1_b_2, w_gu_2, w_down_2,
        ln2_g_2, ln2_b_2,
    )


_drawn_inputs = setup_inputs


def setup_inputs(seed=0):
    import zlib

    import numpy as np

    out = dict(_drawn_inputs(seed))
    spreads = {}
    factors = {'gmlp_b_s_2': 3.404,
     'gmlp_ln_g_2': 7.49,
     'gmlp_ln_b_2': 37.571,
     'lam_q1_2': 4.993,
     'lam_k1_2': 3.666,
     'lam_k2_2': 3.278,
     'diff_subln_g_2': 5.303,
     'ln1_b_2': 2.675,
     'ln2_b_2': 2.84}
    for name, (base, spread) in spreads.items():
        noise = np.random.default_rng([zlib.crc32(name.encode()), seed]).standard_normal(out[name].shape)
        drawn = base * np.exp(spread * noise) if base else spread * noise
        out[name] = jnp.asarray(drawn.astype(out[name].dtype))
    for name, factor in factors.items():
        out[name] = (out[name] * factor).astype(out[name].dtype)
    return out
```

```python
import math
from contextlib import ExitStack, contextmanager

import concourse.bass as bass
from concourse import mybir

FP32 = mybir.dt.float32
FP32R = mybir.dt.float32r
INT32 = mybir.dt.int32
BF16 = mybir.dt.bfloat16
ALU = mybir.AluOpType
ACT = mybir.ActivationFunctionType
AX = mybir.AxisListType

P = 128
D = 1024
T = 1024
KT = D // P
TT = T // P
HALF = 512

LAYERS = 2
CW = D // 2
CB = CW // P
TAPS = 3
WINDOWS = (2, 4, 8, 16)
PAD = 8
RMS_EPS = 1e-6
P1_ROLES = 6
P1_UNITS = P1_ROLES * CB

AG, AD = 4, 64
A_W = AG * AD
BH, BQK, BV = 4, 64, 128
CH, CD = 4, 64
IH, ID = 8, 32
TOPK = 256
CHUNK = 64
OFF_B_Q = 2 * A_W
OFF_B_K = OFF_B_Q + BH * 2 * BQK
OFF_B_V = OFF_B_K + BH * 2 * BQK
OFF_C_Q = OFF_B_V + BH * BV
OFF_C_K = OFF_C_Q + CH * CD
OFF_C_V = OFF_C_K + CH * CD
OFF_I_Q = OFF_C_V + CH * CD
OFF_I_K = OFF_I_Q + IH * ID
IN_W = OFF_I_K + ID + IH
FFN = -(-8 * D // (3 * 256)) * 256
FB = FFN // P
ALPHA = 2 ** 0.25
LN_EPS = 1e-5
LAM_INIT = 0.8 - 0.6 * math.exp(-0.3 * 0)
MASKED = -(2.0 ** 100)

FG = 6
GROUPS = [min(FG, FB - g) for g in range(0, FB, FG)]
SEL0 = TOPK // P
N_TS = TT - SEL0
N_SEL = sum(i + 1 for i in range(SEL0, TT))
BITS = 31


def sel_at(i):
    return P * sum(j + 1 for j in range(SEL0, i))


N_PROJ = OFF_I_Q // P
PB_U, PB_V, PB_BQ, PB_BK, PB_BV = 0, A_W // P, OFF_B_Q // P, OFF_B_K // P, OFF_B_V // P
NATURAL = (2, 3, 12, 13, 14, 15, 20, 21)
PB_CQ, PB_CK, PB_CV = OFF_C_Q // P, OFF_C_K // P, OFF_C_V // P


class Tally:

    def __init__(self, eng, sem, start=0):
        self.eng, self.sem, self.n, self.off = eng, sem, start, 0

    def did(self, instruction):
        instruction.then_inc(self.sem, 1)
        self.n += 1
        self.eng.wait_ge(self.sem, self.n + self.off)


@contextmanager
def loop(eng, count, tally=None, per=0):
    start = tally.n if tally else 0
    with eng.Fori(0, count) as i:
        if tally:
            tally.off = i * per
        yield i
    if tally:
        assert tally.n - start == per, (tally.n - start, per)
        tally.n, tally.off = start + per * count, 0


def build(nc, x, c, w_ada, b_ada, g_pre, w_in, w_conv, w_pool, pool_scale, w_out, g_post,
          w_in_2, gmlp_w_s, gmlp_b_s, gmlp_ln_g, gmlp_ln_b, lam_q1, lam_k1, lam_q2, lam_k2,
          diff_subln_g, w_out_2, ln1_g, ln1_b, w_gu, w_down, ln2_g, ln2_b, out):
    w_in_v = w_in.rearrange("l (k p) n -> l p k n", p=P)
    w_out_v = w_out.rearrange("l (k p) n -> l p k n", p=P)
    w_in_2v = w_in_2[0].rearrange("(k p) n -> p k n", p=P)
    w_out_2v = w_out_2[0].rearrange("(k p) n -> p k n", p=P)
    w_gu_v = w_gu[0].rearrange("(k p) n -> p k n", p=P)
    w_down_v = w_down[0].rearrange("(k p) n -> p k n", p=P)
    x_mid = nc.dram_tensor("x_mid", [P, KT, T], FP32).ap()
    w_ada_v = w_ada.rearrange("l (p t) n -> l p t n", t=KT)

    with ExitStack() as ctx:
        def sb(name, shape, dt=FP32):
            return ctx.enter_context(nc.sbuf_tensor(name, shape, dt))

        def sem(name):
            return ctx.enter_context(nc.semaphore(name))

        act_hi = sb("act_hi", [P, KT, T], FP32R)
        act_lo = sb("act_lo", [P, KT, T], FP32R)
        identity = sb("identity", [P, P])
        ones = sb("ones", [P, P])
        params = sb("params", [P, P])
        params2 = sb("params2", [P, P])
        wpool_now = sb("wpool_now", [P, P])
        c_col = sb("c_col", [P, KT])
        mod = sb("mod", [P, LAYERS, 3 * KT])
        pre_gain = sb("pre_gain", [P, LAYERS, KT])
        post_gain = sb("post_gain", [P, LAYERS, KT])
        win_on = sb("win_on", [P, len(WINDOWS) - 1, CB])
        win_inv = sb("win_inv", [P, CB])
        win_fix = sb("win_fix", [P, CB, 16])
        iota_t = sb("iota_t", [P, 16])

        @contextmanager
        def over():
            with ExitStack() as inner:
                yield lambda name, shape, dt=FP32: inner.enter_context(nc.sbuf_tensor(name, shape, dt))

        with over() as t:
            w_raw = [t(f"w_raw{s}", [P, KT, P]) for s in range(2)]
            w_hi = [t(f"w_hi{s}", [P, KT, P], FP32R) for s in range(2)]
            w_lo = [t(f"w_lo{s}", [P, KT, P], FP32R) for s in range(2)]
        w_region = sb("w_region", [P, 6, T])

        ARENA = N_PROJ * T + N_SEL * P + 2 * T
        with over() as t:
            xT = t("xT", [P, KT, T])
            yT = t("yT", [P, KT, T])
            u_buf = t("u_buf", [P, T])
            cu = t("cu", [P, TAPS - 1 + T])
            conv = t("conv", [P, T])
            gate_buf = t("gate_buf", [P, T])
            p_buf = t("p_buf", [P, PAD + T])
            win_a = t("win_a", [P, PAD + T])
            win_b = t("win_b", [P, PAD + T])
            gp_buf = t("gp_buf", [P, T])
            sq = t("sq", [P, T])
            sq_sum = t("sq_sum", [P, T])
            rstd = t("rstd", [P, T])
            wpool_sb = t("wpool_sb", [P, LAYERS * len(WINDOWS), P])
        with over() as t:
            proj = t("proj", [P, N_PROJ, T])
            score = t("score", [P, N_SEL * P])
            buf_a = t("buf_a", [P, T])
            buf_b = t("buf_b", [P, T])
        with over() as t:
            t("under_proj", [P, N_PROJ, T])
            sel_bias = t("sel_bias", [P, N_SEL * P], FP32R)
            dist_bias = t("dist_bias", [P, T], FP32R)
        with over() as t:
            z = t("z", [P, KT, T])
            x_res = t("x_res", [P, KT, T])
        with over() as t:
            t("under_z", [P, KT, T])
            f_hi = t("f_hi", [P, FG, T], FP32R)
            f_lo = t("f_lo", [P, FG, T], FP32R)
            silu_buf = t("silu_buf", [P, T])
            f_buf = t("f_buf", [P, T])
            sq2 = t("sq2", [P, T])
            sum2 = t("sum2", [P, T])
            rstd2 = t("rstd2", [P, T])
        arena = sb("arena", [P, ARENA])
        index_tmp = buf_b[0:64, :]
        relu_buf = [buf_a, buf_b]
        ws_raw = w_region[:, 0, 0:AG * P].rearrange("p (g s) -> p g s", g=AG)
        wsT = w_region[:, 1, 0:AG * P].rearrange("p (g t) -> p g t", g=AG)
        ln_g_row, ln_b_row = w_region[:, 2, 0:A_W], w_region[:, 2, A_W:2 * A_W]
        bs_tab = w_region[:, 3, 0:2 * P].rearrange("p (b t) -> p b t", b=2)
        ln_stat = w_region[:, 3, 512:576].rearrange("p (a g) -> p a g", a=2)
        gm_tmp = w_region[:, 4:6, :]
        prob = [w_region[:, i, :] for i in range(4)]
        probT = [w_region[:, 4 + i, :] for i in range(2)]
        slope_id = sb("slope_id", [P, BH, P], FP32R)
        one_id = sb("one_id", [P, P], FP32R)
        params_raw, params2_raw = w_region[:, 4, 0:P], w_region[:, 4, P:2 * P]
        lam_rows = w_region[:, 5, 0:4 * BQK].rearrange("p (a d) -> p a d", a=4)
        lam = sb("lam", [P, 2])
        sub_gain = sb("sub_gain", [P, 1])
        index_w = sb("index_w", [P, TT, IH])
        bit_no = sb("bit_no", [P, 32], INT32)
        bit_val = sb("bit_val", [P, 32], INT32)
        thr = sb("thr", [P, N_TS], INT32)
        cand = sb("cand", [P, N_TS], INT32)
        flag = sb("flag", [P, N_TS], INT32)
        cnt, need, sign, thr_s = (sb(n, [P, N_TS]) for n in ("cnt", "need", "sign", "thr_s"))
        neg_max = sb("neg_max", [P, 2])
        den = sb("den", [P, 2, 2])
        den_r = sb("den_r", [P, 2])
        ada_sum = [conv, gate_buf]
        ada_piece = [u_buf[:], gp_buf[:], win_a[:, PAD:], win_b[:, PAD:]]
        bank = [ctx.enter_context(nc.psum_tensor(f"pair{i}", [P, T], FP32)) for i in range(4)]

        raw_loaded = [sem(f"raw_loaded{s}") for s in range(2)]
        hi_ready, lo_ready, unit_done = sem("hi_ready"), sem("lo_ready"), sem("unit_done")
        x_loaded, par_loaded, small_loaded = sem("x_loaded"), sem("par_loaded"), sem("small_loaded")
        ada_loaded = [sem(f"ada_loaded{s}") for s in range(4)]
        ada_used, ada_acc, ada_col, ada_ready = (sem(n) for n in ("ada_used", "ada_acc", "ada_col", "ada_ready"))
        const_ready = sem("const_ready")
        par_T, par_ready, xT_done, xT_ready = sem("par_T"), sem("par_ready"), sem("xT_done"), sem("xT_ready")
        silu_c = sem("silu_c")
        s_hi, s_lo = sem("s_hi"), sem("s_lo")
        t_ready = sem("t_ready")
        u_copied, c_used, b_used, gate_done, p_copied, gp_done = (
            sem(n) for n in ("u_copied", "c_used", "b_used", "gate_done", "p_copied", "gp_done"))
        y_conv, pooled, mixed, y_pool, wpool_ready = (
            sem(n) for n in ("y_conv", "pooled", "mixed", "y_pool", "wpool_ready"))
        o_copied, sq_ready, sq_added = sem("o_copied"), sem("sq_ready"), sem("sq_added")
        x_new = sem("x_new")
        stat_done, var_ready, rstd_ready = sem("stat_done"), sem("var_ready"), sem("rstd_ready")
        act_own, dve_own, pool_own = sem("act_own"), sem("dve_own"), sem("pool_own")
        lam_exp, dist_iota, dist_signed = sem("lam_exp"), sem("dist_iota"), sem("dist_signed")
        outT_done, out_copied, out_stored = sem("outT_done"), sem("out_copied"), sem("out_stored")

        ROW_B_ADA = 0
        ROW_G_PRE = ROW_B_ADA + LAYERS * 3 * KT
        ROW_G_POST = ROW_G_PRE + LAYERS * KT
        ROW_CONV = ROW_G_POST + LAYERS * KT
        ROW_PSCALE = ROW_CONV + LAYERS * TAPS * CB
        N_ROWS = ROW_PSCALE + LAYERS * CB

        def rows(ap2d):
            return ap2d.rearrange("l (r p) -> (l r) p", p=P)

        def f32(ap):
            return ap.bitcast(FP32)

        UL = P1_UNITS + KT

        U_IDX = LAYERS * UL
        U_PROJ = U_IDX + 3
        U_OUT2 = U_PROJ + N_PROJ
        U_FFN = U_OUT2 + KT
        U_GROUP = [U_FFN + sum(2 * n + KT for n in GROUPS[:g]) for g in range(len(GROUPS))]
        U_END = U_GROUP[-1] + 2 * GROUPS[-1] + KT

        ROW2_LN = [0, 2 * KT]
        ROW2_SUB = 4 * KT
        N_ROWS2 = ROW2_SUB + 1
        SP_X, SP_MIX = 2 * LAYERS * KT, (2 * LAYERS + 1) * KT
        SP_X1 = SP_MIX + 2 + BH

        (x_kept, iq_copied, ik_copied, iwT_done, iw_ready, score_mm, relu_done, score_added, p3_copied,
         gm_loaded, gelu_done, nat_done, nat_copied, wsT_done, wsT_copied, ws_masked, v_normed, ln_var, ln_rstd,
         gm_done, mix_ready, dist_ready, logits_done, max_ready, exp_done, attn_ready, pT_done, pT_copied, pv_done,
         o_taken, ob_sq, ob_stat, ob_var, ob_rstd, sel_done, attn_over) = (sem(n) for n in (
             "x_kept", "iq_copied", "ik_copied", "iwT_done", "iw_ready", "score_mm", "relu_done", "score_added",
             "p3_copied", "gm_loaded", "gelu_done", "nat_done", "nat_copied", "wsT_done", "wsT_copied",
             "ws_masked", "v_normed", "ln_var", "ln_rstd", "gm_done", "mix_ready", "dist_ready", "logits_done",
             "max_ready", "exp_done", "attn_ready", "pT_done", "pT_copied", "pv_done", "o_taken", "ob_sq",
             "ob_stat", "ob_var", "ob_rstd", "sel_done", "attn_over"))
        (x_back, z_ready, z_added, mean_mm, xc_ready, sq2_ready, sq2_added, var_mm, ln2_var, ln2_rstd, ln_t,
         x_final, acc_init, g_act, f_mul, f_hi_done, f_lo_done, acc_added, outc, lam_loaded) = (sem(n) for n in (
             "x_back", "z_ready", "z_added", "mean_mm", "xc_ready", "sq2_ready", "sq2_added", "var_mm", "ln2_var",
             "ln2_rstd", "ln_t", "x_final", "acc_init", "g_act", "f_mul", "f_hi_done", "f_lo_done", "acc_added",
             "outc", "lam_loaded"))

        def keys(i):
            return P * (i + 1)

        def pieces(n):
            return [(a, min(HALF, n - a)) for a in range(0, n, HALF)]

        block = ctx.enter_context(nc.Block())

        @block.sync
        def _(sp):
            sp.dma_start(params_raw[ROW_B_ADA:ROW_G_PRE, :], rows(b_ada)).then_inc(par_loaded, 16)
            sp.dma_start(params_raw[ROW_G_PRE:ROW_G_POST, :], rows(g_pre)).then_inc(par_loaded, 16)
            sp.dma_start(params_raw[ROW_G_POST:ROW_CONV, :], rows(g_post)).then_inc(par_loaded, 16)
            sp.dma_start(params_raw[ROW_CONV:ROW_PSCALE, :],
                         w_conv.rearrange("l t (r p) -> (l t r) p", p=P)).then_inc(par_loaded, 16)
            sp.dma_start(params_raw[ROW_PSCALE:N_ROWS, :], rows(pool_scale)).then_inc(par_loaded, 16)
            sp.dma_start(c_col[:], c.rearrange("b (p t) -> (b p) t", t=KT)).then_inc(par_loaded, 16)
            for k in range(2):
                for i, a in enumerate(((ln1_g, ln1_b), (ln2_g, ln2_b))[k]):
                    sp.dma_start(params2_raw[ROW2_LN[k] + i * KT:ROW2_LN[k] + (i + 1) * KT, :], rows(a))\
                      .then_inc(par_loaded, 16)
            sp.dma_start(params2_raw[ROW2_SUB:N_ROWS2, :], diff_subln_g).then_inc(par_loaded, 16)
            for i, a in enumerate((lam_q1, lam_k1, lam_q2, lam_k2)):
                sp.dma_start(lam_rows[:, i, :], a.broadcast_to([P, BQK])).then_inc(lam_loaded, 16)
            sp.dma_start(yT[:], x[0].rearrange("(t p) f -> p t f", p=P)).then_inc(x_loaded, 16)
            sp.dma_start(wpool_sb[:], w_pool.rearrange("l g c d -> c (l g) d")).then_inc(small_loaded, 16)
            n = 0
            for l in range(LAYERS):
                for third in range(3):
                    for t in range(KT):
                        if n >= 4:
                            sp.wait_ge(ada_used, n - 3)
                        sp.dma_start(ada_piece[n % 4], w_ada_v[l, :, t, third * D:(third + 1) * D])\
                          .then_inc(ada_loaded[n % 4], 16)
                        n += 1

            def load(u, slot, src):
                sp.wait_ge(hi_ready, 1 + u)
                sp.wait_ge(lo_ready, 1 + u)
                sp.dma_start(w_raw[slot][:], src).then_inc(raw_loaded[slot], 16)

            for l in range(LAYERS):
                with loop(sp, CB) as j:
                    for r, start in enumerate((0, 2 * CW, CW, 3 * CW, 4 * CW, 5 * CW)):
                        load(l * UL + P1_ROLES * j + r, r % 2, w_in_v[l, :, :, bass.ds(start + j * P, P)])
                with loop(sp, KT // 2) as j:
                    for r in range(2):
                        load(l * UL + P1_UNITS + 2 * j + r, r, w_out_v[l, :, :, bass.ds((2 * j + r) * P, P)])
            load(U_IDX, 0, w_in_2v[:, :, OFF_I_Q:OFF_I_Q + P])
            load(U_IDX + 1, 1, w_in_2v[:, :, OFF_I_Q + P:OFF_I_K])
            sp.wait_ge(x_new, KT * LAYERS)
            sp.dma_start(x_mid, xT[:]).then_inc(x_kept, 16)
            sp.wait_ge(hi_ready, 1 + U_IDX + 2)
            sp.wait_ge(lo_ready, 1 + U_IDX + 2)
            sp.dma_start(w_raw[0][:, :, 0:IN_W - OFF_I_K], w_in_2v[:, :, OFF_I_K:IN_W])\
              .then_inc(raw_loaded[0], 16)
            with loop(sp, N_PROJ // 2) as j:
                for r in range(2):
                    load(U_PROJ + 2 * j + r, (U_PROJ + r) % 2, w_in_2v[:, :, bass.ds((2 * j + r) * P, P)])
            sp.wait_ge(unit_done, 1 + U_OUT2 + 1)
            sp.dma_start(ws_raw, gmlp_w_s[0].rearrange("g t s -> t g s")).then_inc(gm_loaded, 16)
            sp.dma_start(ln_g_row, gmlp_ln_g.rearrange("l g c -> l (g c)").broadcast_to([P, A_W]))\
              .then_inc(gm_loaded, 16)
            sp.dma_start(ln_b_row, gmlp_ln_b.rearrange("l g c -> l (g c)").broadcast_to([P, A_W]))\
              .then_inc(gm_loaded, 16)
            for g in range(AG):
                sp.dma_start(bs_tab[AD * (g % 2):AD * (g % 2 + 1), g // 2, :],
                             gmlp_b_s[0, g:g + 1, :].broadcast_to([AD, P])).then_inc(gm_loaded, 16)
            sp.wait_ge(attn_over, 1)
            for r in range(2):
                u = U_OUT2 + r
                sp.dma_start(w_raw[u % 2][:], w_out_2v[:, :, r * P:(r + 1) * P]).then_inc(raw_loaded[u % 2], 16)
            sp.dma_start(x_res[:], x_mid).then_inc(x_back, 16)
            for r in range(2):
                load(U_OUT2 + 2 + r, (U_OUT2 + r) % 2, w_out_2v[:, :, (2 + r) * P:(3 + r) * P])
            with loop(sp, KT // 2 - 2) as j:
                for r in range(2):
                    load(U_OUT2 + 4 + 2 * j + r, (U_OUT2 + r) % 2, w_out_2v[:, :, bass.ds((2 * j + 4 + r) * P, P)])
            for g, n in enumerate(GROUPS):
                with loop(sp, n) as j:
                    for r in range(2):
                        load(U_GROUP[g] + 2 * j + r, (U_GROUP[g] + r) % 2,
                             w_gu_v[:, :, bass.ds(r * FFN + (g * FG + j) * P, P)])
                with loop(sp, KT // 2) as j:
                    for r in range(2):
                        u, slot = U_GROUP[g] + 2 * n + 2 * j + r, (U_GROUP[g] + r) % 2
                        sp.wait_ge(hi_ready, 1 + u)
                        sp.wait_ge(lo_ready, 1 + u)
                        sp.dma_start(w_raw[slot][:, 0:n, :],
                                     w_down_v[:, g * FG:g * FG + n, bass.ds((2 * j + r) * P, P)])\
                          .then_inc(raw_loaded[slot], 16)
            out_v = out[0].rearrange("(t p) f -> p t f", p=P)
            for t in range(TT):
                sp.wait_ge(out_copied, t + 1)
                sp.dma_start(out_v[:, t, :], x_res[:, t, :]).then_inc(out_stored, 16)
            sp.wait_ge(out_stored, 16 * TT)

        @block.gpsimd
        def _(pool):
            own = Tally(pool, pool_own)
            g = nc.gpsimd
            own.did(g.memset(identity[:], 0.0))
            own.did(g.affine_select(out=identity[:], in_=identity[:], compare_op=ALU.not_equal, fill=1.0,
                                    base=0, pattern=[[-1, P]], channel_multiplier=1))
            own.did(g.memset(ones[:], 1.0))
            own.did(g.memset(cu[:, 0:TAPS - 1], 0.0))
            for b in (p_buf, win_a, win_b):
                own.did(g.memset(b[:, 0:PAD], 0.0))
            for k in range(len(WINDOWS) - 1):
                for i in range(CB):
                    own.did(g.memset(win_on[:, k, i:i + 1], 1.0 if i > k else 0.0))
            for i, w in enumerate(WINDOWS):
                own.did(g.memset(win_inv[:, i:i + 1], 1.0 / w))
            own.did(g.iota(iota_t[:], pattern=[[1, 16]], base=1, channel_multiplier=0,
                           allow_small_or_imprecise_dtypes=True))
            for i, w in enumerate(WINDOWS):
                own.did(g.tensor_scalar(win_fix[:, i, :], iota_t[:], float(w), 1.0 / w, ALU.min, ALU.mult))
            own.did(g.iota(bit_no[:], pattern=[[-1, 32]], base=BITS - 1, channel_multiplier=0))
            own.did(g.tensor_copy(one_id[:], identity[:]))
            for h in range(BH):
                own.did(g.tensor_scalar(slope_id[:, h, :], identity[:], 2.0 ** (-8.0 * (h + 1) / BH) * BQK ** 0.5,
                                        None, ALU.mult))
            pool.sem_inc(const_ready, 1)

            def add_squares(n, first):
                pool.wait_ge(sq_ready, n + 1)
                if first:
                    i = g.tensor_copy(sq_sum[:], sq[:])
                else:
                    i = g.tensor_tensor(sq_sum[:], sq_sum[:], sq[:], ALU.add)
                i.then_inc(sq_added, 1)

            for n in range(2 * LAYERS * KT):
                if n % KT == 0 and n:
                    pool.wait_ge(stat_done, n // KT)
                elif n:
                    pool.wait_ge(sq_added, n)
                add_squares(n, n % KT == 0)

            pool.wait_ge(score_added, N_TS * IH)
            pool.wait_ge(relu_done, N_TS * IH + 1)
            g.iota(buf_a[:], pattern=[[-1, T]], base=T - P, channel_multiplier=1,
                   allow_small_or_imprecise_dtypes=True).then_inc(dist_iota, 1)
            pool.wait_ge(dist_signed, 2)
            g.memset(f32(dist_bias[0:CHUNK, T - CHUNK:T]), MASKED).then_inc(dist_ready, 1)

            for q in range(2):
                for k in range(KT):
                    if q == 0:
                        pool.wait_ge(z_ready, 1 + k + 2)
                    else:
                        pool.wait_ge(acc_added, 1 + (len(GROUPS) - 1) * KT + k + 2)
                    if k == 0:
                        if q:
                            pool.wait_ge(var_mm, q)
                        i = g.tensor_copy(sum2[:], z[:, k, :])
                    else:
                        pool.wait_ge(z_added, q * KT + k)
                        i = g.tensor_tensor(sum2[:], sum2[:], z[:, k, :], ALU.add)
                    i.then_inc(z_added, 1)
                for k in range(KT):
                    pool.wait_ge(sq2_ready, q * KT + k + 1)
                    if k == 0:
                        pool.wait_ge(mean_mm, q + 1)
                        i = g.tensor_copy(sum2[:], sq2[:])
                    else:
                        pool.wait_ge(sq2_added, q * KT + k)
                        i = g.tensor_tensor(sum2[:], sum2[:], sq2[:], ALU.add)
                    i.then_inc(sq2_added, 1)

        @block.scalar
        def _(act):
            own = Tally(act, act_own)
            for s_ in (gate_done, p_copied, gp_done, g_act):
                act.sem_inc(s_, 1)
            A = nc.scalar.activation
            act.wait_ge(par_loaded, 16 * 11)
            A(c_col[:], c_col[:], ACT.Silu).then_inc(silu_c, 1)

            def square(n, src):
                if n:
                    act.wait_ge(sq_added, n)
                A(sq[:], src, ACT.Square).then_inc(sq_ready, 1)

            def root(n):
                act.wait_ge(var_ready, n + 1)
                A(rstd[:], rstd[:], ACT.Sqrt).then_inc(rstd_ready, 1)

            for k in range(KT):
                act.wait_ge(xT_ready, k + 1)
                square(k, xT[:, k, :])
            root(0)
            act.wait_ge(par_ready, 1)
            A(lam[:], lam[:], ACT.Exp).then_inc(lam_exp, 1)
            act.sem_inc(hi_ready, 2)
            act.sem_inc(o_copied, 2)

            def hi_first(l):
                for r in range(2):
                    u = l * UL + r
                    act.wait_ge(raw_loaded[r], 16 * (u // 2 + 1))
                    act.wait_ge(unit_done, 1 + u)
                    A(w_hi[r][:], w_raw[r][:], ACT.Copy).then_inc(hi_ready, 1)

            def hi_next(base, j, per, r):
                act.wait_ge(unit_done, 1 + base + per * j + r + 2)
                s_ = (base + r) % 2
                act.wait_ge(raw_loaded[s_], j * (8 * per) + 16 * ((base + r) // 2 + 2))
                A(w_hi[s_][:], w_raw[s_][:], ACT.Copy).then_inc(hi_ready, 1)

            act.wait_ge(small_loaded, 16)
            hi_first(0)
            for l in range(LAYERS):
                base = l * UL
                for k in range(KT):
                    act.wait_ge(t_ready, l * KT + k + 1)
                    A(act_hi[:, k, :], yT[:, k, :], ACT.Identity, bias=mod[:, l, k:k + 1])\
                        .then_inc(s_hi, 1)
                with loop(act, CB) as j:
                    n = 4 * l + j
                    for r in range(P1_ROLES):
                        hi_next(base, j, P1_ROLES, r)
                        if r == 0:
                            act.wait_ge(c_used, 1 + n)
                            A(u_buf[:], bank[0][:], ACT.Copy).then_inc(u_copied, 1)
                        if r == 3:
                            act.wait_ge(y_conv, 1 + n)
                            A(gate_buf[:], bank[3][:], ACT.Silu).then_inc(gate_done, 1)
                        if r == 4:
                            act.wait_ge(mixed, 1 + n)
                            A(wpool_now[:], wpool_sb[:, bass.ds(4 * l + j, 1), :].rearrange("p a d -> p (a d)"),
                              ACT.Copy).then_inc(wpool_ready, 1)
                            act.wait_ge(pooled, 1 + n)
                            A(p_buf[:, PAD:], bank[0][:], ACT.Copy).then_inc(p_copied, 1)
                        if r == 5:
                            act.wait_ge(y_pool, 1 + n)
                            A(gp_buf[:], bank[1][:], ACT.Silu).then_inc(gp_done, 1)
                act.wait_ge(y_pool, 1 + 4 * l + 4)
                act.wait_ge(y_conv, 1 + 4 * l + 4)
                act.wait_ge(unit_done, 1 + base + P1_UNITS + 1)
                for k in range(KT):
                    A(act_hi[:, k, :], yT[:, k, :], ACT.Copy).then_inc(s_hi, 1)
                act.wait_ge(s_lo, (2 * l + 2) * KT)
                with loop(act, KT // 2) as j:
                    for r in range(2):
                        hi_next(base + P1_UNITS, j, 2, r)
                        act.wait_ge(sq_added, (2 * l + 1) * KT + 2 * j + r)
                        A(sq[:], bank[r][:], ACT.Square).then_inc(sq_ready, 1)
                        act.wait_ge(sq_ready, (2 * l + 1) * KT + 2 * j + r + 1)
                        A(yT[:, bass.ds(2 * j + r, 1), :], bank[r][:].rearrange("p (a t) -> p a t", a=1), ACT.Copy)\
                            .then_inc(o_copied, 1)
                root(2 * l + 1)
                if l < LAYERS - 1:
                    for k in range(KT):
                        act.wait_ge(x_new, l * KT + k + 1)
                        square((2 * l + 2) * KT + k, xT[:, k, :])
                    root(2 * l + 2)

            for k in range(KT):
                act.wait_ge(x_new, (LAYERS - 1) * KT + k + 1)
                A(act_hi[:, k, :], xT[:, k, :], ACT.Copy).then_inc(s_hi, 1)
            act.wait_ge(x_kept, 16)
            act.wait_ge(s_lo, SP_X + KT)
            for r in range(2):
                hi_next(U_IDX, 0, 2, r)
                A(proj[:, N_PROJ - 2 + r, :], bank[r][:], ACT.Copy).then_inc(iq_copied, 1)
            act.wait_ge(unit_done, 1 + U_IDX + 2 + 2)
            act.wait_ge(raw_loaded[U_PROJ % 2 ^ 1], 16 * ((U_PROJ + 1) // 2 + 1))
            A(w_hi[(U_PROJ + 1) % 2][:], w_raw[(U_PROJ + 1) % 2][:], ACT.Copy).then_inc(hi_ready, 1)
            for g in range(4):
                A(proj[32 * g:32 * g + 32, N_PROJ - 3, :], bank[2][0:32, :], ACT.Copy).then_inc(ik_copied, 1)
            A(index_tmp, bank[2][0:64, :], ACT.Copy).then_inc(ik_copied, 1)
            act.sem_inc(relu_done, 1)
            m = 0
            for i in range(SEL0, TT):
                for h in range(IH):
                    act.wait_ge(score_mm, m + 1)
                    act.wait_ge(score_added, max(m - 1, 0))
                    if m == 1:
                        act.wait_ge(iwT_done, 1)
                    A(relu_buf[m % 2][:, 0:keys(i)], bank[m % 2][:, 0:keys(i)], ACT.Relu).then_inc(relu_done, 1)
                    m += 1
            act.wait_ge(dist_iota, 1)
            A(buf_a[:], buf_a[:], ACT.Abs).then_inc(dist_signed, 1)
            act.wait_ge(dist_signed, 1)
            A(dist_bias[:], buf_a[:], ACT.Copy, scale=-1.0).then_inc(dist_signed, 1)
            act.sem_inc(p3_copied, 2)
            with loop(act, N_PROJ // 2 - 1) as j:
                for r in range(2):
                    hi_next(U_PROJ, j, 2, r)
                    A(proj[:, bass.ds(2 * j + r, 1), :], bank[r][:].rearrange("p (a t) -> p a t", a=1), ACT.Copy)\
                        .then_inc(p3_copied, 1)
            for r in range(2):
                act.wait_ge(unit_done, 1 + U_OUT2 - 2 + r + 2)
                A(proj[:, N_PROJ - 2 + r, :], bank[r][:], ACT.Copy).then_inc(p3_copied, 1)
            act.wait_ge(p3_copied, 1 + N_PROJ + 1)
            for b in (2, 3, 0, 1):
                A(proj[:, b, :], proj[:, b, :], ACT.Gelu_apprx_tanh).then_inc(gelu_done, 1)
            for n, b in enumerate(NATURAL):
                act.wait_ge(nat_done, n + 1)
                A(proj[:, b, :], bank[n % 4][:], ACT.Copy).then_inc(nat_copied, 1)
            act.wait_ge(wsT_done, 1)
            A(wsT, bank[0][:, 0:AG * P].rearrange("p (g t) -> p g t", g=AG), ACT.Copy).then_inc(wsT_copied, 1)
            act.wait_ge(ln_var, 1)
            A(ln_stat[:, 1], ln_stat[:, 1], ACT.Sqrt).then_inc(ln_rstd, 1)
            for b in range(2):
                act.wait_ge(mix_ready, b + 1)
                A(act_hi[:, b, :], gm_tmp[:, b, :], ACT.Copy).then_inc(s_hi, 1)

            g = 0
            for i in range(TT):
                for it in range(6):
                    item = 6 * i + it
                    act.wait_ge(max_ready, item + 1)
                    for m in range(2):
                        A(prob[2 * (item % 2) + m][:, 0:keys(i)], bank[m][:, 0:keys(i)], ACT.Exp,
                          bias=neg_max[:, m:m + 1], scale=BQK ** -0.5,
                          accum_out=den[:, item % 2, m:m + 1]).then_inc(exp_done, 1)
                    for k in range(1 if it < BH else 2):
                        act.wait_ge(pT_done, g + 1)
                        if g >= 2:
                            act.wait_ge(pv_done, g - 1)
                        A(probT[g % 2][:, 0:keys(i)], bank[2][:, 0:keys(i)], ACT.Copy).then_inc(pT_copied, 1)
                        g += 1
                act.wait_ge(pv_done, g)
                A(proj[:, 0:BH, i * P:(i + 1) * P], bank[3][:, 0:HALF].rearrange("p (h t) -> p h t", h=BH), ACT.Copy)\
                    .then_inc(o_taken, 1)
                A(act_hi[:, 6:8, i * P:(i + 1) * P], bank[3][:, HALF:HALF + 2 * P].rearrange("p (h t) -> p h t", h=2),
                  ACT.Copy).then_inc(o_taken, 1)

            def hi_plain(u):
                act.wait_ge(raw_loaded[u % 2], 16 * (u // 2 + 1))
                act.wait_ge(unit_done, 1 + u)
                A(w_hi[u % 2][:], w_raw[u % 2][:], ACT.Copy).then_inc(hi_ready, 1)

            hi_plain(U_OUT2)
            hi_plain(U_OUT2 + 1)
            for h in range(BH):
                act.wait_ge(ob_stat, h)
                A(buf_b[:], proj[:, h, :], ACT.Square).then_inc(ob_sq, 1)
                act.wait_ge(ob_var, h + 1)
                A(buf_a[:], buf_a[:], ACT.Sqrt).then_inc(ob_rstd, 1)
                act.wait_ge(mix_ready, 2 + h + 1)
                A(act_hi[:, 2 + h, :], proj[:, h, :], ACT.Copy).then_inc(s_hi, 1)

            with loop(act, KT // 2) as j:
                for r in range(2):
                    hi_next(U_OUT2, j, 2, r)

            def layer_norm_act(q):
                for k in range(KT):
                    act.wait_ge(xc_ready, q * KT + k + 1)
                    if q * KT + k:
                        act.wait_ge(sq2_added, q * KT + k)
                    A(sq2[:], z[:, k, :], ACT.Square).then_inc(sq2_ready, 1)
                act.wait_ge(ln2_var, q + 1)
                A(rstd2[:], rstd2[:], ACT.Sqrt).then_inc(ln2_rstd, 1)

            layer_norm_act(0)
            for k in range(KT):
                act.wait_ge(ln_t, k + 1)
                A(act_hi[:, k, :], z[:, k, :], ACT.Identity, bias=params2[:, KT + k:KT + k + 1]).then_inc(s_hi, 1)

            for g, n in enumerate(GROUPS):
                act.wait_ge(unit_done, 1 + U_GROUP[g] + 1)
                with loop(act, n) as j:
                    f = FG * g + j
                    hi_next(U_GROUP[g], j, 2, 0)
                    act.wait_ge(f_mul, 1 + f)
                    A(silu_buf[:], bank[0][:], ACT.Silu).then_inc(g_act, 1)
                    hi_next(U_GROUP[g], j, 2, 1)
                    act.wait_ge(f_mul, 1 + f + 1)
                    A(f_hi[:, bass.ds(j, 1), :], f_buf[:].rearrange("p (a t) -> p a t", a=1), ACT.Copy)\
                        .then_inc(f_hi_done, 1)
                last = g == len(GROUPS) - 1
                with loop(act, KT // 2 - last) as j:
                    for r in range(2):
                        hi_next(U_GROUP[g] + 2 * n, j, 2, r)
            layer_norm_act(1)
            for k in range(KT):
                act.wait_ge(ln_t, KT + k + 1)
                A(z[:, k, :], z[:, k, :], ACT.Identity, bias=params2[:, 3 * KT + k:3 * KT + k + 1]).then_inc(x_final, 1)
            for t in range(TT):
                act.wait_ge(outT_done, t + 1)
                A(x_res[:, t, :], bank[t % 4][:], ACT.Copy).then_inc(out_copied, 1)

        @block.vector
        def _(dve):
            v = nc.vector
            own = Tally(dve, dve_own)
            for s_ in (c_used, y_conv, pooled, y_pool, f_mul):
                dve.sem_inc(s_, 1)
            dve.wait_ge(par_T, 1)
            own.did(v.tensor_copy(params[:, 0:N_ROWS], bank[0][:, 0:N_ROWS]))
            own.did(v.tensor_copy(params2[:, 0:N_ROWS2], bank[0][:, HALF:HALF + N_ROWS2]))
            dve.wait_ge(lam_loaded, 16 * 4)
            for m in range(2):
                own.did(v.tensor_tensor(lam_rows[:, 2 * m, :], lam_rows[:, 2 * m, :], lam_rows[:, 2 * m + 1, :],
                                        ALU.mult))
                own.did(v.tensor_reduce(lam[:, m:m + 1], lam_rows[:, 2 * m, :], AX.X, ALU.add))
            dve.sem_inc(par_ready, 1)
            for k in range(KT):
                dve.wait_ge(xT_done, k + 1)
                v.tensor_copy(xT[:, k, :], bank[1 + k % 2][:]).then_inc(xT_ready, 1)
            dve.wait_ge(silu_c, 1)
            dve.wait_ge(const_ready, 1)
            own.did(v.reciprocal(win_fix[:], win_fix[:]))
            n = 0
            for l in range(LAYERS):
                for third in range(3):
                    s = l * 3 + third
                    acc = ada_sum[s % 2]
                    if s >= 2:
                        dve.wait_ge(ada_col, s - 1)
                    for t in range(KT):
                        dve.wait_ge(ada_loaded[n % 4], 16 * (n // 4 + 1))
                        piece = ada_piece[n % 4]
                        if t == 0:
                            i = v.tensor_scalar(acc[:], piece, c_col[:, t:t + 1], None, ALU.mult)
                        else:
                            i = v.scalar_tensor_tensor(acc[:], piece, c_col[:, t:t + 1], acc[:], ALU.mult, ALU.add)
                        i.then_inc(ada_used, 1)
                        n += 1
                        dve.wait_ge(ada_used, n)
                    dve.sem_inc(ada_acc, 1)
            dve.wait_ge(ada_col, 3 * LAYERS)
            own.did(v.tensor_tensor(mod[:].rearrange("p l n -> p (l n)"), bank[3][:, 0:LAYERS * 3 * KT],
                                    params[:, ROW_B_ADA:ROW_G_PRE], ALU.add))
            for l in range(LAYERS):
                own.did(v.scalar_tensor_tensor(pre_gain[:, l], mod[:, l, KT:2 * KT], 1.0,
                                               params[:, ROW_G_PRE + l * KT:ROW_G_PRE + (l + 1) * KT],
                                               ALU.add, ALU.mult))
                own.did(v.tensor_tensor(post_gain[:, l], mod[:, l, 2 * KT:3 * KT],
                                        params[:, ROW_G_POST + l * KT:ROW_G_POST + (l + 1) * KT], ALU.mult))

            def variance(n):
                dve.wait_ge(stat_done, n + 1)
                own.did(v.tensor_scalar(rstd[:], bank[2][:], 1.0 / D, RMS_EPS, ALU.mult, ALU.add))
                v.reciprocal(rstd[:], rstd[:]).then_inc(var_ready, 1)
                dve.wait_ge(rstd_ready, n + 1)

            def lo_first(l):
                for r in range(2):
                    u = l * UL + r
                    dve.wait_ge(hi_ready, 1 + u + 2)
                    v.tensor_tensor(w_lo[r][:], w_raw[r][:], f32(w_hi[r][:]), ALU.subtract).then_inc(lo_ready, 1)

            def lo_next(base, j, per, r):
                dve.wait_ge(hi_ready, 1 + base + per * j + r + 4)
                s_ = (base + r) % 2
                v.tensor_tensor(w_lo[s_][:], w_raw[s_][:], f32(w_hi[s_][:]), ALU.subtract)\
                    .then_inc(lo_ready, 1)

            variance(0)
            dve.sem_inc(lo_ready, 2)
            lo_first(0)
            for l in range(LAYERS):
                base = l * UL
                for k in range(KT):
                    v.scalar_tensor_tensor(yT[:, k, :], xT[:, k, :], pre_gain[:, l, k:k + 1], rstd[:],
                                           ALU.mult, ALU.mult).then_inc(t_ready, 1)
                for k in range(KT):
                    dve.wait_ge(s_hi, 2 * l * KT + k + 1)
                    v.scalar_tensor_tensor(act_lo[:, k, :], yT[:, k, :], mod[:, l, k:k + 1], f32(act_hi[:, k, :]),
                                           ALU.add, ALU.subtract).then_inc(s_lo, 1)
                dve.wait_ge(s_lo, (2 * l + 1) * KT)
                with loop(dve, CB, own, 8) as j:
                    n = 4 * l + j

                    def col(row):
                        return params[:, bass.ds(row + j, 1)]

                    lo_next(base, j, P1_ROLES, 0)
                    lo_next(base, j, P1_ROLES, 1)
                    dve.wait_ge(u_copied, n + 1)
                    v.tensor_tensor(cu[:, TAPS - 1:], bank[1][:], u_buf[:], ALU.mult).then_inc(c_used, 1)
                    dve.wait_ge(c_used, 1 + n + 1)
                    tap = ROW_CONV + l * TAPS * CB
                    own.did(v.tensor_scalar(conv[:], cu[:, 0:T], col(tap), None, ALU.mult))
                    for k in range(1, TAPS):
                        own.did(v.scalar_tensor_tensor(conv[:], cu[:, k:k + T], col(tap + k * CB), conv[:],
                                                       ALU.mult, ALU.add))
                    lo_next(base, j, P1_ROLES, 2)
                    v.tensor_tensor(conv[:], bank[2][:], conv[:], ALU.mult).then_inc(b_used, 1)
                    dve.wait_ge(b_used, n + 1)
                    lo_next(base, j, P1_ROLES, 3)
                    dve.wait_ge(gate_done, 1 + n + 1)
                    v.tensor_tensor(yT[:, bass.ds(j, 1), :].rearrange("p a t -> p (a t)"), conv[:], gate_buf[:],
                                    ALU.mult).then_inc(y_conv, 1)
                    lo_next(base, j, P1_ROLES, 4)
                    dve.wait_ge(p_copied, 1 + n + 1)
                    own.did(v.tensor_tensor(win_a[:, PAD:], p_buf[:, PAD:], p_buf[:, PAD - 1:PAD - 1 + T], ALU.add))
                    src, dst = win_a, win_b
                    for k in range(len(WINDOWS) - 1):
                        s = 2 << k
                        own.did(v.scalar_tensor_tensor(dst[:, PAD:], src[:, PAD - s:PAD - s + T],
                                                       win_on[:, k, bass.ds(j, 1)], src[:, PAD:],
                                                       ALU.mult, ALU.add))
                        src, dst = dst, src
                    own.did(v.tensor_tensor(src[:, PAD:PAD + 16], src[:, PAD:PAD + 16],
                                            win_fix[:, bass.ds(j, 1), :].rearrange("p a t -> p (a t)"), ALU.mult))
                    v.scalar_tensor_tensor(win_a[:, PAD:], src[:, PAD:], win_inv[:, bass.ds(j, 1)], p_buf[:, PAD:],
                                           ALU.mult, ALU.subtract).then_inc(pooled, 1)
                    dve.wait_ge(pooled, 1 + n + 1)
                    lo_next(base, j, P1_ROLES, 5)
                    dve.wait_ge(gp_done, 1 + n + 1)
                    dve.wait_ge(mixed, 1 + n + 1)
                    v.scalar_tensor_tensor(yT[:, bass.ds(CB + j, 1), :].rearrange("p a t -> p (a t)"), bank[2][:],
                                           col(ROW_PSCALE + l * CB), gp_buf[:], ALU.mult, ALU.mult)\
                        .then_inc(y_pool, 1)
                for k in range(KT):
                    dve.wait_ge(s_hi, (2 * l + 1) * KT + k + 1)
                    v.tensor_tensor(act_lo[:, k, :], yT[:, k, :], f32(act_hi[:, k, :]), ALU.subtract)\
                        .then_inc(s_lo, 1)
                with loop(dve, KT // 2) as j:
                    for r in range(2):
                        lo_next(base + P1_UNITS, j, 2, r)
                variance(2 * l + 1)
                dve.wait_ge(o_copied, 1 + KT * (l + 1) + 1)
                for k in range(KT):
                    own.did(v.scalar_tensor_tensor(yT[:, k, :], yT[:, k, :], post_gain[:, l, k:k + 1], rstd[:],
                                                   ALU.mult, ALU.mult))
                    v.tensor_tensor(xT[:, k, :], xT[:, k, :], yT[:, k, :], ALU.add).then_inc(x_new, 1)
                if l < LAYERS - 1:
                    variance(2 * l + 2)

            dve.wait_ge(lam_exp, 1)
            own.did(v.tensor_tensor(lam[:, 0:1], lam[:, 1:2], lam[:, 0:1], ALU.subtract))
            own.did(v.tensor_scalar(lam[:, 0:1], lam[:, 0:1], LAM_INIT, None, ALU.subtract))
            own.did(v.tensor_scalar(sub_gain[:], params2[:, ROW2_SUB:N_ROWS2], 1.0 - LAM_INIT, None, ALU.mult))
            own.did(v.memset(bit_val[:], 1))
            own.did(v.tensor_tensor(bit_val[:, 0:BITS], bit_val[:, 0:BITS], bit_no[:, 0:BITS],
                                    ALU.logical_shift_left))
            for k in range(KT):
                dve.wait_ge(s_hi, SP_X + k + 1)
                v.tensor_tensor(act_lo[:, k, :], xT[:, k, :], f32(act_hi[:, k, :]), ALU.subtract).then_inc(s_lo, 1)
            for r in range(2):
                lo_next(U_IDX, 0, 2, r)
            dve.wait_ge(hi_ready, 1 + U_PROJ + 3)
            q = (U_PROJ + 1) % 2
            v.tensor_tensor(w_lo[q][:], w_raw[q][:], f32(w_hi[q][:]), ALU.subtract).then_inc(lo_ready, 1)
            dve.wait_ge(iwT_done, 1)
            v.tensor_scalar(index_w[:], bank[3][:, 0:TT * 64].rearrange("p (t c) -> p t c", c=64)[:, :, ID:ID + IH],
                            (IH * ID) ** -0.5, None, ALU.mult).then_inc(iw_ready, 1)
            dve.wait_ge(iw_ready, 1)
            m = 0
            for i in range(SEL0, TT):
                sc = score[:, sel_at(i):sel_at(i) + keys(i)]
                for h in range(IH):
                    dve.wait_ge(relu_done, m + 2)
                    r = relu_buf[m % 2][:, 0:keys(i)]
                    if h == 0:
                        x_ = v.tensor_scalar(sc, r, index_w[:, i, h:h + 1], None, ALU.mult)
                    else:
                        x_ = v.scalar_tensor_tensor(sc, r, index_w[:, i, h:h + 1], sc, ALU.mult, ALU.add)
                    x_.then_inc(score_added, 1)
                    m += 1
                    dve.wait_ge(score_added, m)
                own.did(v.memset(score[0:CHUNK, sel_at(i) + keys(i) - CHUNK:sel_at(i) + keys(i)], -3.0e38))

            def tile(i):
                return score[:, sel_at(i):sel_at(i) + keys(i)]

            for q, i in enumerate(range(SEL0, TT)):
                own.did(v.tensor_scalar(buf_b[:, 0:keys(i)], tile(i), 0.0, 0.0, ALU.is_ge, ALU.add,
                                        accum_out=cnt[:, q:q + 1]))
            own.did(v.tensor_scalar(sign[:], cnt[:], float(TOPK), None, ALU.is_ge))
            for q, i in enumerate(range(SEL0, TT)):
                n = keys(i)
                own.did(v.tensor_scalar(need[:, q:q + 1], sign[:, q:q + 1], float(2 * TOPK - 1 - n),
                                        float(n - TOPK + 1), ALU.mult, ALU.add))
            own.did(v.tensor_scalar(sign[:], sign[:], 2.0, -1.0, ALU.mult, ALU.add))
            for q, i in enumerate(range(SEL0, TT)):
                own.did(v.tensor_scalar(tile(i), tile(i), sign[:, q:q + 1], None, ALU.mult))
            own.did(v.memset(thr[:], 0))

            def bit_step(s_):
                own.did(v.tensor_scalar(cand[:], thr[:], bit_val[:, bass.ds(s_, 1)], None, ALU.bitwise_or))
                for q, i in enumerate(range(SEL0, TT)):
                    own.did(v.tensor_scalar(buf_b[:, 0:keys(i)], tile(i), f32(cand[:, q:q + 1]), 0.0,
                                            ALU.is_ge, ALU.add, accum_out=cnt[:, q:q + 1]))
                own.did(v.tensor_tensor(flag[:], cnt[:], need[:], ALU.is_ge))
                own.did(v.scalar_tensor_tensor(thr[:], flag[:], bit_no[:, bass.ds(s_, 1)], thr[:],
                                               ALU.logical_shift_left, ALU.bitwise_or))

            with loop(dve, N_PROJ // 2 - 1, own, 3 * (3 + N_TS)) as j:
                for r in range(2):
                    lo_next(U_PROJ, j, 2, r)
                    for s_ in range(2 - r):
                        bit_step(3 * j + 2 * r + s_)
            bit_step(BITS - 1)
            own.did(v.tensor_tensor(thr_s[:], f32(thr[:]), sign[:], ALU.mult))
            for q, i in enumerate(range(SEL0, TT)):
                n, t1 = keys(i), thr_s[:, q:q + 1]
                pre, eq = bank[3][:, 0:n], buf_b[:, 0:n]
                own.did(v.tensor_scalar(tile(i), tile(i), sign[:, q:q + 1], None, ALU.mult))
                own.did(v.tensor_scalar(eq, tile(i), t1, 0.0, ALU.is_gt, ALU.add, accum_out=cnt[:, q:q + 1]))
                own.did(v.tensor_scalar(cnt[:, q:q + 1], cnt[:, q:q + 1], -1.0, float(TOPK), ALU.mult, ALU.add))
                own.did(v.tensor_scalar(eq, tile(i), t1, None, ALU.is_equal))
                own.did(v.tensor_tensor_scan(pre, eq, eq, 0.0, ALU.bypass, ALU.add))
                own.did(v.scalar_tensor_tensor(eq, pre, cnt[:, q:q + 1], eq, ALU.is_le, ALU.mult))
                own.did(v.scalar_tensor_tensor(eq, tile(i), t1, eq, ALU.is_gt, ALU.add))
                own.did(v.tensor_scalar(sel_bias[:, sel_at(i):sel_at(i) + n], eq, -1.0, -MASKED, ALU.add, ALU.mult))
            dve.sem_inc(sel_done, 1)

            dve.wait_ge(wsT_copied, 1)
            v.memset(wsT[CHUNK:P, :, 0:CHUNK], 0.0).then_inc(ws_masked, 1)
            dve.wait_ge(nat_copied, 2)
            vv = proj[:, 2:4, :].rearrange("p b (n c) -> p (b n) c", c=AD)
            G = vv.shape[1]
            tmp = gm_tmp.rearrange("p b (n c) -> p (b n) c", c=AD)
            mean, var = ln_stat[:, 0], ln_stat[:, 1]
            own.did(v.tensor_reduce(mean, vv, AX.X, ALU.add))
            own.did(v.tensor_scalar(mean, mean, 1.0 / AD, None, ALU.mult))
            own.did(v.tensor_tensor(vv, vv, mean.unsqueeze(2).broadcast_to([P, G, AD]), ALU.subtract))
            own.did(v.tensor_tensor(tmp, vv, vv, ALU.mult))
            own.did(v.tensor_reduce(var, tmp, AX.X, ALU.add))
            own.did(v.tensor_scalar(var, var, 1.0 / AD, LN_EPS, ALU.mult, ALU.add))
            v.reciprocal(var, var).then_inc(ln_var, 1)
            dve.wait_ge(ln_rstd, 1)
            own.did(v.tensor_tensor(vv, vv, var.unsqueeze(2).broadcast_to([P, G, AD]), ALU.mult))
            dve.wait_ge(gm_loaded, 16 * 7)
            for b in range(2):
                w = proj[:, 2 + b, :].rearrange("p (t c) -> p t c", c=P)
                for row, op in ((ln_g_row, ALU.mult), (ln_b_row, ALU.add)):
                    own.did(v.tensor_tensor(w, w, row[:, b * P:(b + 1) * P].unsqueeze(1).broadcast_to([P, TT, P]), op))
            dve.sem_inc(v_normed, 1)
            dve.wait_ge(gm_done, 1)
            for b in range(2):
                t3 = gm_tmp[:, b, :].rearrange("p (t c) -> p t c", c=P)
                own.did(v.tensor_tensor(t3, bank[b][:].rearrange("p (t c) -> p t c", c=P),
                                        bs_tab[:, b, :].unsqueeze(1).broadcast_to([P, TT, P]), ALU.add))
                dve.wait_ge(gelu_done, 4)
                v.tensor_tensor(gm_tmp[:, b, :], gm_tmp[:, b, :], proj[:, b, :], ALU.mult).then_inc(mix_ready, 1)
            for b in range(2):
                dve.wait_ge(s_hi, SP_MIX + b + 1)
                v.tensor_tensor(act_lo[:, b, :], gm_tmp[:, b, :], f32(act_hi[:, b, :]), ALU.subtract)\
                    .then_inc(s_lo, 1)
            dve.wait_ge(s_lo, SP_MIX + 2)

            g = 0
            for i in range(TT):
                n = keys(i)
                for it in range(6):
                    item = 6 * i + it
                    dve.wait_ge(logits_done, item + 1)
                    if item:
                        dve.wait_ge(exp_done, 2 * item)
                    for m in range(2):
                        own.did(v.tensor_reduce(neg_max[:, m:m + 1], bank[m][:, 0:n], AX.X, ALU.max, negate=True))
                    v.tensor_scalar(neg_max[:], neg_max[:], BQK ** -0.5, None, ALU.mult).then_inc(max_ready, 1)
                    dve.wait_ge(exp_done, 2 * item + 2)
                    p0, p1 = (prob[2 * (item % 2) + m][:, 0:n] for m in range(2))
                    own.did(v.reciprocal(den_r[:], den[:, item % 2]))
                    if it < BH:
                        own.did(v.tensor_tensor(den_r[:, 1:2], den_r[:, 1:2], lam[:, 0:1], ALU.mult))
                        own.did(v.tensor_scalar(p1, p1, den_r[:, 1:2], None, ALU.mult))
                        v.scalar_tensor_tensor(p0, p0, den_r[:, 0:1], p1, ALU.mult, ALU.add).then_inc(attn_ready, 1)
                        g += 1
                        dve.wait_ge(attn_ready, g)
                    else:
                        for p_, c_ in ((p0, 0), (p1, 1)):
                            v.tensor_scalar(p_, p_, den_r[:, c_:c_ + 1], None, ALU.mult).then_inc(attn_ready, 1)
                            g += 1
                        dve.wait_ge(attn_ready, g)
                dve.wait_ge(o_taken, 3 * i + 2)
                own.did(v.tensor_tensor(act_lo[:, 6:8, i * P:(i + 1) * P],
                                        bank[3][:, HALF:HALF + 2 * P].rearrange("p (h t) -> p h t", h=2),
                                        f32(act_hi[:, 6:8, i * P:(i + 1) * P]), ALU.subtract))
                dve.sem_inc(o_taken, 1)
            dve.sem_inc(attn_over, 1)

            def lo_plain(u):
                dve.wait_ge(hi_ready, 1 + u + 2)
                v.tensor_tensor(w_lo[u % 2][:], w_raw[u % 2][:], f32(w_hi[u % 2][:]), ALU.subtract)\
                    .then_inc(lo_ready, 1)

            lo_plain(U_OUT2)
            lo_plain(U_OUT2 + 1)
            for h in range(BH):
                dve.wait_ge(ob_stat, h + 1)
                own.did(v.tensor_scalar(buf_a[:], bank[h % 2][:], 1.0 / BV, LN_EPS, ALU.mult, ALU.add))
                v.reciprocal(buf_a[:], buf_a[:]).then_inc(ob_var, 1)
                dve.wait_ge(ob_rstd, h + 1)
                v.scalar_tensor_tensor(proj[:, h, :], proj[:, h, :], sub_gain[:], buf_a[:], ALU.mult, ALU.mult)\
                    .then_inc(mix_ready, 1)
                dve.wait_ge(s_hi, SP_MIX + 2 + h + 1)
                v.tensor_tensor(act_lo[:, 2 + h, :], proj[:, h, :], f32(act_hi[:, 2 + h, :]), ALU.subtract)\
                    .then_inc(s_lo, 1)
            dve.wait_ge(s_lo, SP_MIX + 6)

            dve.wait_ge(x_back, 16)
            dve.sem_inc(z_ready, 2)
            with loop(dve, KT // 2) as j:
                for r in range(2):
                    lo_next(U_OUT2, j, 2, r)
                    v.scalar_tensor_tensor(z[:, bass.ds(2 * j + r, 1), :].rearrange("p a t -> p (a t)"),
                                           x_res[:, bass.ds(2 * j + r, 1), :].rearrange("p a t -> p (a t)"),
                                           ALPHA, bank[r][:], ALU.mult, ALU.add).then_inc(z_ready, 1)

            def layer_norm_dve(q):
                pair = bank[2 - 2 * q]
                dve.wait_ge(mean_mm, q + 1)
                own.did(v.tensor_scalar(rstd2[:], pair[:], 1.0 / D, None, ALU.mult))
                for k in range(KT):
                    v.tensor_tensor(z[:, k, :], z[:, k, :], rstd2[:], ALU.subtract).then_inc(xc_ready, 1)
                dve.wait_ge(xc_ready, (q + 1) * KT)
                dve.wait_ge(var_mm, q + 1)
                own.did(v.tensor_scalar(rstd2[:], pair[:], 1.0 / D, LN_EPS, ALU.mult, ALU.add))
                v.reciprocal(rstd2[:], rstd2[:]).then_inc(ln2_var, 1)
                dve.wait_ge(ln2_rstd, q + 1)
                for k in range(KT):
                    v.scalar_tensor_tensor(z[:, k, :], z[:, k, :], params2[:, ROW2_LN[q] + k:ROW2_LN[q] + k + 1],
                                           rstd2[:], ALU.mult, ALU.mult).then_inc(ln_t, 1)

            dve.wait_ge(z_ready, 1 + KT + 1)
            layer_norm_dve(0)
            for k in range(KT):
                shift = params2[:, KT + k:KT + k + 1]
                dve.wait_ge(s_hi, SP_X1 + k + 1)
                v.scalar_tensor_tensor(act_lo[:, k, :], z[:, k, :], shift, f32(act_hi[:, k, :]),
                                       ALU.add, ALU.subtract).then_inc(s_lo, 1)
                v.tensor_scalar(z[:, k, :], z[:, k, :], shift, ALPHA, ALU.add, ALU.mult).then_inc(acc_init, 1)
            dve.wait_ge(acc_init, KT)
            dve.sem_inc(acc_added, 2)
            for g, n in enumerate(GROUPS):
                last = g == len(GROUPS) - 1
                dve.wait_ge(unit_done, 1 + U_GROUP[g] + 1)
                with loop(dve, n) as j:
                    f = FG * g + j
                    lo_next(U_GROUP[g], j, 2, 0)
                    lo_next(U_GROUP[g], j, 2, 1)
                    dve.wait_ge(g_act, 1 + f + 1)
                    v.tensor_tensor(f_buf[:], silu_buf[:], bank[1][:], ALU.mult).then_inc(f_mul, 1)
                    dve.wait_ge(f_hi_done, f + 1)
                    v.tensor_tensor(f_lo[:, bass.ds(j, 1), :].rearrange("p a t -> p (a t)"), f_buf[:],
                                    f32(f_hi[:, bass.ds(j, 1), :].rearrange("p a t -> p (a t)")), ALU.subtract)\
                        .then_inc(f_lo_done, 1)
                    dve.wait_ge(f_lo_done, f + 1)

                def accumulate(d, r):
                    zz = z[:, bass.ds(d, 1), :].rearrange("p a t -> p (a t)")
                    v.tensor_tensor(zz, bank[2 + r][:], zz, ALU.add).then_inc(acc_added, 1)

                base = U_GROUP[g] + 2 * n
                if last:
                    with loop(dve, KT // 2 - 1) as j:
                        for r in range(2):
                            lo_next(base, j, 2, r)
                            accumulate(2 * j + r, r)
                    for r in range(2):
                        dve.wait_ge(unit_done, 1 + U_END + r)
                        accumulate(KT - 2 + r, r)
                else:
                    with loop(dve, KT // 2) as j:
                        for r in range(2):
                            lo_next(base, j, 2, r)
                            accumulate(2 * j + r, r)
                dve.wait_ge(acc_added, 1 + (g + 1) * KT + 1)
            layer_norm_dve(1)

        @block.tensor
        def _(pe):
            mm = nc.tensor.matmul
            pe.sem_inc(mixed, 1)
            pe.wait_ge(const_ready, 1)
            pe.wait_ge(par_loaded, 16 * 11)
            nc.tensor.transpose(bank[0][:, 0:N_ROWS], params_raw[0:N_ROWS, :], identity[0:N_ROWS, 0:N_ROWS])
            nc.tensor.transpose(bank[0][:, HALF:HALF + N_ROWS2], params2_raw[0:N_ROWS2, :],
                                identity[0:N_ROWS2, 0:N_ROWS2]).then_inc(par_T, 1)
            pe.wait_ge(x_loaded, 16)
            for k in range(KT):
                if k >= 2:
                    pe.wait_ge(xT_ready, k - 1)
                for t in range(TT):
                    i = nc.tensor.transpose(bank[1 + k % 2][:, t * P:(t + 1) * P], yT[:, t, k * P:(k + 1) * P],
                                            identity[:])
                i.then_inc(xT_done, 1)

            def statistic(n, count):
                pe.wait_ge(sq_added, count)
                for h in range(2):
                    i = mm(bank[2][:, h * HALF:(h + 1) * HALF], ones[:], sq_sum[:, h * HALF:(h + 1) * HALF],
                           start=True, stop=True)
                i.then_inc(stat_done, 1)

            pe.wait_ge(xT_ready, KT)
            statistic(0, KT)
            for s in range(3 * LAYERS):
                pe.wait_ge(ada_acc, s + 1)
                acc = ada_sum[s % 2]
                for k in range(KT):
                    i = mm(bank[3][:, s * KT + k:s * KT + k + 1], acc[:, k * P:(k + 1) * P], ones[:, 0:1],
                           start=True, stop=True)
                i.then_inc(ada_col, 1)
            pe.sem_inc(unit_done, 2)

            def product(u, slot, pair, split=None, kt=KT, hi=act_hi, lo=act_lo, sems=(s_hi, s_lo)):
                pe.wait_ge(hi_ready, 1 + u + 2)
                pe.wait_ge(lo_ready, 1 + u + 2)
                for k in range(kt):
                    if split is not None:
                        pe.wait_ge(sems[0], split + k + 1)
                        pe.wait_ge(sems[1], split + k + 1)
                    for w, a in ((w_hi, hi), (w_hi, lo), (w_lo, hi)):
                        for h in range(2):
                            i = mm(bank[pair][:, h * HALF:(h + 1) * HALF], w[slot][:, k, :],
                                   a[:, k, h * HALF:(h + 1) * HALF],
                                   start=(k == 0 and w is w_hi and a is hi), stop=(k == kt - 1 and w is w_lo))
                i.then_inc(unit_done, 1)

            for l in range(LAYERS):
                base = l * UL
                pe.wait_ge(var_ready, 2 * l + 1)
                with loop(pe, CB) as j:
                    n = 4 * l + j
                    u = base + P1_ROLES * j
                    pe.wait_ge(p_copied, 1 + n)
                    product(u, 0, 0, split=2 * l * KT)
                    pe.wait_ge(gp_done, 1 + n)
                    product(u + 1, 1, 1)
                    pe.wait_ge(y_pool, 1 + n)
                    product(u + 2, 0, 2)
                    pe.wait_ge(gate_done, 1 + n)
                    product(u + 3, 1, 3)
                    pe.wait_ge(u_copied, n + 1)
                    product(u + 4, 0, 0)
                    pe.wait_ge(c_used, 1 + n + 1)
                    product(u + 5, 1, 1)
                    pe.wait_ge(pooled, 1 + n + 1)
                    pe.wait_ge(wpool_ready, n + 1)
                    for h in range(2):
                        i = mm(bank[2][:, h * HALF:(h + 1) * HALF], wpool_now[:],
                               win_a[:, PAD + h * HALF:PAD + (h + 1) * HALF], start=True, stop=True)
                    i.then_inc(mixed, 1)
                pe.wait_ge(gp_done, 1 + 4 * l + 4)
                with loop(pe, KT // 2) as j:
                    for r in range(2):
                        pe.wait_ge(o_copied, 1 + KT * l + 2 * j + r)
                        product(base + P1_UNITS + 2 * j + r, r, r, split=(2 * l + 1) * KT if r == 0 else None)
                pe.wait_ge(y_pool, 1 + 4 * l + 4)
                statistic(2 * l + 1, (2 * l + 2) * KT)
                if l < LAYERS - 1:
                    statistic(2 * l + 2, (2 * l + 3) * KT)

            tr = nc.tensor.transpose
            pe.wait_ge(o_copied, 1 + KT * LAYERS + 1)
            pe.wait_ge(var_ready, 2 * LAYERS)
            product(U_IDX, 0, 0, split=SP_X)
            product(U_IDX + 1, 1, 1)
            product(U_IDX + 2, 0, 2)
            pe.wait_ge(ik_copied, 5)
            for t in range(TT):
                i_ = tr(bank[3][:, t * 64:(t + 1) * 64], index_tmp[:, t * P:(t + 1) * P], identity[0:64, 0:64])
            i_.then_inc(iwT_done, 1)
            pe.wait_ge(iq_copied, 2)
            m = 0
            for i in range(SEL0, TT):
                for h in range(IH):
                    pe.wait_ge(relu_done, m)
                    at = slice(32 * (h % 4), 32 * (h % 4) + 32)
                    for a, w in pieces(keys(i)):
                        i_ = mm(bank[m % 2][:, a:a + w], proj[at, N_PROJ - 2 + h // 4, i * P:(i + 1) * P],
                                proj[at, N_PROJ - 3, a:a + w], start=True, stop=True)
                    i_.then_inc(score_mm, 1)
                    m += 1
            pe.wait_ge(relu_done, m + 1)
            with loop(pe, N_PROJ // 2) as j:
                for r in range(2):
                    pe.wait_ge(p3_copied, 1 + 2 * j + r)
                    product(U_PROJ + 2 * j + r, (U_PROJ + r) % 2, r)
            pe.wait_ge(p3_copied, 1 + N_PROJ + 1)
            pe.wait_ge(gelu_done, 2)
            for n, b in enumerate(NATURAL):
                if n == 3:
                    pe.wait_ge(sel_done, 1)
                if n >= 4:
                    pe.wait_ge(nat_copied, n - 3)
                for t in range(TT):
                    i_ = tr(bank[n % 4][:, t * P:(t + 1) * P], proj[:, b, t * P:(t + 1) * P], identity[:])
                i_.then_inc(nat_done, 1)
            pe.wait_ge(gm_loaded, 16 * 7)
            pe.wait_ge(nat_copied, len(NATURAL))
            for g in range(AG):
                i_ = tr(bank[0][:, g * P:(g + 1) * P], ws_raw[:, g, :], identity[:])
            i_.then_inc(wsT_done, 1)
            pe.wait_ge(ws_masked, 1)
            pe.wait_ge(v_normed, 1)
            for b in range(2):
                for gg in range(2):
                    for t in range(TT):
                        i_ = mm(bank[b][AD * gg:AD * (gg + 1), t * P:(t + 1) * P],
                                proj[:, 2 + b, t * P + AD * gg:t * P + AD * (gg + 1)], wsT[:, 2 * b + gg, :],
                                start=True, stop=True)
            i_.then_inc(gm_done, 1)
            pe.wait_ge(dist_ready, 1)
            pe.wait_ge(s_lo, SP_MIX + 2)

            def logits(i, it):
                item = 6 * i + it
                if item:
                    pe.wait_ge(exp_done, 2 * item)
                for m in range(2):
                    at = slice(64 * m, 64 * m + 64)
                    if it < BH:
                        q, k, slope = PB_BQ + it, PB_BK + it, it
                    else:
                        q, k, slope = PB_CQ + it - BH, PB_CK + it - BH, 2 * (it - BH) + m
                    for a, w in pieces(keys(i)):
                        o = bank[m][:, a:a + w]
                        mm(o, slope_id[:, slope, :], dist_bias[:, (TT - 1 - i) * P + a:(TT - 1 - i) * P + a + w],
                           start=True, stop=False)
                        if it >= BH and i >= SEL0:
                            mm(o, one_id[:], sel_bias[:, sel_at(i) + a:sel_at(i) + a + w], start=False, stop=False)
                        i_ = mm(o, proj[at, q, i * P:(i + 1) * P], proj[at, k, a:a + w], start=False, stop=True)
                i_.then_inc(logits_done, 1)

            logits(0, 0)
            g = 0
            for i in range(TT):
                if i:
                    pe.wait_ge(o_taken, 3 * i)
                for it in range(6):
                    item = 6 * i + it
                    n_g = 1 if it < BH else 2
                    for k in range(n_g):
                        pe.wait_ge(attn_ready, g + 1)
                        if g:
                            pe.wait_ge(pT_copied, g)
                        for t in range(i + 1):
                            i_ = tr(bank[2][:, t * P:(t + 1) * P], prob[2 * (item % 2) + k][:, t * P:(t + 1) * P],
                                    identity[:])
                        i_.then_inc(pT_done, 1)
                        if k == n_g - 1 and item + 1 < 6 * TT:
                            logits(*divmod(item + 1, 6))
                        pe.wait_ge(pT_copied, g + 1)
                        for t in range(i + 1):
                            if it < BH:
                                o = bank[3][:, it * P:(it + 1) * P]
                                w = proj[:, PB_BV + it, t * P:(t + 1) * P]
                            else:
                                o = bank[3][64 * k:64 * k + 64, HALF + (it - BH) * P:HALF + (it - BH + 1) * P]
                                w = proj[:, PB_CV + it - BH, t * P + 64 * k:t * P + 64 * k + 64]
                            i_ = mm(o, w, probT[g % 2][:, t * P:(t + 1) * P], start=(t == 0), stop=(t == i))
                        i_.then_inc(pv_done, 1)
                        g += 1

            pe.wait_ge(o_taken, 3 * TT)
            for h in range(BH):
                pe.wait_ge(ob_sq, h + 1)
                for a in range(2):
                    i_ = mm(bank[h % 2][:, a * HALF:(a + 1) * HALF], ones[:], buf_b[:, a * HALF:(a + 1) * HALF],
                            start=True, stop=True)
                i_.then_inc(ob_stat, 1)
            pe.wait_ge(s_hi, SP_MIX + 2 + BH)
            pe.wait_ge(s_lo, SP_MIX + 2 + BH)
            with loop(pe, KT // 2) as j:
                for r in range(2):
                    pe.wait_ge(z_ready, 1 + 2 * j + r)
                    product(U_OUT2 + 2 * j + r, (U_OUT2 + r) % 2, r)

            def layer_norm_pe(q):
                for ready, count, done in ((z_added, (q + 1) * KT, mean_mm), (sq2_added, (q + 1) * KT, var_mm)):
                    pe.wait_ge(ready, count)
                    if done is var_mm:
                        pe.wait_ge(xc_ready, q * KT + 1)
                    for a in range(2):
                        i_ = mm(bank[2 - 2 * q][:, a * HALF:(a + 1) * HALF], ones[:], sum2[:, a * HALF:(a + 1) * HALF],
                                start=True, stop=True)
                    i_.then_inc(done, 1)

            layer_norm_pe(0)
            pe.wait_ge(ln_t, 1)
            for g, n in enumerate(GROUPS):
                with loop(pe, n) as j:
                    f = FG * g + j
                    for r, pair_used in ((0, g_act), (1, f_mul)):
                        pe.wait_ge(pair_used, 1 + f)
                        product(U_GROUP[g] + 2 * j + r, (U_GROUP[g] + r) % 2, r,
                                split=SP_X1 if g == 0 and r == 0 else None)
                with loop(pe, KT // 2) as j:
                    for r in range(2):
                        pe.wait_ge(acc_added, 1 + g * KT + 2 * j + r)
                        product(U_GROUP[g] + 2 * n + 2 * j + r, (U_GROUP[g] + r) % 2, 2 + r,
                                split=FG * g if r == 0 else None, kt=n, hi=f_hi, lo=f_lo,
                                sems=(f_hi_done, f_lo_done))
            layer_norm_pe(1)
            pe.wait_ge(x_final, KT)
            for t in range(TT):
                if t >= 4:
                    pe.wait_ge(out_copied, t - 3)
                for k in range(KT):
                    i_ = tr(bank[t % 4][:, k * P:(k + 1) * P], z[:, k, t * P:(t + 1) * P], identity[:])
                i_.then_inc(outT_done, 1)



_INS = ['x', 'c', 'w_ada', 'b_ada', 'g_pre', 'w_in', 'w_conv', 'w_pool', 'pool_scale', 'w_out', 'g_post', 'w_in_2',
        'gmlp_w_s_2', 'gmlp_b_s_2', 'gmlp_ln_g_2', 'gmlp_ln_b_2', 'lam_q1_2', 'lam_k1_2', 'lam_q2_2', 'lam_k2_2',
        'diff_subln_g_2', 'w_out_2', 'ln1_g_2', 'ln1_b_2', 'w_gu_2', 'w_down_2', 'ln2_g_2', 'ln2_b_2']


def kernel(**inputs):
    import numpy as np
    import concourse.bacc as bacc
    from concourse.bass_utils import run_bass_kernel_spmd

    nc = bacc.Bacc("TRN2", target_bir_lowering=False, num_devices=1)
    arrays, args = {}, []
    for name in _INS:
        a = np.ascontiguousarray(inputs[name])
        arrays[name] = a
        args.append(nc.dram_tensor(name, a.shape, mybir.dt.from_np(a.dtype), kind="ExternalInput").ap())
    out = nc.dram_tensor("out", (1, T, D), FP32, kind="ExternalOutput").ap()
    build(nc, *args, out)
    return run_bass_kernel_spmd(nc, [arrays], core_ids=[0]).results[0]["out"]
```

```python
import math
from contextlib import ExitStack, contextmanager

import concourse.bass as bass
from concourse import mybir

FP32 = mybir.dt.float32
FP32R = mybir.dt.float32r
INT32 = mybir.dt.int32
BF16 = mybir.dt.bfloat16
ALU = mybir.AluOpType
ACT = mybir.ActivationFunctionType
AX = mybir.AxisListType

P = 128
D = 1024
T = 1024
KT = D // P
TT = T // P
HALF = 512

LAYERS = 2
CW = D // 2
CB = CW // P
TAPS = 3
WINDOWS = (2, 4, 8, 16)
PAD = 8
RMS_EPS = 1e-6
P1_ROLES = 6
P1_UNITS = P1_ROLES * CB

AG, AD = 4, 64
A_W = AG * AD
BH, BQK, BV = 4, 64, 128
CH, CD = 4, 64
IH, ID = 8, 32
TOPK = 256
CHUNK = 64
OFF_B_Q = 2 * A_W
OFF_B_K = OFF_B_Q + BH * 2 * BQK
OFF_B_V = OFF_B_K + BH * 2 * BQK
OFF_C_Q = OFF_B_V + BH * BV
OFF_C_K = OFF_C_Q + CH * CD
OFF_C_V = OFF_C_K + CH * CD
OFF_I_Q = OFF_C_V + CH * CD
OFF_I_K = OFF_I_Q + IH * ID
IN_W = OFF_I_K + ID + IH
FFN = -(-8 * D // (3 * 256)) * 256
FB = FFN // P
ALPHA = 2 ** 0.25
LN_EPS = 1e-5
LAM_INIT = 0.8 - 0.6 * math.exp(-0.3 * 0)
MASKED = -(2.0 ** 100)

FG = 6
GROUPS = [min(FG, FB - g) for g in range(0, FB, FG)]
SEL0 = TOPK // P
N_TS = TT - SEL0
N_SEL = sum(i + 1 for i in range(SEL0, TT))
BITS = 31


def sel_at(i):
    return P * sum(j + 1 for j in range(SEL0, i))


N_PROJ = OFF_I_Q // P
PB_U, PB_V, PB_BQ, PB_BK, PB_BV = 0, A_W // P, OFF_B_Q // P, OFF_B_K // P, OFF_B_V // P
NATURAL = (12, 13, 14, 15, 20, 21, 2, 3)
N_EARLY = 4
ITEMS = BH + CH // 2
Q_BLOCKS = (4, 5, 6, 7, 16, 17)
MIX_CHUNKS = 4
PB_CQ, PB_CK, PB_CV = OFF_C_Q // P, OFF_C_K // P, OFF_C_V // P


class Tally:

    def __init__(self, eng, sem, start=0):
        self.eng, self.sem, self.n, self.off = eng, sem, start, 0

    def did(self, instruction):
        instruction.then_inc(self.sem, 1)
        self.n += 1
        self.eng.wait_ge(self.sem, self.n + self.off)


@contextmanager
def loop(eng, count, tally=None, per=0):
    start = tally.n if tally else 0
    with eng.Fori(0, count) as i:
        if tally:
            tally.off = i * per
        yield i
    if tally:
        assert tally.n - start == per, (tally.n - start, per)
        tally.n, tally.off = start + per * count, 0


def build(nc, x, c, w_ada, b_ada, g_pre, w_in, w_conv, w_pool, pool_scale, w_out, g_post,
          w_in_2, gmlp_w_s, gmlp_b_s, gmlp_ln_g, gmlp_ln_b, lam_q1, lam_k1, lam_q2, lam_k2,
          diff_subln_g, w_out_2, ln1_g, ln1_b, w_gu, w_down, ln2_g, ln2_b, out):
    w_in_v = w_in.rearrange("l (k p) n -> l p k n", p=P)
    w_out_v = w_out.rearrange("l (k p) n -> l p k n", p=P)
    w_in_2v = w_in_2[0].rearrange("(k p) n -> p k n", p=P)
    w_out_2v = w_out_2[0].rearrange("(k p) n -> p k n", p=P)
    w_gu_v = w_gu[0].rearrange("(k p) n -> p k n", p=P)
    w_down_v = w_down[0].rearrange("(k p) n -> p k n", p=P)
    x_mid = nc.dram_tensor("x_mid", [P, KT, T], FP32).ap()
    w_ada_v = w_ada.rearrange("l (p t) n -> l p t n", t=KT)

    with ExitStack() as ctx:
        def sb(name, shape, dt=FP32):
            return ctx.enter_context(nc.sbuf_tensor(name, shape, dt))

        def sem(name):
            return ctx.enter_context(nc.semaphore(name))

        with ExitStack() as inner:
            act_hi = inner.enter_context(nc.sbuf_tensor("act_hi", [P, KT, T], FP32R))
            act_lo = inner.enter_context(nc.sbuf_tensor("act_lo", [P, KT, T], FP32R))
        act_region = sb("act_region", [P, 2 * KT, T])
        gm_tmp = act_region[:, 2:4, :]
        junk = act_region[:, 4, :]
        c_nat = act_region[:, 5, 0:CH * CD]
        v_nat = act_region[:, KT + 2:KT + 4, :]
        ws_raw = act_region[:, KT + 4, 0:AG * P].rearrange("p (g s) -> p g s", g=AG)
        wsT = act_region[:, KT + 4, AG * P:2 * AG * P].rearrange("p (g t) -> p g t", g=AG)
        ln_g_row, ln_b_row = act_region[:, KT + 5, 0:A_W], act_region[:, KT + 5, A_W:2 * A_W]
        bs_tab = act_region[:, KT + 5, 512:512 + 2 * P].rearrange("p (b t) -> p b t", b=2)
        ln_stat = act_region[:, KT + 5, 768:832].rearrange("p (a g) -> p a g", a=2)
        identity = sb("identity", [P, P])
        ones = sb("ones", [P, P])
        params = sb("params", [P, P])
        params2 = sb("params2", [P, P])
        wpool_now = sb("wpool_now", [P, P])
        c_col = sb("c_col", [P, KT])
        mod = sb("mod", [P, LAYERS, 3 * KT])
        pre_gain = sb("pre_gain", [P, LAYERS, KT])
        post_gain = sb("post_gain", [P, LAYERS, KT])
        win_on = sb("win_on", [P, len(WINDOWS) - 1, CB])
        win_inv = sb("win_inv", [P, CB])
        win_fix = sb("win_fix", [P, CB, 16])
        iota_t = sb("iota_t", [P, 16])

        @contextmanager
        def over():
            with ExitStack() as inner:
                yield lambda name, shape, dt=FP32: inner.enter_context(nc.sbuf_tensor(name, shape, dt))

        with over() as t:
            w_raw = [t(f"w_raw{s}", [P, KT, P]) for s in range(2)]
            w_hi = [t(f"w_hi{s}", [P, KT, P], FP32R) for s in range(2)]
            w_lo = [t(f"w_lo{s}", [P, KT, P], FP32R) for s in range(2)]
        w_region = sb("w_region", [P, 6, T])

        ARENA = N_PROJ * T + N_SEL * P + 2 * T
        with over() as t:
            xT = t("xT", [P, KT, T])
            yT = t("yT", [P, KT, T])
            u_buf = t("u_buf", [P, T])
            cu = t("cu", [P, TAPS - 1 + T])
            conv = t("conv", [P, T])
            gate_buf = t("gate_buf", [P, T])
            p_buf = t("p_buf", [P, PAD + T])
            win_a = t("win_a", [P, PAD + T])
            win_b = t("win_b", [P, PAD + T])
            gp_buf = t("gp_buf", [P, T])
            sq = t("sq", [P, T])
            sq_sum = t("sq_sum", [P, T])
            rstd = t("rstd", [P, T])
            wpool_sb = t("wpool_sb", [P, LAYERS * len(WINDOWS), P])
        with over() as t:
            proj = t("proj", [P, N_PROJ, T])
            score = t("score", [P, N_SEL * P])
            buf_a = t("buf_a", [P, T])
            buf_b = t("buf_b", [P, T])
        with over() as t:
            t("under_proj", [P, N_PROJ, T])
            sel_bias = t("sel_bias", [P, N_SEL * P], FP32R)
            dist_bias = t("dist_bias", [P, T], FP32R)
        with over() as t:
            z = t("z", [P, KT, T])
            x_res = t("x_res", [P, KT, T])
        with over() as t:
            t("under_z", [P, KT, T])
            f_hi = t("f_hi", [P, FG, T], FP32R)
            f_lo = t("f_lo", [P, FG, T], FP32R)
            silu_buf = t("silu_buf", [P, T])
            f_buf = t("f_buf", [P, T])
            sq2 = t("sq2", [P, T])
            sum2 = t("sum2", [P, T])
            rstd2 = t("rstd2", [P, T])
        arena = sb("arena", [P, ARENA])
        index_tmp = buf_b[0:64, :]
        relu_buf = [buf_a, buf_b]
        prob = [w_region[:, i, :] for i in range(4)]
        probT = [w_region[:, 4 + i, :] for i in range(2)]
        slope_id = sb("slope_id", [P, BH, P], FP32R)
        one_id = sb("one_id", [P, P], FP32R)
        params_raw, params2_raw = w_region[:, 4, 0:P], w_region[:, 4, P:2 * P]
        lam_rows = w_region[:, 5, 0:4 * BQK].rearrange("p (a d) -> p a d", a=4)
        lam = sb("lam", [P, 2])
        sub_gain = sb("sub_gain", [P, 1])
        index_w = sb("index_w", [P, TT, IH])
        bit_no = sb("bit_no", [P, 32], INT32)
        bit_val = sb("bit_val", [P, 32], INT32)
        thr = sb("thr", [P, N_TS], INT32)
        cand = sb("cand", [P, N_TS], INT32)
        flag = sb("flag", [P, N_TS], INT32)
        cnt, need, sign, thr_s = (sb(n, [P, N_TS]) for n in ("cnt", "need", "sign", "thr_s"))
        neg_max = sb("neg_max", [P, 2, 2])
        o_ss = sb("o_ss", [P, TT, BH])
        den = sb("den", [P, 2, 2])
        den_r = sb("den_r", [P, 2])
        ada_sum = [conv, gate_buf]
        ada_piece = [u_buf[:], gp_buf[:], win_a[:, PAD:], win_b[:, PAD:]]
        bank = [ctx.enter_context(nc.psum_tensor(f"pair{i}", [P, T], FP32)) for i in range(4)]

        raw_loaded = [sem(f"raw_loaded{s}") for s in range(2)]
        hi_ready, lo_ready, unit_done = sem("hi_ready"), sem("lo_ready"), sem("unit_done")
        x_loaded, par_loaded, small_loaded = sem("x_loaded"), sem("par_loaded"), sem("small_loaded")
        ada_loaded = [sem(f"ada_loaded{s}") for s in range(4)]
        ada_used, ada_acc, ada_col, ada_ready = (sem(n) for n in ("ada_used", "ada_acc", "ada_col", "ada_ready"))
        const_ready = sem("const_ready")
        par_T, par_ready, xT_done, xT_ready = sem("par_T"), sem("par_ready"), sem("xT_done"), sem("xT_ready")
        silu_c = sem("silu_c")
        s_hi, s_lo = sem("s_hi"), sem("s_lo")
        t_ready = sem("t_ready")
        u_copied, c_used, b_used, gate_done, p_copied, gp_done = (
            sem(n) for n in ("u_copied", "c_used", "b_used", "gate_done", "p_copied", "gp_done"))
        y_conv, pooled, mixed, y_pool, wpool_ready = (
            sem(n) for n in ("y_conv", "pooled", "mixed", "y_pool", "wpool_ready"))
        o_copied, sq_ready, sq_added = sem("o_copied"), sem("sq_ready"), sem("sq_added")
        x_new = sem("x_new")
        stat_done, var_ready, rstd_ready = sem("stat_done"), sem("var_ready"), sem("rstd_ready")
        act_own, dve_own, pool_own = sem("act_own"), sem("dve_own"), sem("pool_own")
        lam_exp, dist_iota, dist_signed = sem("lam_exp"), sem("dist_iota"), sem("dist_signed")
        outT_done, out_copied, out_stored = sem("outT_done"), sem("out_copied"), sem("out_stored")

        ROW_B_ADA = 0
        ROW_G_PRE = ROW_B_ADA + LAYERS * 3 * KT
        ROW_G_POST = ROW_G_PRE + LAYERS * KT
        ROW_CONV = ROW_G_POST + LAYERS * KT
        ROW_PSCALE = ROW_CONV + LAYERS * TAPS * CB
        N_ROWS = ROW_PSCALE + LAYERS * CB

        def rows(ap2d):
            return ap2d.rearrange("l (r p) -> (l r) p", p=P)

        def f32(ap):
            return ap.bitcast(FP32)

        UL = P1_UNITS + KT

        U_IDX = LAYERS * UL
        U_PROJ = U_IDX + 3
        U_OUT2 = U_PROJ + N_PROJ
        U_FFN = U_OUT2 + KT
        U_GROUP = [U_FFN + sum(2 * n + KT for n in GROUPS[:g]) for g in range(len(GROUPS))]
        U_END = U_GROUP[-1] + 2 * GROUPS[-1] + KT

        ROW2_LN = [0, 2 * KT]
        ROW2_SUB = 4 * KT
        N_ROWS2 = ROW2_SUB + 1
        SP_X, SP_MIX = 2 * LAYERS * KT, (2 * LAYERS + 1) * KT
        SP_X1 = SP_MIX + MIX_CHUNKS + BH

        (x_kept, iq_copied, ik_copied, iwT_done, iw_ready, score_mm, relu_done, score_added, p3_copied,
         gm_loaded, gelu_done, nat_done, nat_copied, wsT_done, wsT_copied, ws_masked, v_normed, ln_var, ln_rstd,
         gm_done, mix_ready, dist_ready, logits_done, max_ready, exp_done, attn_ready, pT_done, pT_copied, pv_done,
         o_taken, ob_sq, ob_stat, ob_var, ob_rstd, sel_done, attn_over) = (sem(n) for n in (
             "x_kept", "iq_copied", "ik_copied", "iwT_done", "iw_ready", "score_mm", "relu_done", "score_added",
             "p3_copied", "gm_loaded", "gelu_done", "nat_done", "nat_copied", "wsT_done", "wsT_copied",
             "ws_masked", "v_normed", "ln_var", "ln_rstd", "gm_done", "mix_ready", "dist_ready", "logits_done",
             "max_ready", "exp_done", "attn_ready", "pT_done", "pT_copied", "pv_done", "o_taken", "ob_sq",
             "ob_stat", "ob_var", "ob_rstd", "sel_done", "attn_over"))
        (x_back, z_ready, z_added, mean_mm, xc_ready, sq2_ready, sq2_added, var_mm, ln2_var, ln2_rstd, ln_t,
         x_final, acc_init, g_act, f_mul, f_hi_done, f_lo_done, acc_added, outc, lam_loaded) = (sem(n) for n in (
             "x_back", "z_ready", "z_added", "mean_mm", "xc_ready", "sq2_ready", "sq2_added", "var_mm", "ln2_var",
             "ln2_rstd", "ln_t", "x_final", "acc_init", "g_act", "f_mul", "f_hi_done", "f_lo_done", "acc_added",
             "outc", "lam_loaded"))

        q_scaled, cT_done, c_hi, c_lo, obT_done, ob_normed, attn_last = (sem(n) for n in (
            "q_scaled", "cT_done", "c_hi", "c_lo", "obT_done", "ob_normed", "attn_last"))

        N_ITEMS = TT * ITEMS
        MIX_AT = 1
        cT_bank = bank[3][:, HALF + CH * CD:T].rearrange("p (b t) -> p b t", b=2)

        def groups_of(item):
            return 1 if item % ITEMS < BH else 2

        def group(item, k):
            return sum(groups_of(n) for n in range(item)) + k

        def o_nat(i):
            a, b = divmod(i, 4)
            return proj[:, 2 - 2 * a + b // 2, (b % 2) * HALF:(b % 2 + 1) * HALF]

        def keys(i):
            return P * (i + 1)

        def pieces(n):
            return [(a, min(HALF, n - a)) for a in range(0, n, HALF)]

        block = ctx.enter_context(nc.Block())

        @block.sync
        def _(sp):
            sp.dma_start(params_raw[ROW_B_ADA:ROW_G_PRE, :], rows(b_ada)).then_inc(par_loaded, 16)
            sp.dma_start(params_raw[ROW_G_PRE:ROW_G_POST, :], rows(g_pre)).then_inc(par_loaded, 16)
            sp.dma_start(params_raw[ROW_G_POST:ROW_CONV, :], rows(g_post)).then_inc(par_loaded, 16)
            sp.dma_start(params_raw[ROW_CONV:ROW_PSCALE, :],
                         w_conv.rearrange("l t (r p) -> (l t r) p", p=P)).then_inc(par_loaded, 16)
            sp.dma_start(params_raw[ROW_PSCALE:N_ROWS, :], rows(pool_scale)).then_inc(par_loaded, 16)
            sp.dma_start(c_col[:], c.rearrange("b (p t) -> (b p) t", t=KT)).then_inc(par_loaded, 16)
            for k in range(2):
                for i, a in enumerate(((ln1_g, ln1_b), (ln2_g, ln2_b))[k]):
                    sp.dma_start(params2_raw[ROW2_LN[k] + i * KT:ROW2_LN[k] + (i + 1) * KT, :], rows(a))\
                      .then_inc(par_loaded, 16)
            sp.dma_start(params2_raw[ROW2_SUB:N_ROWS2, :], diff_subln_g).then_inc(par_loaded, 16)
            for i, a in enumerate((lam_q1, lam_k1, lam_q2, lam_k2)):
                sp.dma_start(lam_rows[:, i, :], a.broadcast_to([P, BQK])).then_inc(lam_loaded, 16)
            sp.dma_start(yT[:], x[0].rearrange("(t p) f -> p t f", p=P)).then_inc(x_loaded, 16)
            sp.dma_start(wpool_sb[:], w_pool.rearrange("l g c d -> c (l g) d")).then_inc(small_loaded, 16)
            n = 0
            for l in range(LAYERS):
                for third in range(3):
                    for t in range(KT):
                        if n >= 4:
                            sp.wait_ge(ada_used, n - 3)
                        sp.dma_start(ada_piece[n % 4], w_ada_v[l, :, t, third * D:(third + 1) * D])\
                          .then_inc(ada_loaded[n % 4], 16)
                        n += 1

            def load(u, slot, src):
                sp.wait_ge(hi_ready, 1 + u)
                sp.wait_ge(lo_ready, 1 + u)
                sp.dma_start(w_raw[slot][:], src).then_inc(raw_loaded[slot], 16)

            for l in range(LAYERS):
                with loop(sp, CB) as j:
                    for r, start in enumerate((0, 2 * CW, CW, 3 * CW, 4 * CW, 5 * CW)):
                        load(l * UL + P1_ROLES * j + r, r % 2, w_in_v[l, :, :, bass.ds(start + j * P, P)])
                with loop(sp, KT // 2) as j:
                    for r in range(2):
                        load(l * UL + P1_UNITS + 2 * j + r, r, w_out_v[l, :, :, bass.ds((2 * j + r) * P, P)])
            load(U_IDX, 0, w_in_2v[:, :, OFF_I_Q:OFF_I_Q + P])
            load(U_IDX + 1, 1, w_in_2v[:, :, OFF_I_Q + P:OFF_I_K])
            sp.wait_ge(x_new, KT * LAYERS)
            sp.dma_start(x_mid, xT[:]).then_inc(x_kept, 16)
            sp.wait_ge(hi_ready, 1 + U_IDX + 2)
            sp.wait_ge(lo_ready, 1 + U_IDX + 2)
            sp.dma_start(w_raw[0][:, :, 0:IN_W - OFF_I_K], w_in_2v[:, :, OFF_I_K:IN_W])\
              .then_inc(raw_loaded[0], 16)
            with loop(sp, N_PROJ // 2) as j:
                for r in range(2):
                    load(U_PROJ + 2 * j + r, (U_PROJ + r) % 2, w_in_2v[:, :, bass.ds((2 * j + r) * P, P)])
            sp.wait_ge(unit_done, 1 + U_OUT2 + 1)
            sp.dma_start(ws_raw, gmlp_w_s[0].rearrange("g t s -> t g s")).then_inc(gm_loaded, 16)
            sp.dma_start(ln_g_row, gmlp_ln_g.rearrange("l g c -> l (g c)").broadcast_to([P, A_W]))\
              .then_inc(gm_loaded, 16)
            sp.dma_start(ln_b_row, gmlp_ln_b.rearrange("l g c -> l (g c)").broadcast_to([P, A_W]))\
              .then_inc(gm_loaded, 16)
            for g in range(AG):
                sp.dma_start(bs_tab[AD * (g % 2):AD * (g % 2 + 1), g // 2, :],
                             gmlp_b_s[0, g:g + 1, :].broadcast_to([AD, P])).then_inc(gm_loaded, 16)
            sp.wait_ge(pv_done, group(N_ITEMS, 0))
            sp.wait_ge(cT_done, TT)
            for r in range(2):
                u = U_OUT2 + r
                sp.dma_start(w_raw[u % 2][:], w_out_2v[:, :, r * P:(r + 1) * P]).then_inc(raw_loaded[u % 2], 16)
            sp.dma_start(x_res[:], x_mid).then_inc(x_back, 16)
            for r in range(2):
                load(U_OUT2 + 2 + r, (U_OUT2 + r) % 2, w_out_2v[:, :, (2 + r) * P:(3 + r) * P])
            with loop(sp, KT // 2 - 2) as j:
                for r in range(2):
                    load(U_OUT2 + 4 + 2 * j + r, (U_OUT2 + r) % 2, w_out_2v[:, :, bass.ds((2 * j + 4 + r) * P, P)])
            for g, n in enumerate(GROUPS):
                with loop(sp, n) as j:
                    for r in range(2):
                        load(U_GROUP[g] + 2 * j + r, (U_GROUP[g] + r) % 2,
                             w_gu_v[:, :, bass.ds(r * FFN + (g * FG + j) * P, P)])
                with loop(sp, KT // 2) as j:
                    for r in range(2):
                        u, slot = U_GROUP[g] + 2 * n + 2 * j + r, (U_GROUP[g] + r) % 2
                        sp.wait_ge(hi_ready, 1 + u)
                        sp.wait_ge(lo_ready, 1 + u)
                        sp.dma_start(w_raw[slot][:, 0:n, :],
                                     w_down_v[:, g * FG:g * FG + n, bass.ds((2 * j + r) * P, P)])\
                          .then_inc(raw_loaded[slot], 16)
            out_v = out[0].rearrange("(t p) f -> p t f", p=P)
            for t in range(TT):
                sp.wait_ge(out_copied, t + 1)
                sp.dma_start(out_v[:, t, :], x_res[:, t, :]).then_inc(out_stored, 16)
            sp.wait_ge(out_stored, 16 * TT)

        @block.gpsimd
        def _(pool):
            own = Tally(pool, pool_own)
            g = nc.gpsimd
            own.did(g.memset(identity[:], 0.0))
            own.did(g.affine_select(out=identity[:], in_=identity[:], compare_op=ALU.not_equal, fill=1.0,
                                    base=0, pattern=[[-1, P]], channel_multiplier=1))
            own.did(g.memset(ones[:], 1.0))
            own.did(g.memset(cu[:, 0:TAPS - 1], 0.0))
            for b in (p_buf, win_a, win_b):
                own.did(g.memset(b[:, 0:PAD], 0.0))
            for k in range(len(WINDOWS) - 1):
                for i in range(CB):
                    own.did(g.memset(win_on[:, k, i:i + 1], 1.0 if i > k else 0.0))
            for i, w in enumerate(WINDOWS):
                own.did(g.memset(win_inv[:, i:i + 1], 1.0 / w))
            own.did(g.iota(iota_t[:], pattern=[[1, 16]], base=1, channel_multiplier=0,
                           allow_small_or_imprecise_dtypes=True))
            for i, w in enumerate(WINDOWS):
                own.did(g.tensor_scalar(win_fix[:, i, :], iota_t[:], float(w), 1.0 / w, ALU.min, ALU.mult))
            own.did(g.iota(bit_no[:], pattern=[[-1, 32]], base=BITS - 1, channel_multiplier=0))
            own.did(g.tensor_copy(one_id[:], identity[:]))
            for h in range(BH):
                own.did(g.tensor_scalar(slope_id[:, h, :], identity[:], 2.0 ** (-8.0 * (h + 1) / BH),
                                        None, ALU.mult))
            pool.sem_inc(const_ready, 1)

            def add_squares(n, first):
                pool.wait_ge(sq_ready, n + 1)
                if first:
                    i = g.tensor_copy(sq_sum[:], sq[:])
                else:
                    i = g.tensor_tensor(sq_sum[:], sq_sum[:], sq[:], ALU.add)
                i.then_inc(sq_added, 1)

            for n in range(2 * LAYERS * KT):
                if n % KT == 0 and n:
                    pool.wait_ge(stat_done, n // KT)
                elif n:
                    pool.wait_ge(sq_added, n)
                add_squares(n, n % KT == 0)

            pool.wait_ge(score_added, N_TS * IH)
            pool.wait_ge(relu_done, N_TS * IH + 1)
            g.iota(buf_a[:], pattern=[[-1, T]], base=T - P, channel_multiplier=1,
                   allow_small_or_imprecise_dtypes=True).then_inc(dist_iota, 1)
            pool.wait_ge(dist_signed, 2)
            g.memset(f32(dist_bias[0:CHUNK, T - CHUNK:T]), MASKED).then_inc(dist_ready, 1)

            for n, b in enumerate(Q_BLOCKS):
                pool.wait_ge(p3_copied, 1 + b + 1 + 1)
                g.tensor_scalar(proj[:, b, :], proj[:, b, :], BQK ** -0.5, None, ALU.mult).then_inc(q_scaled, 1)

            for q in range(2):
                for k in range(KT):
                    if q == 0:
                        pool.wait_ge(z_ready, 1 + k + 2)
                    else:
                        pool.wait_ge(acc_added, 1 + (len(GROUPS) - 1) * KT + k + 2)
                    if k == 0:
                        if q:
                            pool.wait_ge(var_mm, q)
                        i = g.tensor_copy(sum2[:], z[:, k, :])
                    else:
                        pool.wait_ge(z_added, q * KT + k)
                        i = g.tensor_tensor(sum2[:], sum2[:], z[:, k, :], ALU.add)
                    i.then_inc(z_added, 1)
                for k in range(KT):
                    pool.wait_ge(sq2_ready, q * KT + k + 1)
                    if k == 0:
                        pool.wait_ge(mean_mm, q + 1)
                        i = g.tensor_copy(sum2[:], sq2[:])
                    else:
                        pool.wait_ge(sq2_added, q * KT + k)
                        i = g.tensor_tensor(sum2[:], sum2[:], sq2[:], ALU.add)
                    i.then_inc(sq2_added, 1)

        @block.scalar
        def _(act):
            own = Tally(act, act_own)
            for s_ in (gate_done, p_copied, gp_done, g_act):
                act.sem_inc(s_, 1)
            A = nc.scalar.activation
            act.wait_ge(par_loaded, 16 * 11)
            A(c_col[:], c_col[:], ACT.Silu).then_inc(silu_c, 1)

            def square(n, src):
                if n:
                    act.wait_ge(sq_added, n)
                A(sq[:], src, ACT.Square).then_inc(sq_ready, 1)

            def root(n):
                act.wait_ge(var_ready, n + 1)
                A(rstd[:], rstd[:], ACT.Sqrt).then_inc(rstd_ready, 1)

            for k in range(KT):
                act.wait_ge(xT_ready, k + 1)
                square(k, xT[:, k, :])
            root(0)
            act.wait_ge(par_ready, 1)
            A(lam[:], lam[:], ACT.Exp).then_inc(lam_exp, 1)
            act.sem_inc(hi_ready, 2)
            act.sem_inc(o_copied, 2)

            def hi_first(l):
                for r in range(2):
                    u = l * UL + r
                    act.wait_ge(raw_loaded[r], 16 * (u // 2 + 1))
                    act.wait_ge(unit_done, 1 + u)
                    A(w_hi[r][:], w_raw[r][:], ACT.Copy).then_inc(hi_ready, 1)

            def hi_next(base, j, per, r):
                act.wait_ge(unit_done, 1 + base + per * j + r + 2)
                s_ = (base + r) % 2
                act.wait_ge(raw_loaded[s_], j * (8 * per) + 16 * ((base + r) // 2 + 2))
                A(w_hi[s_][:], w_raw[s_][:], ACT.Copy).then_inc(hi_ready, 1)

            act.wait_ge(small_loaded, 16)
            hi_first(0)
            for l in range(LAYERS):
                base = l * UL
                for k in range(KT):
                    act.wait_ge(t_ready, l * KT + k + 1)
                    A(act_hi[:, k, :], yT[:, k, :], ACT.Identity, bias=mod[:, l, k:k + 1])\
                        .then_inc(s_hi, 1)
                with loop(act, CB) as j:
                    n = 4 * l + j
                    for r in range(P1_ROLES):
                        hi_next(base, j, P1_ROLES, r)
                        if r == 0:
                            act.wait_ge(c_used, 1 + n)
                            A(u_buf[:], bank[0][:], ACT.Copy).then_inc(u_copied, 1)
                        if r == 3:
                            act.wait_ge(y_conv, 1 + n)
                            A(gate_buf[:], bank[3][:], ACT.Silu).then_inc(gate_done, 1)
                        if r == 4:
                            act.wait_ge(mixed, 1 + n)
                            A(wpool_now[:], wpool_sb[:, bass.ds(4 * l + j, 1), :].rearrange("p a d -> p (a d)"),
                              ACT.Copy).then_inc(wpool_ready, 1)
                            act.wait_ge(pooled, 1 + n)
                            A(p_buf[:, PAD:], bank[0][:], ACT.Copy).then_inc(p_copied, 1)
                        if r == 5:
                            act.wait_ge(y_pool, 1 + n)
                            A(gp_buf[:], bank[1][:], ACT.Silu).then_inc(gp_done, 1)
                act.wait_ge(y_pool, 1 + 4 * l + 4)
                act.wait_ge(y_conv, 1 + 4 * l + 4)
                act.wait_ge(unit_done, 1 + base + P1_UNITS + 1)
                for k in range(KT):
                    A(act_hi[:, k, :], yT[:, k, :], ACT.Copy).then_inc(s_hi, 1)
                act.wait_ge(s_lo, (2 * l + 2) * KT)
                with loop(act, KT // 2) as j:
                    for r in range(2):
                        hi_next(base + P1_UNITS, j, 2, r)
                        act.wait_ge(sq_added, (2 * l + 1) * KT + 2 * j + r)
                        A(sq[:], bank[r][:], ACT.Square).then_inc(sq_ready, 1)
                        act.wait_ge(sq_ready, (2 * l + 1) * KT + 2 * j + r + 1)
                        A(yT[:, bass.ds(2 * j + r, 1), :], bank[r][:].rearrange("p (a t) -> p a t", a=1), ACT.Copy)\
                            .then_inc(o_copied, 1)
                root(2 * l + 1)
                if l < LAYERS - 1:
                    for k in range(KT):
                        act.wait_ge(x_new, l * KT + k + 1)
                        square((2 * l + 2) * KT + k, xT[:, k, :])
                    root(2 * l + 2)

            for k in range(KT):
                act.wait_ge(x_new, (LAYERS - 1) * KT + k + 1)
                A(act_hi[:, k, :], xT[:, k, :], ACT.Copy).then_inc(s_hi, 1)
            act.wait_ge(x_kept, 16)
            act.wait_ge(s_lo, SP_X + KT)
            for r in range(2):
                hi_next(U_IDX, 0, 2, r)
                A(proj[:, N_PROJ - 2 + r, :], bank[r][:], ACT.Copy).then_inc(iq_copied, 1)
            act.wait_ge(unit_done, 1 + U_IDX + 2 + 2)
            act.wait_ge(raw_loaded[U_PROJ % 2 ^ 1], 16 * ((U_PROJ + 1) // 2 + 1))
            A(w_hi[(U_PROJ + 1) % 2][:], w_raw[(U_PROJ + 1) % 2][:], ACT.Copy).then_inc(hi_ready, 1)
            for g in range(4):
                A(proj[32 * g:32 * g + 32, N_PROJ - 3, :], bank[2][0:32, :], ACT.Copy).then_inc(ik_copied, 1)
            A(index_tmp, bank[2][0:64, :], ACT.Copy).then_inc(ik_copied, 1)
            act.sem_inc(relu_done, 1)
            m = 0
            for i in range(SEL0, TT):
                for h in range(IH):
                    act.wait_ge(score_mm, m + 1)
                    act.wait_ge(score_added, max(m - 1, 0))
                    if m == 1:
                        act.wait_ge(iwT_done, 1)
                    A(relu_buf[m % 2][:, 0:keys(i)], bank[m % 2][:, 0:keys(i)], ACT.Relu).then_inc(relu_done, 1)
                    m += 1
            act.wait_ge(dist_iota, 1)
            A(buf_a[:], buf_a[:], ACT.Abs).then_inc(dist_signed, 1)
            act.wait_ge(dist_signed, 1)
            A(dist_bias[:], buf_a[:], ACT.Copy, scale=-1.0).then_inc(dist_signed, 1)
            act.sem_inc(p3_copied, 2)
            with loop(act, N_PROJ // 2 - 1) as j:
                for r in range(2):
                    hi_next(U_PROJ, j, 2, r)
                    A(proj[:, bass.ds(2 * j + r, 1), :], bank[r][:].rearrange("p (a t) -> p a t", a=1), ACT.Copy)\
                        .then_inc(p3_copied, 1)
            act.wait_ge(p3_copied, 1 + 4 + 1)
            for b in (2, 3, 0, 1):
                A(proj[:, b, :], proj[:, b, :], ACT.Gelu_apprx_tanh).then_inc(gelu_done, 1)

            def natural(n):
                b = NATURAL[n]
                act.wait_ge(nat_done, n + 1)
                A(v_nat[:, b - 2, :] if b in (2, 3) else proj[:, b, :], bank[2 + n % 2][:], ACT.Copy)\
                    .then_inc(nat_copied, 1)

            for n in range(N_EARLY):
                natural(n)
            for r in range(2):
                act.wait_ge(unit_done, 1 + U_OUT2 - 2 + r + 2)
                A(proj[:, N_PROJ - 2 + r, :], bank[r][:], ACT.Copy).then_inc(p3_copied, 1)
            for n in range(N_EARLY, len(NATURAL)):
                natural(n)
            act.wait_ge(wsT_done, 1)
            A(wsT, bank[2][:, 0:AG * P].rearrange("p (g t) -> p g t", g=AG), ACT.Copy).then_inc(wsT_copied, 1)

            def exps(item, m):
                n = keys(item // ITEMS)
                act.wait_ge(max_ready, 2 * item + m + 1)
                A(prob[2 * (item % 2) + m][:, 0:n], bank[m][:, 0:n], ACT.Exp, bias=neg_max[:, item % 2, m:m + 1],
                  accum_out=den[:, item % 2, m:m + 1]).then_inc(exp_done, 1)

            def turned(item, k):
                g = group(item, k)
                n = keys(item // ITEMS)
                act.wait_ge(pT_done, g + 1)
                if g >= 2:
                    act.wait_ge(pv_done, g - 1)
                A(probT[g % 2][:, 0:n], bank[2][:, 0:n], ACT.Copy).then_inc(pT_copied, 1)

            for m in range(2):
                exps(0, m)
            for k in range(N_ITEMS + 1):
                for m in range(2):
                    if k and m < groups_of(k - 1):
                        turned(k - 1, m)
                    if k + 1 < N_ITEMS:
                        exps(k + 1, m)
                if k and k % ITEMS == 0:
                    i = k // ITEMS - 1
                    act.wait_ge(pv_done, group(k - 1, 1) + 1)
                    for h in range(BH):
                        A(junk[:, h * P:(h + 1) * P], bank[3][:, h * P:(h + 1) * P], ACT.Square,
                          accum_out=o_ss[:, i, h:h + 1]).then_inc(ob_sq, 1)
                    A(o_nat(i), bank[3][:, 0:HALF], ACT.Copy).then_inc(o_taken, 1)
                    A(c_nat, bank[3][:, HALF:HALF + CH * CD], ACT.Copy).then_inc(o_taken, 1)
                if k > ITEMS and k % ITEMS == 1:
                    i = k // ITEMS - 1
                    act.wait_ge(cT_done, i + 1)
                    A(act_hi[:, 6:8, i * P:(i + 1) * P], cT_bank, ACT.Copy).then_inc(c_hi, 1)
                if k == MIX_AT + 4:
                    act.wait_ge(ln_var, 1)
                    A(ln_stat[:, 1], ln_stat[:, 1], ACT.Sqrt).then_inc(ln_rstd, 1)
                if 0 <= k - MIX_AT - 11 < MIX_CHUNKS:
                    b, a = divmod(k - MIX_AT - 11, 2)
                    act.wait_ge(mix_ready, 2 * b + a + 1)
                    A(act_hi[:, b, a * HALF:(a + 1) * HALF], gm_tmp[:, b, a * HALF:(a + 1) * HALF], ACT.Copy)\
                        .then_inc(s_hi, 1)
            act.wait_ge(cT_done, TT)
            A(act_hi[:, 6:8, T - P:T], cT_bank, ACT.Copy).then_inc(c_hi, 1)

            def hi_plain(u):
                act.wait_ge(raw_loaded[u % 2], 16 * (u // 2 + 1))
                act.wait_ge(unit_done, 1 + u)
                A(w_hi[u % 2][:], w_raw[u % 2][:], ACT.Copy).then_inc(hi_ready, 1)

            hi_plain(U_OUT2)
            hi_plain(U_OUT2 + 1)
            act.wait_ge(ob_var, 1)
            A(o_ss[:], o_ss[:], ACT.Sqrt).then_inc(ob_rstd, 1)
            for h in range(BH):
                act.wait_ge(obT_done, h + 1)
                A(act_hi[:, 2 + h, :], bank[h % 2][:], ACT.Identity, scale=sub_gain[:]).then_inc(s_hi, 1)

            with loop(act, KT // 2) as j:
                for r in range(2):
                    hi_next(U_OUT2, j, 2, r)

            def layer_norm_act(q):
                for k in range(KT):
                    act.wait_ge(xc_ready, q * KT + k + 1)
                    if q * KT + k:
                        act.wait_ge(sq2_added, q * KT + k)
                    A(sq2[:], z[:, k, :], ACT.Square).then_inc(sq2_ready, 1)
                act.wait_ge(ln2_var, q + 1)
                A(rstd2[:], rstd2[:], ACT.Sqrt).then_inc(ln2_rstd, 1)

            layer_norm_act(0)
            for k in range(KT):
                act.wait_ge(ln_t, k + 1)
                A(act_hi[:, k, :], z[:, k, :], ACT.Identity, bias=params2[:, KT + k:KT + k + 1]).then_inc(s_hi, 1)

            for g, n in enumerate(GROUPS):
                act.wait_ge(unit_done, 1 + U_GROUP[g] + 1)
                with loop(act, n) as j:
                    f = FG * g + j
                    hi_next(U_GROUP[g], j, 2, 0)
                    act.wait_ge(f_mul, 1 + f)
                    A(silu_buf[:], bank[0][:], ACT.Silu).then_inc(g_act, 1)
                    hi_next(U_GROUP[g], j, 2, 1)
                    act.wait_ge(f_mul, 1 + f + 1)
                    A(f_hi[:, bass.ds(j, 1), :], f_buf[:].rearrange("p (a t) -> p a t", a=1), ACT.Copy)\
                        .then_inc(f_hi_done, 1)
                last = g == len(GROUPS) - 1
                with loop(act, KT // 2 - last) as j:
                    for r in range(2):
                        hi_next(U_GROUP[g] + 2 * n, j, 2, r)
            layer_norm_act(1)
            for k in range(KT):
                act.wait_ge(ln_t, KT + k + 1)
                A(z[:, k, :], z[:, k, :], ACT.Identity, bias=params2[:, 3 * KT + k:3 * KT + k + 1]).then_inc(x_final, 1)
            for t in range(TT):
                act.wait_ge(outT_done, t + 1)
                A(x_res[:, t, :], bank[t % 4][:], ACT.Copy).then_inc(out_copied, 1)

        @block.vector
        def _(dve):
            v = nc.vector
            own = Tally(dve, dve_own)
            for s_ in (c_used, y_conv, pooled, y_pool, f_mul):
                dve.sem_inc(s_, 1)
            dve.wait_ge(par_T, 1)
            own.did(v.tensor_copy(params[:, 0:N_ROWS], bank[0][:, 0:N_ROWS]))
            own.did(v.tensor_copy(params2[:, 0:N_ROWS2], bank[0][:, HALF:HALF + N_ROWS2]))
            dve.wait_ge(lam_loaded, 16 * 4)
            for m in range(2):
                own.did(v.tensor_tensor(lam_rows[:, 2 * m, :], lam_rows[:, 2 * m, :], lam_rows[:, 2 * m + 1, :],
                                        ALU.mult))
                own.did(v.tensor_reduce(lam[:, m:m + 1], lam_rows[:, 2 * m, :], AX.X, ALU.add))
            dve.sem_inc(par_ready, 1)
            for k in range(KT):
                dve.wait_ge(xT_done, k + 1)
                v.tensor_copy(xT[:, k, :], bank[1 + k % 2][:]).then_inc(xT_ready, 1)
            dve.wait_ge(silu_c, 1)
            dve.wait_ge(const_ready, 1)
            own.did(v.reciprocal(win_fix[:], win_fix[:]))
            n = 0
            for l in range(LAYERS):
                for third in range(3):
                    s = l * 3 + third
                    acc = ada_sum[s % 2]
                    if s >= 2:
                        dve.wait_ge(ada_col, s - 1)
                    for t in range(KT):
                        dve.wait_ge(ada_loaded[n % 4], 16 * (n // 4 + 1))
                        piece = ada_piece[n % 4]
                        if t == 0:
                            i = v.tensor_scalar(acc[:], piece, c_col[:, t:t + 1], None, ALU.mult)
                        else:
                            i = v.scalar_tensor_tensor(acc[:], piece, c_col[:, t:t + 1], acc[:], ALU.mult, ALU.add)
                        i.then_inc(ada_used, 1)
                        n += 1
                        dve.wait_ge(ada_used, n)
                    dve.sem_inc(ada_acc, 1)
            dve.wait_ge(ada_col, 3 * LAYERS)
            own.did(v.tensor_tensor(mod[:].rearrange("p l n -> p (l n)"), bank[3][:, 0:LAYERS * 3 * KT],
                                    params[:, ROW_B_ADA:ROW_G_PRE], ALU.add))
            for l in range(LAYERS):
                own.did(v.scalar_tensor_tensor(pre_gain[:, l], mod[:, l, KT:2 * KT], 1.0,
                                               params[:, ROW_G_PRE + l * KT:ROW_G_PRE + (l + 1) * KT],
                                               ALU.add, ALU.mult))
                own.did(v.tensor_tensor(post_gain[:, l], mod[:, l, 2 * KT:3 * KT],
                                        params[:, ROW_G_POST + l * KT:ROW_G_POST + (l + 1) * KT], ALU.mult))

            def variance(n):
                dve.wait_ge(stat_done, n + 1)
                own.did(v.tensor_scalar(rstd[:], bank[2][:], 1.0 / D, RMS_EPS, ALU.mult, ALU.add))
                v.reciprocal(rstd[:], rstd[:]).then_inc(var_ready, 1)
                dve.wait_ge(rstd_ready, n + 1)

            def lo_first(l):
                for r in range(2):
                    u = l * UL + r
                    dve.wait_ge(hi_ready, 1 + u + 2)
                    v.tensor_tensor(w_lo[r][:], w_raw[r][:], f32(w_hi[r][:]), ALU.subtract).then_inc(lo_ready, 1)

            def lo_next(base, j, per, r):
                dve.wait_ge(hi_ready, 1 + base + per * j + r + 4)
                s_ = (base + r) % 2
                v.tensor_tensor(w_lo[s_][:], w_raw[s_][:], f32(w_hi[s_][:]), ALU.subtract)\
                    .then_inc(lo_ready, 1)

            variance(0)
            dve.sem_inc(lo_ready, 2)
            lo_first(0)
            for l in range(LAYERS):
                base = l * UL
                for k in range(KT):
                    v.scalar_tensor_tensor(yT[:, k, :], xT[:, k, :], pre_gain[:, l, k:k + 1], rstd[:],
                                           ALU.mult, ALU.mult).then_inc(t_ready, 1)
                for k in range(KT):
                    dve.wait_ge(s_hi, 2 * l * KT + k + 1)
                    v.scalar_tensor_tensor(act_lo[:, k, :], yT[:, k, :], mod[:, l, k:k + 1], f32(act_hi[:, k, :]),
                                           ALU.add, ALU.subtract).then_inc(s_lo, 1)
                dve.wait_ge(s_lo, (2 * l + 1) * KT)
                with loop(dve, CB, own, 8) as j:
                    n = 4 * l + j

                    def col(row):
                        return params[:, bass.ds(row + j, 1)]

                    lo_next(base, j, P1_ROLES, 0)
                    lo_next(base, j, P1_ROLES, 1)
                    dve.wait_ge(u_copied, n + 1)
                    v.tensor_tensor(cu[:, TAPS - 1:], bank[1][:], u_buf[:], ALU.mult).then_inc(c_used, 1)
                    dve.wait_ge(c_used, 1 + n + 1)
                    tap = ROW_CONV + l * TAPS * CB
                    own.did(v.tensor_scalar(conv[:], cu[:, 0:T], col(tap), None, ALU.mult))
                    for k in range(1, TAPS):
                        own.did(v.scalar_tensor_tensor(conv[:], cu[:, k:k + T], col(tap + k * CB), conv[:],
                                                       ALU.mult, ALU.add))
                    lo_next(base, j, P1_ROLES, 2)
                    v.tensor_tensor(conv[:], bank[2][:], conv[:], ALU.mult).then_inc(b_used, 1)
                    dve.wait_ge(b_used, n + 1)
                    lo_next(base, j, P1_ROLES, 3)
                    dve.wait_ge(gate_done, 1 + n + 1)
                    v.tensor_tensor(yT[:, bass.ds(j, 1), :].rearrange("p a t -> p (a t)"), conv[:], gate_buf[:],
                                    ALU.mult).then_inc(y_conv, 1)
                    lo_next(base, j, P1_ROLES, 4)
                    dve.wait_ge(p_copied, 1 + n + 1)
                    own.did(v.tensor_tensor(win_a[:, PAD:], p_buf[:, PAD:], p_buf[:, PAD - 1:PAD - 1 + T], ALU.add))
                    src, dst = win_a, win_b
                    for k in range(len(WINDOWS) - 1):
                        s = 2 << k
                        own.did(v.scalar_tensor_tensor(dst[:, PAD:], src[:, PAD - s:PAD - s + T],
                                                       win_on[:, k, bass.ds(j, 1)], src[:, PAD:],
                                                       ALU.mult, ALU.add))
                        src, dst = dst, src
                    own.did(v.tensor_tensor(src[:, PAD:PAD + 16], src[:, PAD:PAD + 16],
                                            win_fix[:, bass.ds(j, 1), :].rearrange("p a t -> p (a t)"), ALU.mult))
                    v.scalar_tensor_tensor(win_a[:, PAD:], src[:, PAD:], win_inv[:, bass.ds(j, 1)], p_buf[:, PAD:],
                                           ALU.mult, ALU.subtract).then_inc(pooled, 1)
                    dve.wait_ge(pooled, 1 + n + 1)
                    lo_next(base, j, P1_ROLES, 5)
                    dve.wait_ge(gp_done, 1 + n + 1)
                    dve.wait_ge(mixed, 1 + n + 1)
                    v.scalar_tensor_tensor(yT[:, bass.ds(CB + j, 1), :].rearrange("p a t -> p (a t)"), bank[2][:],
                                           col(ROW_PSCALE + l * CB), gp_buf[:], ALU.mult, ALU.mult)\
                        .then_inc(y_pool, 1)
                for k in range(KT):
                    dve.wait_ge(s_hi, (2 * l + 1) * KT + k + 1)
                    v.tensor_tensor(act_lo[:, k, :], yT[:, k, :], f32(act_hi[:, k, :]), ALU.subtract)\
                        .then_inc(s_lo, 1)
                with loop(dve, KT // 2) as j:
                    for r in range(2):
                        lo_next(base + P1_UNITS, j, 2, r)
                variance(2 * l + 1)
                dve.wait_ge(o_copied, 1 + KT * (l + 1) + 1)
                for k in range(KT):
                    own.did(v.scalar_tensor_tensor(yT[:, k, :], yT[:, k, :], post_gain[:, l, k:k + 1], rstd[:],
                                                   ALU.mult, ALU.mult))
                    v.tensor_tensor(xT[:, k, :], xT[:, k, :], yT[:, k, :], ALU.add).then_inc(x_new, 1)
                if l < LAYERS - 1:
                    variance(2 * l + 2)

            dve.wait_ge(lam_exp, 1)
            own.did(v.tensor_tensor(lam[:, 0:1], lam[:, 1:2], lam[:, 0:1], ALU.subtract))
            own.did(v.tensor_scalar(lam[:, 0:1], lam[:, 0:1], LAM_INIT, None, ALU.subtract))
            own.did(v.tensor_scalar(sub_gain[:], params2[:, ROW2_SUB:N_ROWS2], 1.0 - LAM_INIT, None, ALU.mult))
            own.did(v.memset(bit_val[:], 1))
            own.did(v.tensor_tensor(bit_val[:, 0:BITS], bit_val[:, 0:BITS], bit_no[:, 0:BITS],
                                    ALU.logical_shift_left))
            for k in range(KT):
                dve.wait_ge(s_hi, SP_X + k + 1)
                v.tensor_tensor(act_lo[:, k, :], xT[:, k, :], f32(act_hi[:, k, :]), ALU.subtract).then_inc(s_lo, 1)
            for r in range(2):
                lo_next(U_IDX, 0, 2, r)
            dve.wait_ge(hi_ready, 1 + U_PROJ + 3)
            q = (U_PROJ + 1) % 2
            v.tensor_tensor(w_lo[q][:], w_raw[q][:], f32(w_hi[q][:]), ALU.subtract).then_inc(lo_ready, 1)
            dve.wait_ge(iwT_done, 1)
            v.tensor_scalar(index_w[:], bank[3][:, 0:TT * 64].rearrange("p (t c) -> p t c", c=64)[:, :, ID:ID + IH],
                            (IH * ID) ** -0.5, None, ALU.mult).then_inc(iw_ready, 1)
            dve.wait_ge(iw_ready, 1)
            m = 0
            for i in range(SEL0, TT):
                sc = score[:, sel_at(i):sel_at(i) + keys(i)]
                for h in range(IH):
                    dve.wait_ge(relu_done, m + 2)
                    r = relu_buf[m % 2][:, 0:keys(i)]
                    if h == 0:
                        x_ = v.tensor_scalar(sc, r, index_w[:, i, h:h + 1], None, ALU.mult)
                    else:
                        x_ = v.scalar_tensor_tensor(sc, r, index_w[:, i, h:h + 1], sc, ALU.mult, ALU.add)
                    x_.then_inc(score_added, 1)
                    m += 1
                    dve.wait_ge(score_added, m)
                own.did(v.memset(score[0:CHUNK, sel_at(i) + keys(i) - CHUNK:sel_at(i) + keys(i)], -3.0e38))

            def tile(i):
                return score[:, sel_at(i):sel_at(i) + keys(i)]

            for q, i in enumerate(range(SEL0, TT)):
                own.did(v.tensor_scalar(buf_b[:, 0:keys(i)], tile(i), 0.0, 0.0, ALU.is_ge, ALU.add,
                                        accum_out=cnt[:, q:q + 1]))
            own.did(v.tensor_scalar(sign[:], cnt[:], float(TOPK), None, ALU.is_ge))
            for q, i in enumerate(range(SEL0, TT)):
                n = keys(i)
                own.did(v.tensor_scalar(need[:, q:q + 1], sign[:, q:q + 1], float(2 * TOPK - 1 - n),
                                        float(n - TOPK + 1), ALU.mult, ALU.add))
            own.did(v.tensor_scalar(sign[:], sign[:], 2.0, -1.0, ALU.mult, ALU.add))
            for q, i in enumerate(range(SEL0, TT)):
                own.did(v.tensor_scalar(tile(i), tile(i), sign[:, q:q + 1], None, ALU.mult))
            own.did(v.memset(thr[:], 0))

            def bit_step(s_):
                own.did(v.tensor_scalar(cand[:], thr[:], bit_val[:, bass.ds(s_, 1)], None, ALU.bitwise_or))
                for q, i in enumerate(range(SEL0, TT)):
                    own.did(v.tensor_scalar(buf_b[:, 0:keys(i)], tile(i), f32(cand[:, q:q + 1]), 0.0,
                                            ALU.is_ge, ALU.add, accum_out=cnt[:, q:q + 1]))
                own.did(v.tensor_tensor(flag[:], cnt[:], need[:], ALU.is_ge))
                own.did(v.scalar_tensor_tensor(thr[:], flag[:], bit_no[:, bass.ds(s_, 1)], thr[:],
                                               ALU.logical_shift_left, ALU.bitwise_or))

            with loop(dve, N_PROJ // 2 - 1, own, 3 * (3 + N_TS)) as j:
                for r in range(2):
                    lo_next(U_PROJ, j, 2, r)
                    for s_ in range(2 - r):
                        bit_step(3 * j + 2 * r + s_)
            bit_step(BITS - 1)
            own.did(v.tensor_tensor(thr_s[:], f32(thr[:]), sign[:], ALU.mult))

            def select(i, step):
                q, n = i - SEL0, keys(i)
                t1, eq = thr_s[:, q:q + 1], buf_b[:, 0:n]
                if step == 0:
                    own.did(v.tensor_scalar(tile(i), tile(i), sign[:, q:q + 1], None, ALU.mult))
                    own.did(v.tensor_scalar(eq, tile(i), t1, 0.0, ALU.is_gt, ALU.add, accum_out=cnt[:, q:q + 1]))
                    own.did(v.tensor_scalar(cnt[:, q:q + 1], cnt[:, q:q + 1], -1.0, float(TOPK), ALU.mult, ALU.add))
                if step == 1:
                    own.did(v.tensor_scalar(eq, tile(i), t1, None, ALU.is_equal))
                    own.did(v.tensor_tensor_scan(eq, eq, eq, 0.0, ALU.bypass, ALU.add))
                if step == 2:
                    own.did(v.tensor_scalar(eq, eq, cnt[:, q:q + 1], None, ALU.is_le))
                    own.did(v.scalar_tensor_tensor(eq, tile(i), t1, eq, ALU.is_equal, ALU.mult))
                if step == 3:
                    own.did(v.scalar_tensor_tensor(eq, tile(i), t1, eq, ALU.is_gt, ALU.add))
                    v.tensor_scalar(sel_bias[:, sel_at(i):sel_at(i) + n], eq, -1.0, -MASKED, ALU.add, ALU.mult)\
                        .then_inc(sel_done, 1)
                    dve.wait_ge(sel_done, q + 1)

            vv = v_nat.rearrange("p b (n c) -> p (b n) c", c=AD)
            G = vv.shape[1]
            tmp = gm_tmp.rearrange("p b (n c) -> p (b n) c", c=AD)
            mean, var = ln_stat[:, 0], ln_stat[:, 1]

            def mixer_step(k):
                if k == 0:
                    dve.wait_ge(nat_copied, len(NATURAL))
                    own.did(v.tensor_reduce(mean, vv, AX.X, ALU.add))
                    own.did(v.tensor_scalar(mean, mean, 1.0 / AD, None, ALU.mult))
                if k == 1:
                    own.did(v.tensor_tensor(vv, vv, mean.unsqueeze(2).broadcast_to([P, G, AD]), ALU.subtract))
                if k == 2:
                    own.did(v.tensor_tensor(tmp, vv, vv, ALU.mult))
                if k == 3:
                    own.did(v.tensor_reduce(var, tmp, AX.X, ALU.add))
                    own.did(v.tensor_scalar(var, var, 1.0 / AD, LN_EPS, ALU.mult, ALU.add))
                    v.reciprocal(var, var).then_inc(ln_var, 1)
                if k == 5:
                    dve.wait_ge(ln_rstd, 1)
                    own.did(v.tensor_tensor(vv, vv, var.unsqueeze(2).broadcast_to([P, G, AD]), ALU.mult))
                if k in (6, 7):
                    b = k - 6
                    dve.wait_ge(gm_loaded, 16 * 7)
                    w = v_nat[:, b, :].rearrange("p (t c) -> p t c", c=P)
                    for row, op in ((ln_g_row, ALU.mult), (ln_b_row, ALU.add)):
                        own.did(v.tensor_tensor(w, w, row[:, b * P:(b + 1) * P].unsqueeze(1).broadcast_to([P, TT, P]),
                                                op))
                if k == 7:
                    dve.wait_ge(wsT_copied, 1)
                    v.memset(wsT[CHUNK:P, :, 0:CHUNK], 0.0).then_inc(v_normed, 1)
                if 0 <= k - 9 < MIX_CHUNKS:
                    c_ = k - 9
                    b, a = divmod(c_, 2)
                    dve.wait_ge(gm_done, c_ + 1)
                    t_ = gm_tmp[:, b, a * HALF:(a + 1) * HALF]
                    own.did(v.tensor_tensor(t_.rearrange("p (t c) -> p t c", c=P),
                                            bank[a][:, HALF:T].rearrange("p (t c) -> p t c", c=P),
                                            bs_tab[:, b, :].unsqueeze(1).broadcast_to([P, HALF // P, P]), ALU.add))
                    v.tensor_tensor(t_, t_, proj[:, b, a * HALF:(a + 1) * HALF], ALU.mult).then_inc(mix_ready, 1)
                if 0 <= k - 12 < MIX_CHUNKS:
                    b, a = divmod(k - 12, 2)
                    dve.wait_ge(s_hi, SP_MIX + k - 12 + 1)
                    v.tensor_tensor(act_lo[:, b, a * HALF:(a + 1) * HALF], gm_tmp[:, b, a * HALF:(a + 1) * HALF],
                                    f32(act_hi[:, b, a * HALF:(a + 1) * HALF]), ALU.subtract).then_inc(s_lo, 1)

            def softmax(item):
                i, it = divmod(item, ITEMS)
                n, par = keys(i), item % 2
                for m in range(2):
                    dve.wait_ge(logits_done, 2 * item + m + 1)
                    v.tensor_reduce(neg_max[:, par, m:m + 1], bank[m][:, 0:n], AX.X, ALU.max, negate=True)\
                        .then_inc(max_ready, 1)
                dve.wait_ge(exp_done, 2 * item + 2)
                p0, p1 = (prob[2 * par + m][:, 0:n] for m in range(2))
                own.did(v.reciprocal(den_r[:], den[:, par]))
                if it < BH:
                    own.did(v.tensor_tensor(den_r[:, 1:2], den_r[:, 1:2], lam[:, 0:1], ALU.mult))
                    own.did(v.tensor_scalar(p1, p1, den_r[:, 1:2], None, ALU.mult))
                    v.scalar_tensor_tensor(p0, p0, den_r[:, 0:1], p1, ALU.mult, ALU.add).then_inc(attn_ready, 1)
                else:
                    for m, p_ in enumerate((p0, p1)):
                        v.tensor_scalar(p_, p_, den_r[:, m:m + 1], None, ALU.mult).then_inc(attn_ready, 1)

            softmax(0)
            for k in range(N_ITEMS + 1):
                if k + 1 < N_ITEMS:
                    softmax(k + 1)
                if k >= MIX_AT:
                    mixer_step(k - MIX_AT)
                i, it = divmod(k, ITEMS)
                if it < 4 and SEL0 <= i + 1 < TT:
                    select(i + 1, it)
                if k > ITEMS and k % ITEMS == 2:
                    i = k // ITEMS - 1
                    dve.wait_ge(c_hi, i + 1)
                    v.tensor_tensor(act_lo[:, 6:8, i * P:(i + 1) * P], cT_bank, f32(act_hi[:, 6:8, i * P:(i + 1) * P]),
                                    ALU.subtract).then_inc(c_lo, 1)
            dve.wait_ge(ob_sq, TT * BH)
            own.did(v.tensor_scalar(o_ss[:], o_ss[:], 1.0 / BV, LN_EPS, ALU.mult, ALU.add))
            v.reciprocal(o_ss[:], o_ss[:]).then_inc(ob_var, 1)
            dve.wait_ge(c_hi, TT)
            v.tensor_tensor(act_lo[:, 6:8, T - P:T], cT_bank, f32(act_hi[:, 6:8, T - P:T]), ALU.subtract)\
                .then_inc(c_lo, 1)
            dve.wait_ge(o_taken, 2 * TT)
            dve.wait_ge(ob_rstd, 1)
            for a in range(2):
                o4 = proj[:, 2 - 2 * a:4 - 2 * a, :].rearrange("p b (n e) -> p (b n) e", e=BV)
                r4 = o_ss[:, 4 * a:4 * a + 4, :].rearrange("p i h -> p (i h)")
                v.tensor_tensor(o4, o4, r4.unsqueeze(2).broadcast_to([P, 16, BV]), ALU.mult).then_inc(ob_normed, 1)

            def lo_plain(u):
                dve.wait_ge(hi_ready, 1 + u + 2)
                v.tensor_tensor(w_lo[u % 2][:], w_raw[u % 2][:], f32(w_hi[u % 2][:]), ALU.subtract)\
                    .then_inc(lo_ready, 1)

            lo_plain(U_OUT2)
            lo_plain(U_OUT2 + 1)
            for h in range(BH):
                dve.wait_ge(s_hi, SP_MIX + MIX_CHUNKS + h + 1)
                v.scalar_tensor_tensor(act_lo[:, 2 + h, :], bank[h % 2][:], sub_gain[:], f32(act_hi[:, 2 + h, :]),
                                       ALU.mult, ALU.subtract).then_inc(s_lo, 1)

            dve.wait_ge(x_back, 16)
            dve.sem_inc(z_ready, 2)
            with loop(dve, KT // 2) as j:
                for r in range(2):
                    lo_next(U_OUT2, j, 2, r)
                    v.scalar_tensor_tensor(z[:, bass.ds(2 * j + r, 1), :].rearrange("p a t -> p (a t)"),
                                           x_res[:, bass.ds(2 * j + r, 1), :].rearrange("p a t -> p (a t)"),
                                           ALPHA, bank[r][:], ALU.mult, ALU.add).then_inc(z_ready, 1)

            def layer_norm_dve(q):
                pair = bank[2 - 2 * q]
                dve.wait_ge(mean_mm, q + 1)
                own.did(v.tensor_scalar(rstd2[:], pair[:], 1.0 / D, None, ALU.mult))
                for k in range(KT):
                    v.tensor_tensor(z[:, k, :], z[:, k, :], rstd2[:], ALU.subtract).then_inc(xc_ready, 1)
                dve.wait_ge(xc_ready, (q + 1) * KT)
                dve.wait_ge(var_mm, q + 1)
                own.did(v.tensor_scalar(rstd2[:], pair[:], 1.0 / D, LN_EPS, ALU.mult, ALU.add))
                v.reciprocal(rstd2[:], rstd2[:]).then_inc(ln2_var, 1)
                dve.wait_ge(ln2_rstd, q + 1)
                for k in range(KT):
                    v.scalar_tensor_tensor(z[:, k, :], z[:, k, :], params2[:, ROW2_LN[q] + k:ROW2_LN[q] + k + 1],
                                           rstd2[:], ALU.mult, ALU.mult).then_inc(ln_t, 1)

            dve.wait_ge(z_ready, 1 + KT + 1)
            layer_norm_dve(0)
            for k in range(KT):
                shift = params2[:, KT + k:KT + k + 1]
                dve.wait_ge(s_hi, SP_X1 + k + 1)
                v.scalar_tensor_tensor(act_lo[:, k, :], z[:, k, :], shift, f32(act_hi[:, k, :]),
                                       ALU.add, ALU.subtract).then_inc(s_lo, 1)
                v.tensor_scalar(z[:, k, :], z[:, k, :], shift, ALPHA, ALU.add, ALU.mult).then_inc(acc_init, 1)
            dve.wait_ge(acc_init, KT)
            dve.sem_inc(acc_added, 2)
            for g, n in enumerate(GROUPS):
                last = g == len(GROUPS) - 1
                dve.wait_ge(unit_done, 1 + U_GROUP[g] + 1)
                with loop(dve, n) as j:
                    f = FG * g + j
                    lo_next(U_GROUP[g], j, 2, 0)
                    lo_next(U_GROUP[g], j, 2, 1)
                    dve.wait_ge(g_act, 1 + f + 1)
                    v.tensor_tensor(f_buf[:], silu_buf[:], bank[1][:], ALU.mult).then_inc(f_mul, 1)
                    dve.wait_ge(f_hi_done, f + 1)
                    v.tensor_tensor(f_lo[:, bass.ds(j, 1), :].rearrange("p a t -> p (a t)"), f_buf[:],
                                    f32(f_hi[:, bass.ds(j, 1), :].rearrange("p a t -> p (a t)")), ALU.subtract)\
                        .then_inc(f_lo_done, 1)
                    dve.wait_ge(f_lo_done, f + 1)

                def accumulate(d, r):
                    zz = z[:, bass.ds(d, 1), :].rearrange("p a t -> p (a t)")
                    v.tensor_tensor(zz, bank[2 + r][:], zz, ALU.add).then_inc(acc_added, 1)

                base = U_GROUP[g] + 2 * n
                if last:
                    with loop(dve, KT // 2 - 1) as j:
                        for r in range(2):
                            lo_next(base, j, 2, r)
                            accumulate(2 * j + r, r)
                    for r in range(2):
                        dve.wait_ge(unit_done, 1 + U_END + r)
                        accumulate(KT - 2 + r, r)
                else:
                    with loop(dve, KT // 2) as j:
                        for r in range(2):
                            lo_next(base, j, 2, r)
                            accumulate(2 * j + r, r)
                dve.wait_ge(acc_added, 1 + (g + 1) * KT + 1)
            layer_norm_dve(1)

        @block.tensor
        def _(pe):
            mm = nc.tensor.matmul
            pe.sem_inc(mixed, 1)
            pe.wait_ge(const_ready, 1)
            pe.wait_ge(par_loaded, 16 * 11)
            nc.tensor.transpose(bank[0][:, 0:N_ROWS], params_raw[0:N_ROWS, :], identity[0:N_ROWS, 0:N_ROWS])
            nc.tensor.transpose(bank[0][:, HALF:HALF + N_ROWS2], params2_raw[0:N_ROWS2, :],
                                identity[0:N_ROWS2, 0:N_ROWS2]).then_inc(par_T, 1)
            pe.wait_ge(x_loaded, 16)
            for k in range(KT):
                if k >= 2:
                    pe.wait_ge(xT_ready, k - 1)
                for t in range(TT):
                    i = nc.tensor.transpose(bank[1 + k % 2][:, t * P:(t + 1) * P], yT[:, t, k * P:(k + 1) * P],
                                            identity[:])
                i.then_inc(xT_done, 1)

            def statistic(n, count):
                pe.wait_ge(sq_added, count)
                for h in range(2):
                    i = mm(bank[2][:, h * HALF:(h + 1) * HALF], ones[:], sq_sum[:, h * HALF:(h + 1) * HALF],
                           start=True, stop=True)
                i.then_inc(stat_done, 1)

            pe.wait_ge(xT_ready, KT)
            statistic(0, KT)
            for s in range(3 * LAYERS):
                pe.wait_ge(ada_acc, s + 1)
                acc = ada_sum[s % 2]
                for k in range(KT):
                    i = mm(bank[3][:, s * KT + k:s * KT + k + 1], acc[:, k * P:(k + 1) * P], ones[:, 0:1],
                           start=True, stop=True)
                i.then_inc(ada_col, 1)
            pe.sem_inc(unit_done, 2)

            def product(u, slot, pair, split=None, kt=KT, hi=act_hi, lo=act_lo, sems=(s_hi, s_lo)):
                pe.wait_ge(hi_ready, 1 + u + 2)
                pe.wait_ge(lo_ready, 1 + u + 2)
                for k in range(kt):
                    if split is not None:
                        pe.wait_ge(sems[0], split + k + 1)
                        pe.wait_ge(sems[1], split + k + 1)
                    for w, a in ((w_hi, hi), (w_hi, lo), (w_lo, hi)):
                        for h in range(2):
                            i = mm(bank[pair][:, h * HALF:(h + 1) * HALF], w[slot][:, k, :],
                                   a[:, k, h * HALF:(h + 1) * HALF],
                                   start=(k == 0 and w is w_hi and a is hi), stop=(k == kt - 1 and w is w_lo))
                i.then_inc(unit_done, 1)

            for l in range(LAYERS):
                base = l * UL
                pe.wait_ge(var_ready, 2 * l + 1)
                with loop(pe, CB) as j:
                    n = 4 * l + j
                    u = base + P1_ROLES * j
                    pe.wait_ge(p_copied, 1 + n)
                    product(u, 0, 0, split=2 * l * KT)
                    pe.wait_ge(gp_done, 1 + n)
                    product(u + 1, 1, 1)
                    pe.wait_ge(y_pool, 1 + n)
                    product(u + 2, 0, 2)
                    pe.wait_ge(gate_done, 1 + n)
                    product(u + 3, 1, 3)
                    pe.wait_ge(u_copied, n + 1)
                    product(u + 4, 0, 0)
                    pe.wait_ge(c_used, 1 + n + 1)
                    product(u + 5, 1, 1)
                    pe.wait_ge(pooled, 1 + n + 1)
                    pe.wait_ge(wpool_ready, n + 1)
                    for h in range(2):
                        i = mm(bank[2][:, h * HALF:(h + 1) * HALF], wpool_now[:],
                               win_a[:, PAD + h * HALF:PAD + (h + 1) * HALF], start=True, stop=True)
                    i.then_inc(mixed, 1)
                pe.wait_ge(gp_done, 1 + 4 * l + 4)
                with loop(pe, KT // 2) as j:
                    for r in range(2):
                        pe.wait_ge(o_copied, 1 + KT * l + 2 * j + r)
                        product(base + P1_UNITS + 2 * j + r, r, r, split=(2 * l + 1) * KT if r == 0 else None)
                pe.wait_ge(y_pool, 1 + 4 * l + 4)
                statistic(2 * l + 1, (2 * l + 2) * KT)
                if l < LAYERS - 1:
                    statistic(2 * l + 2, (2 * l + 3) * KT)

            tr = nc.tensor.transpose
            pe.wait_ge(o_copied, 1 + KT * LAYERS + 1)
            pe.wait_ge(var_ready, 2 * LAYERS)
            product(U_IDX, 0, 0, split=SP_X)
            product(U_IDX + 1, 1, 1)
            product(U_IDX + 2, 0, 2)
            pe.wait_ge(ik_copied, 5)
            for t in range(TT):
                i_ = tr(bank[3][:, t * 64:(t + 1) * 64], index_tmp[:, t * P:(t + 1) * P], identity[0:64, 0:64])
            i_.then_inc(iwT_done, 1)
            pe.wait_ge(iq_copied, 2)
            m = 0
            for i in range(SEL0, TT):
                for h in range(IH):
                    pe.wait_ge(relu_done, m)
                    at = slice(32 * (h % 4), 32 * (h % 4) + 32)
                    for a, w in pieces(keys(i)):
                        i_ = mm(bank[m % 2][:, a:a + w], proj[at, N_PROJ - 2 + h // 4, i * P:(i + 1) * P],
                                proj[at, N_PROJ - 3, a:a + w], start=True, stop=True)
                    i_.then_inc(score_mm, 1)
                    m += 1
            pe.wait_ge(relu_done, m + 1)
            def natural(n):
                b = NATURAL[n]
                if n >= 2:
                    pe.wait_ge(nat_copied, n - 1)
                for t in range(TT):
                    i_ = tr(bank[2 + n % 2][:, t * P:(t + 1) * P], proj[:, b, t * P:(t + 1) * P], identity[:])
                i_.then_inc(nat_done, 1)

            with loop(pe, N_PROJ // 2 - 1) as j:
                for r in range(2):
                    pe.wait_ge(p3_copied, 1 + 2 * j + r)
                    product(U_PROJ + 2 * j + r, (U_PROJ + r) % 2, r)
            pe.wait_ge(p3_copied, 1 + N_PROJ - 2 + 1)
            for n in range(N_EARLY):
                natural(n)
            for r in range(2):
                product(U_OUT2 - 2 + r, (U_OUT2 + r) % 2, r)
            pe.wait_ge(p3_copied, 1 + N_PROJ + 1)
            pe.wait_ge(gelu_done, 2)
            for n in range(N_EARLY, len(NATURAL)):
                natural(n)
            pe.wait_ge(dist_ready, 1)
            pe.wait_ge(q_scaled, len(Q_BLOCKS))

            def logits(item, m):
                i, it = divmod(item, ITEMS)
                if item:
                    pe.wait_ge(exp_done, 2 * item + m - 1)
                at = slice(64 * m, 64 * m + 64)
                if it < BH:
                    q, k, slope = PB_BQ + it, PB_BK + it, it
                else:
                    q, k, slope = PB_CQ + it - BH, PB_CK + it - BH, 2 * (it - BH) + m
                    if i >= SEL0:
                        pe.wait_ge(sel_done, i - SEL0 + 1)
                for a, w in pieces(keys(i)):
                    o = bank[m][:, a:a + w]
                    mm(o, slope_id[:, slope, :], dist_bias[:, (TT - 1 - i) * P + a:(TT - 1 - i) * P + a + w],
                       start=True, stop=False)
                    if it >= BH and i >= SEL0:
                        mm(o, one_id[:], sel_bias[:, sel_at(i) + a:sel_at(i) + a + w], start=False, stop=False)
                    i_ = mm(o, proj[at, q, i * P:(i + 1) * P], proj[at, k, a:a + w], start=False, stop=True)
                i_.then_inc(logits_done, 1)

            def turn(item, k):
                g, i = group(item, k), item // ITEMS
                pe.wait_ge(attn_ready, g + 1)
                if g:
                    pe.wait_ge(pT_copied, g)
                for t in range(i + 1):
                    i_ = tr(bank[2][:, t * P:(t + 1) * P], prob[2 * (item % 2) + k][:, t * P:(t + 1) * P],
                            identity[:])
                i_.then_inc(pT_done, 1)

            def values(item, k):
                g = group(item, k)
                i, it = divmod(item, ITEMS)
                pe.wait_ge(pT_copied, g + 1)
                if i:
                    pe.wait_ge(o_taken, 2 * i)
                for t in range(i + 1):
                    if it < BH:
                        o, w = bank[3][:, it * P:(it + 1) * P], proj[:, PB_BV + it, t * P:(t + 1) * P]
                    else:
                        c_ = (2 * (it - BH) + k) * CD
                        o = bank[3][:, HALF + c_:HALF + c_ + CD]
                        w = proj[:, PB_CV + it - BH, t * P + k * CD:t * P + (k + 1) * CD]
                    i_ = mm(o, probT[g % 2][:, t * P:(t + 1) * P], w, start=(t == 0), stop=(t == i))
                i_.then_inc(pv_done, 1)

            for m in range(2):
                logits(0, m)
            pe.wait_ge(gm_loaded, 16 * 7)
            pe.wait_ge(nat_copied, len(NATURAL))
            for g in range(AG):
                i_ = tr(bank[2][:, g * P:(g + 1) * P], ws_raw[:, g, :], identity[:])
            i_.then_inc(wsT_done, 1)
            pe.wait_ge(wsT_copied, 1)
            for k in range(N_ITEMS + 1):
                for m in range(2):
                    if k and m < groups_of(k - 1):
                        turn(k - 1, m)
                    if k + 1 < N_ITEMS:
                        logits(k + 1, m)
                    if k and m < groups_of(k - 1):
                        values(k - 1, m)
                if k > ITEMS and k % ITEMS == 1 or k == N_ITEMS:
                    i = TT - 1 if k == N_ITEMS else k // ITEMS - 1
                    pe.wait_ge(o_taken, 2 * i + 2)
                    if i:
                        pe.wait_ge(c_lo, i)
                    for b in range(2):
                        i_ = tr(cT_bank[:, b, :], c_nat[:, b * P:(b + 1) * P], identity[:])
                    i_.then_inc(cT_done, 1)
                if 0 <= k - MIX_AT - 8 < MIX_CHUNKS:
                    c_ = k - MIX_AT - 8
                    b, a = divmod(c_, 2)
                    pe.wait_ge(v_normed, 1)
                    if c_ >= 2:
                        pe.wait_ge(mix_ready, c_ - 1)
                    for gg in range(2):
                        for t in range(HALF // P):
                            tt = a * (HALF // P) + t
                            i_ = mm(bank[a][AD * gg:AD * (gg + 1), HALF + t * P:HALF + (t + 1) * P],
                                    v_nat[:, b, tt * P + AD * gg:tt * P + AD * (gg + 1)], wsT[:, 2 * b + gg, :],
                                    start=True, stop=True)
                    i_.then_inc(gm_done, 1)

            pe.wait_ge(ob_normed, 2)
            for h in range(BH):
                if h >= 2:
                    pe.wait_ge(s_lo, SP_MIX + MIX_CHUNKS + h - 1)
                for i in range(TT):
                    i_ = tr(bank[h % 2][:, i * P:(i + 1) * P], o_nat(i)[:, h * P:(h + 1) * P], identity[:])
                i_.then_inc(obT_done, 1)
            pe.wait_ge(c_lo, TT)
            pe.wait_ge(s_hi, SP_MIX + MIX_CHUNKS + BH)
            pe.wait_ge(s_lo, SP_MIX + MIX_CHUNKS + BH)
            with loop(pe, KT // 2) as j:
                for r in range(2):
                    pe.wait_ge(z_ready, 1 + 2 * j + r)
                    product(U_OUT2 + 2 * j + r, (U_OUT2 + r) % 2, r)

            def layer_norm_pe(q):
                for ready, count, done in ((z_added, (q + 1) * KT, mean_mm), (sq2_added, (q + 1) * KT, var_mm)):
                    pe.wait_ge(ready, count)
                    if done is var_mm:
                        pe.wait_ge(xc_ready, q * KT + 1)
                    for a in range(2):
                        i_ = mm(bank[2 - 2 * q][:, a * HALF:(a + 1) * HALF], ones[:], sum2[:, a * HALF:(a + 1) * HALF],
                                start=True, stop=True)
                    i_.then_inc(done, 1)

            layer_norm_pe(0)
            pe.wait_ge(ln_t, 1)
            for g, n in enumerate(GROUPS):
                with loop(pe, n) as j:
                    f = FG * g + j
                    for r, pair_used in ((0, g_act), (1, f_mul)):
                        pe.wait_ge(pair_used, 1 + f)
                        product(U_GROUP[g] + 2 * j + r, (U_GROUP[g] + r) % 2, r,
                                split=SP_X1 if g == 0 and r == 0 else None)
                with loop(pe, KT // 2) as j:
                    for r in range(2):
                        pe.wait_ge(acc_added, 1 + g * KT + 2 * j + r)
                        product(U_GROUP[g] + 2 * n + 2 * j + r, (U_GROUP[g] + r) % 2, 2 + r,
                                split=FG * g if r == 0 else None, kt=n, hi=f_hi, lo=f_lo,
                                sems=(f_hi_done, f_lo_done))
            layer_norm_pe(1)
            pe.wait_ge(x_final, KT)
            for t in range(TT):
                if t >= 4:
                    pe.wait_ge(out_copied, t - 3)
                for k in range(KT):
                    i_ = tr(bank[t % 4][:, k * P:(k + 1) * P], z[:, k, t * P:(t + 1) * P], identity[:])
                i_.then_inc(outT_done, 1)



_INS = ['x', 'c', 'w_ada', 'b_ada', 'g_pre', 'w_in', 'w_conv', 'w_pool', 'pool_scale', 'w_out', 'g_post', 'w_in_2',
        'gmlp_w_s_2', 'gmlp_b_s_2', 'gmlp_ln_g_2', 'gmlp_ln_b_2', 'lam_q1_2', 'lam_k1_2', 'lam_q2_2', 'lam_k2_2',
        'diff_subln_g_2', 'w_out_2', 'ln1_g_2', 'ln1_b_2', 'w_gu_2', 'w_down_2', 'ln2_g_2', 'ln2_b_2']


def kernel(**inputs):
    import numpy as np
    import concourse.bacc as bacc
    from concourse.bass_utils import run_bass_kernel_spmd

    nc = bacc.Bacc("TRN2", target_bir_lowering=False, num_devices=1)
    arrays, args = {}, []
    for name in _INS:
        a = np.ascontiguousarray(inputs[name])
        arrays[name] = a
        args.append(nc.dram_tensor(name, a.shape, mybir.dt.from_np(a.dtype), kind="ExternalInput").ap())
    out = nc.dram_tensor("out", (1, T, D), FP32, kind="ExternalOutput").ap()
    build(nc, *args, out)
    return run_bass_kernel_spmd(nc, [arrays], core_ids=[0]).results[0]["out"]
```

```python
import math
from contextlib import ExitStack, contextmanager

import concourse.bass as bass
from concourse import mybir

FP32 = mybir.dt.float32
FP32R = mybir.dt.float32r
INT32 = mybir.dt.int32
ALU = mybir.AluOpType
ACT = mybir.ActivationFunctionType
AX = mybir.AxisListType

P = 128
D = 1024
T = 1024
KT = D // P
TT = T // P
HALF = 512

LAYERS = 2
CW = D // 2
CB = CW // P
TAPS = 3
WINDOWS = (2, 4, 8, 16)
PAD = 8
RMS_EPS = 1e-6
P1_ROLES = 6
P1_UNITS = P1_ROLES * CB

AG, AD = 4, 64
A_W = AG * AD
BH, BQK, BV = 4, 64, 128
CH, CD = 4, 64
IH, ID = 8, 32
TOPK = 256
CHUNK = 64
OFF_B_Q = 2 * A_W
OFF_B_K = OFF_B_Q + BH * 2 * BQK
OFF_B_V = OFF_B_K + BH * 2 * BQK
OFF_C_Q = OFF_B_V + BH * BV
OFF_C_K = OFF_C_Q + CH * CD
OFF_C_V = OFF_C_K + CH * CD
OFF_I_Q = OFF_C_V + CH * CD
OFF_I_K = OFF_I_Q + IH * ID
IN_W = OFF_I_K + ID + IH
FFN = -(-8 * D // (3 * 256)) * 256
FB = FFN // P
ALPHA = 2 ** 0.25
LN_EPS = 1e-5
LAM_INIT = 0.8 - 0.6 * math.exp(-0.3 * 0)
MASKED = -(2.0 ** 100)

FG = 6
GROUPS = [min(FG, FB - g) for g in range(0, FB, FG)]
SEL0 = TOPK // P
N_TS = TT - SEL0
N_SEL = sum(i + 1 for i in range(SEL0, TT))
BITS = 31


def sel_at(i):
    return P * sum(j + 1 for j in range(SEL0, i))


N_PROJ = OFF_I_Q // P
PB_U, PB_V, PB_BQ, PB_BK, PB_BV = 0, A_W // P, OFF_B_Q // P, OFF_B_K // P, OFF_B_V // P
NATURAL = (12, 13, 14, 15, 20, 21, 2, 3)
N_EARLY = 4
ITEMS = BH + CH // 2
Q_BLOCKS = (4, 5, 6, 7, 16, 17)
MIX_CHUNKS = 4
PB_CQ, PB_CK, PB_CV = OFF_C_Q // P, OFF_C_K // P, OFF_C_V // P


class Tally:

    def __init__(self, eng, sem, start=0):
        self.eng, self.sem, self.n, self.off = eng, sem, start, 0

    def did(self, instruction):
        instruction.then_inc(self.sem, 1)
        self.n += 1
        self.eng.wait_ge(self.sem, self.n + self.off)

    def did_behind(self, instruction):
        instruction.then_inc(self.sem, 1)
        self.n += 1
        self.eng.wait_ge(self.sem, self.n - 1 + self.off)

    def catch_up(self):
        self.eng.wait_ge(self.sem, self.n + self.off)


@contextmanager
def loop(eng, count, tally=None, per=0):
    start = tally.n if tally else 0
    with eng.Fori(0, count) as i:
        if tally:
            tally.off = i * per
        yield i
    if tally:
        assert tally.n - start == per, (tally.n - start, per)
        tally.n, tally.off = start + per * count, 0


def build(nc, x, c, w_ada, b_ada, g_pre, w_in, w_conv, w_pool, pool_scale, w_out, g_post,
          w_in_2, gmlp_w_s, gmlp_b_s, gmlp_ln_g, gmlp_ln_b, lam_q1, lam_k1, lam_q2, lam_k2,
          diff_subln_g, w_out_2, ln1_g, ln1_b, w_gu, w_down, ln2_g, ln2_b, out):
    w_in_v = w_in.rearrange("l (k p) n -> l p k n", p=P)
    w_out_v = w_out.rearrange("l (k p) n -> l p k n", p=P)
    w_in_2v = w_in_2[0].rearrange("(k p) n -> p k n", p=P)
    w_out_2v = w_out_2[0].rearrange("(k p) n -> p k n", p=P)
    w_gu_v = w_gu[0].rearrange("(k p) n -> p k n", p=P)
    w_down_v = w_down[0].rearrange("(k p) n -> p k n", p=P)
    x_mid = nc.dram_tensor("x_mid", [P, KT, T], FP32).ap()
    w_ada_v = w_ada.rearrange("l (p t) n -> l p t n", t=KT)

    with ExitStack() as ctx:
        def sb(name, shape, dt=FP32):
            return ctx.enter_context(nc.sbuf_tensor(name, shape, dt))

        def sem(name):
            return ctx.enter_context(nc.semaphore(name))

        with ExitStack() as inner:
            act_hi = inner.enter_context(nc.sbuf_tensor("act_hi", [P, KT, T], FP32R))
            act_lo = inner.enter_context(nc.sbuf_tensor("act_lo", [P, KT, T], FP32R))
        act_region = sb("act_region", [P, 2 * KT, T])
        gm_tmp = act_region[:, 2:4, :]
        junk = act_region[:, 4, :]
        c_nat = act_region[:, 5, 0:CH * CD]
        v_nat = act_region[:, KT + 2:KT + 4, :]
        ws_raw = act_region[:, KT + 4, 0:AG * P].rearrange("p (g s) -> p g s", g=AG)
        wsT = act_region[:, KT + 4, AG * P:2 * AG * P].rearrange("p (g t) -> p g t", g=AG)
        ln_g_row, ln_b_row = act_region[:, KT + 5, 0:A_W], act_region[:, KT + 5, A_W:2 * A_W]
        bs_tab = act_region[:, KT + 5, 512:512 + 2 * P].rearrange("p (b t) -> p b t", b=2)
        ln_stat = act_region[:, KT + 5, 768:832].rearrange("p (a g) -> p a g", a=2)
        identity = sb("identity", [P, P])
        ones = sb("ones", [P, P])
        params = sb("params", [P, P])
        params2 = sb("params2", [P, P])
        wpool_now = sb("wpool_now", [P, P])
        c_col = sb("c_col", [P, KT])
        mod = sb("mod", [P, LAYERS, 3 * KT])
        pre_gain = sb("pre_gain", [P, LAYERS, KT])
        post_gain = sb("post_gain", [P, LAYERS, KT])
        win_on = sb("win_on", [P, len(WINDOWS) - 1, CB])
        win_inv = sb("win_inv", [P, CB])
        win_fix = sb("win_fix", [P, CB, 16])
        iota_t = sb("iota_t", [P, 16])

        @contextmanager
        def over():
            with ExitStack() as inner:
                yield lambda name, shape, dt=FP32: inner.enter_context(nc.sbuf_tensor(name, shape, dt))

        with over() as t:
            w_raw = [t(f"w_raw{s}", [P, KT, P]) for s in range(2)]
            w_hi = [t(f"w_hi{s}", [P, KT, P], FP32R) for s in range(2)]
            w_lo = [t(f"w_lo{s}", [P, KT, P], FP32R) for s in range(2)]
        w_region = sb("w_region", [P, 6, T])

        ARENA = N_PROJ * T + N_SEL * P + 2 * T
        with over() as t:
            xT = t("xT", [P, KT, T])
            yT = t("yT", [P, KT, T])
            u_buf = t("u_buf", [P, T])
            cu = t("cu", [P, TAPS - 1 + T])
            conv = t("conv", [P, T])
            gate_buf = t("gate_buf", [P, T])
            p_buf = t("p_buf", [P, PAD + T])
            win_a = t("win_a", [P, PAD + T])
            win_b = t("win_b", [P, PAD + T])
            gp_buf = t("gp_buf", [P, T])
            sq = t("sq", [P, T])
            sq_sum = t("sq_sum", [P, T])
            sq_odd = t("sq_odd", [P, T])
            wpool_sb = t("wpool_sb", [P, LAYERS * len(WINDOWS), P])
        with over() as t:
            proj = t("proj", [P, N_PROJ, T])
            score = t("score", [P, N_SEL * P])
            buf_a = t("buf_a", [P, T])
            buf_b = t("buf_b", [P, T])
        with over() as t:
            t("under_proj", [P, N_PROJ, T])
            sel_bias = t("sel_bias", [P, N_SEL * P], FP32R)
            dist_bias = t("dist_bias", [P, T], FP32R)
        with over() as t:
            z = t("z", [P, KT, T])
            x_res = t("x_res", [P, KT, T])
        with over() as t:
            t("under_z", [P, KT, T])
            f_hi = t("f_hi", [P, FG, T], FP32R)
            f_lo = t("f_lo", [P, FG, T], FP32R)
            silu_buf = t("silu_buf", [P, T])
            f_buf = t("f_buf", [P, T])
            sq2 = t("sq2", [P, T])
            sum2 = t("sum2", [P, T])
            rstd2_diag = t("rstd2_diag", [P, T])
        arena = sb("arena", [P, ARENA])
        index_tmp = buf_b[0:64, :]
        relu_buf = [buf_a, buf_b]
        prob = [w_region[:, i, :] for i in range(4)]
        probT = [w_region[:, 4 + i, :] for i in range(2)]
        slope_id = sb("slope_id", [P, BH, P], FP32R)
        one_id = sb("one_id", [P, P], FP32R)
        params_raw, params2_raw = w_region[:, 4, 0:P], w_region[:, 4, P:2 * P]
        lam_rows = w_region[:, 5, 0:4 * BQK].rearrange("p (a d) -> p a d", a=4)
        lam = sb("lam", [P, 2])
        sub_gain = sb("sub_gain", [P, 1])
        index_w = sb("index_w", [P, TT, IH])
        bit_no = sb("bit_no", [P, 32], INT32)
        bit_val = sb("bit_val", [P, 32], INT32)
        thr = sb("thr", [P, N_TS], INT32)
        cand = sb("cand", [P, N_TS], INT32)
        flag = sb("flag", [P, N_TS], INT32)
        cnt, need, sign, thr_s = (sb(n, [P, N_TS]) for n in ("cnt", "need", "sign", "thr_s"))
        neg_max = sb("neg_max", [P, 2, 2])
        o_ss = sb("o_ss", [P, TT, BH])
        den = sb("den", [P, 2, 2])
        den_r = sb("den_r", [P, 2])
        rstd_col = sb("rstd_col", [P, TT])
        table = sb("table", [P, 1])
        sqs = [sq, sq_odd]
        sqs2 = [sq2, silu_buf]
        rstd_diag = sq_sum
        late_piece, late_sum = [sq, sq_sum], sq_odd
        ada_sum = [conv, gate_buf]
        ada_piece = [u_buf[:], gp_buf[:], win_a[:, PAD:], win_b[:, PAD:]]
        bank = [ctx.enter_context(nc.psum_tensor(f"pair{i}", [P, T], FP32)) for i in range(4)]

        ada_cols = bank[0][:, 256:256 + 2 * KT]
        raw_loaded = [sem(f"raw_loaded{s}") for s in range(2)]
        hi_ready, lo_ready, unit_done = sem("hi_ready"), sem("lo_ready"), sem("unit_done")
        x_loaded, par_loaded, small_loaded = sem("x_loaded"), sem("par_loaded"), sem("small_loaded")
        ada_loaded = [sem(f"ada_loaded{s}") for s in range(4)]
        ada_used, ada_col = sem("ada_used"), sem("ada_col")
        const_ready = sem("const_ready")
        par_T, par_ready, xT_done, xT_ready = sem("par_T"), sem("par_ready"), sem("xT_done"), sem("xT_ready")
        silu_c = sem("silu_c")
        s_hi, s_lo = sem("s_hi"), sem("s_lo")
        t_ready = sem("t_ready")
        u_copied, c_used, b_used, gate_done, p_copied, gp_done = (
            sem(n) for n in ("u_copied", "c_used", "b_used", "gate_done", "p_copied", "gp_done"))
        y_conv, pooled, mixed, y_pool, wpool_ready = (
            sem(n) for n in ("y_conv", "pooled", "mixed", "y_pool", "wpool_ready"))
        o_copied, sq_ready, sq_added = sem("o_copied"), sem("sq_ready"), sem("sq_added")
        sq_taken, diag_ready, rstd_spread = sem("sq_taken"), sem("diag_ready"), sem("rstd_spread")
        sq2_taken, diag2_ready, rstd2_spread = sem("sq2_taken"), sem("diag2_ready"), sem("rstd2_spread")
        late_loaded = [sem(f"late_loaded{n}") for n in range(2)]
        late_used, late_col, late_taken = sem("late_used"), sem("late_col"), sem("late_taken")
        x_even, x_odd, y_scaled = sem("x_even"), sem("x_odd"), sem("y_scaled")
        stat_done, var_ready, rstd_ready = sem("stat_done"), sem("var_ready"), sem("rstd_ready")
        act_own, dve_own, pool_own = sem("act_own"), sem("dve_own"), sem("pool_own")
        lam_exp, dist_iota, dist_signed = sem("lam_exp"), sem("dist_iota"), sem("dist_signed")
        outT_done, out_copied, out_stored = sem("outT_done"), sem("out_copied"), sem("out_stored")

        ROW_B_ADA = 0
        ROW_G_PRE = ROW_B_ADA + LAYERS * 3 * KT
        ROW_G_POST = ROW_G_PRE + LAYERS * KT
        ROW_CONV = ROW_G_POST + LAYERS * KT
        ROW_PSCALE = ROW_CONV + LAYERS * TAPS * CB
        N_ROWS = ROW_PSCALE + LAYERS * CB

        def rows(ap2d):
            return ap2d.rearrange("l (r p) -> (l r) p", p=P)

        def f32(ap):
            return ap.bitcast(FP32)

        UL = P1_UNITS + KT

        U_IDX = LAYERS * UL
        U_PROJ = U_IDX + 3
        U_OUT2 = U_PROJ + N_PROJ
        U_FFN = U_OUT2 + KT
        U_GROUP = [U_FFN + sum(2 * n + KT for n in GROUPS[:g]) for g in range(len(GROUPS))]
        U_END = U_GROUP[-1] + 2 * GROUPS[-1] + KT

        ROW2_LN = [0, 2 * KT]
        ROW2_SUB = 4 * KT
        N_ROWS2 = ROW2_SUB + 1
        SP_X, SP_MIX = 2 * LAYERS * KT, (2 * LAYERS + 1) * KT
        SP_X1 = SP_MIX + MIX_CHUNKS + BH

        (x_kept, iq_copied, ik_copied, iwT_done, iw_ready, score_mm, relu_done, score_added, p3_copied,
         gm_loaded, gelu_done, nat_done, nat_copied, wsT_done, wsT_copied, v_normed, ln_var, ln_rstd,
         gm_done, mix_ready, dist_ready, logits_done, max_ready, exp_done, attn_ready, pT_done, pT_copied, pv_done,
         o_taken, ob_sq, ob_var, ob_rstd, sel_done) = (sem(n) for n in (
             "x_kept", "iq_copied", "ik_copied", "iwT_done", "iw_ready", "score_mm", "relu_done", "score_added",
             "p3_copied", "gm_loaded", "gelu_done", "nat_done", "nat_copied", "wsT_done", "wsT_copied",
             "v_normed", "ln_var", "ln_rstd", "gm_done", "mix_ready", "dist_ready", "logits_done",
             "max_ready", "exp_done", "attn_ready", "pT_done", "pT_copied", "pv_done", "o_taken", "ob_sq",
             "ob_var", "ob_rstd", "sel_done"))
        (x_back, z_ready, z_added, mean_mm, xc_ready, sq2_ready, sq2_added, var_mm, ln2_var, ln2_rstd, ln_t,
         x_final, acc_init, g_act, f_mul, f_hi_done, f_lo_done, acc_added, lam_loaded) = (sem(n) for n in (
             "x_back", "z_ready", "z_added", "mean_mm", "xc_ready", "sq2_ready", "sq2_added", "var_mm", "ln2_var",
             "ln2_rstd", "ln_t", "x_final", "acc_init", "g_act", "f_mul", "f_hi_done", "f_lo_done", "acc_added",
             "lam_loaded"))

        bits_done = sem("bits_done")
        q_scaled, cT_done, c_hi, c_lo, obT_done, ob_normed = (sem(n) for n in (
            "q_scaled", "cT_done", "c_hi", "c_lo", "obT_done", "ob_normed"))

        N_ITEMS = TT * ITEMS
        MIX_AT = 1
        cT_bank = bank[3][:, HALF + CH * CD:T].rearrange("p (b t) -> p b t", b=2)

        def groups_of(item):
            return 1 if item % ITEMS < BH else 2

        def group(item, k):
            return sum(groups_of(n) for n in range(item)) + k

        def o_nat(i):
            a, b = divmod(i, 4)
            return proj[:, 2 - 2 * a + b // 2, (b % 2) * HALF:(b % 2 + 1) * HALF]

        def keys(i):
            return P * (i + 1)

        def pieces(n):
            return [(a, min(HALF, n - a)) for a in range(0, n, HALF)]

        OUT_PAIR = (1, 2, 3)

        ADA_EARLY = 2
        LATE_ROLE = (0, 0, 1, 1, 2, 2, 3, 3)

        block = ctx.enter_context(nc.Block())

        @block.sync
        def _(sp):
            sp.dma_start(params_raw[ROW_B_ADA:ROW_G_PRE, :], rows(b_ada)).then_inc(par_loaded, 16)
            sp.dma_start(params_raw[ROW_G_PRE:ROW_G_POST, :], rows(g_pre)).then_inc(par_loaded, 16)
            sp.dma_start(params_raw[ROW_G_POST:ROW_CONV, :], rows(g_post)).then_inc(par_loaded, 16)
            sp.dma_start(params_raw[ROW_CONV:ROW_PSCALE, :],
                         w_conv.rearrange("l t (r p) -> (l t r) p", p=P)).then_inc(par_loaded, 16)
            sp.dma_start(params_raw[ROW_PSCALE:N_ROWS, :], rows(pool_scale)).then_inc(par_loaded, 16)
            sp.dma_start(c_col[:], c.rearrange("b (p t) -> (b p) t", t=KT)).then_inc(par_loaded, 16)
            for k in range(2):
                for i, a in enumerate(((ln1_g, ln1_b), (ln2_g, ln2_b))[k]):
                    sp.dma_start(params2_raw[ROW2_LN[k] + i * KT:ROW2_LN[k] + (i + 1) * KT, :], rows(a))\
                      .then_inc(par_loaded, 16)
            sp.dma_start(params2_raw[ROW2_SUB:N_ROWS2, :], diff_subln_g).then_inc(par_loaded, 16)
            for i, a in enumerate((lam_q1, lam_k1, lam_q2, lam_k2)):
                sp.dma_start(lam_rows[:, i, :], a.broadcast_to([P, BQK])).then_inc(lam_loaded, 16)
            sp.dma_start(yT[:], x[0].rearrange("(t p) f -> p t f", p=P)).then_inc(x_loaded, 16)
            for n in range(ADA_EARLY * KT):
                third, t = divmod(n, KT)
                if n >= 4:
                    sp.wait_ge(ada_used, n - 3)
                sp.dma_start(ada_piece[n % 4], w_ada_v[0, :, t, third * D:(third + 1) * D])\
                  .then_inc(ada_loaded[n % 4], 16)
            sp.dma_start(wpool_sb[:], w_pool.rearrange("l g c d -> c (l g) d")).then_inc(small_loaded, 16)

            def load(u, slot, src):
                sp.wait_ge(hi_ready, 1 + u)
                sp.wait_ge(lo_ready, 1 + u)
                sp.dma_start(w_raw[slot][:], src).then_inc(raw_loaded[slot], 16)

            for l in range(LAYERS):
                with loop(sp, CB) as j:
                    for r, start in enumerate((0, 2 * CW, CW, 3 * CW, 4 * CW, 5 * CW)):
                        load(l * UL + P1_ROLES * j + r, r % 2, w_in_v[l, :, :, bass.ds(start + j * P, P)])
                with loop(sp, KT // 2) as j:
                    for r in range(2):
                        load(l * UL + P1_UNITS + 2 * j + r, r, w_out_v[l, :, :, bass.ds((2 * j + r) * P, P)])
            load(U_IDX, 0, w_in_2v[:, :, OFF_I_Q:OFF_I_Q + P])
            load(U_IDX + 1, 1, w_in_2v[:, :, OFF_I_Q + P:OFF_I_K])
            sp.wait_ge(x_even, KT // 2 * LAYERS)
            sp.wait_ge(x_odd, KT // 2 * LAYERS)
            sp.dma_start(x_mid, xT[:]).then_inc(x_kept, 16)
            sp.wait_ge(hi_ready, 1 + U_IDX + 2)
            sp.wait_ge(lo_ready, 1 + U_IDX + 2)
            sp.dma_start(w_raw[0][:, :, 0:IN_W - OFF_I_K], w_in_2v[:, :, OFF_I_K:IN_W])\
              .then_inc(raw_loaded[0], 16)
            with loop(sp, N_PROJ // 2) as j:
                for r in range(2):
                    load(U_PROJ + 2 * j + r, (U_PROJ + r) % 2, w_in_2v[:, :, bass.ds((2 * j + r) * P, P)])
            sp.wait_ge(unit_done, 1 + U_OUT2 + 1)
            sp.dma_start(ws_raw, gmlp_w_s[0].rearrange("g t s -> t g s")).then_inc(gm_loaded, 16)
            sp.dma_start(ln_g_row, gmlp_ln_g.rearrange("l g c -> l (g c)").broadcast_to([P, A_W]))\
              .then_inc(gm_loaded, 16)
            sp.dma_start(ln_b_row, gmlp_ln_b.rearrange("l g c -> l (g c)").broadcast_to([P, A_W]))\
              .then_inc(gm_loaded, 16)
            for g in range(AG):
                sp.dma_start(bs_tab[AD * (g % 2):AD * (g % 2 + 1), g // 2, :],
                             gmlp_b_s[0, g:g + 1, :].broadcast_to([AD, P])).then_inc(gm_loaded, 16)
            sp.wait_ge(pv_done, group(N_ITEMS, 0))
            sp.wait_ge(cT_done, TT)
            for r in range(2):
                u = U_OUT2 + r
                sp.dma_start(w_raw[u % 2][:], w_out_2v[:, :, r * P:(r + 1) * P]).then_inc(raw_loaded[u % 2], 16)
            sp.dma_start(x_res[:], x_mid).then_inc(x_back, 16)
            for r in range(2):
                load(U_OUT2 + 2 + r, (U_OUT2 + r) % 2, w_out_2v[:, :, (2 + r) * P:(3 + r) * P])
            with loop(sp, KT // 2 - 2) as j:
                for r in range(2):
                    load(U_OUT2 + 4 + 2 * j + r, (U_OUT2 + r) % 2, w_out_2v[:, :, bass.ds((2 * j + 4 + r) * P, P)])
            for g, n in enumerate(GROUPS):
                with loop(sp, n) as j:
                    for r in range(2):
                        load(U_GROUP[g] + 2 * j + r, (U_GROUP[g] + r) % 2,
                             w_gu_v[:, :, bass.ds(r * FFN + (g * FG + j) * P, P)])
                with loop(sp, KT // 2) as j:
                    for r in range(2):
                        u, slot = U_GROUP[g] + 2 * n + 2 * j + r, (U_GROUP[g] + r) % 2
                        sp.wait_ge(hi_ready, 1 + u)
                        sp.wait_ge(lo_ready, 1 + u)
                        sp.dma_start(w_raw[slot][:, 0:n, :],
                                     w_down_v[:, g * FG:g * FG + n, bass.ds((2 * j + r) * P, P)])\
                          .then_inc(raw_loaded[slot], 16)
            out_v = out[0].rearrange("(t p) f -> p t f", p=P)
            for t in range(TT):
                sp.wait_ge(out_copied, t + 1)
                sp.dma_start(out_v[:, t, :], x_res[:, t, :]).then_inc(out_stored, 16)
            sp.wait_ge(out_stored, 16 * TT)

        @block.gpsimd
        def _(pool):
            own = Tally(pool, pool_own)
            g = nc.gpsimd
            own.did(g.memset(identity[:], 0.0))
            own.did(g.affine_select(out=identity[:], in_=identity[:], compare_op=ALU.not_equal, fill=1.0,
                                    base=0, pattern=[[-1, P]], channel_multiplier=1))
            own.did(g.memset(ones[:], 1.0))
            own.did(g.memset(cu[:, 0:TAPS - 1], 0.0))
            for b in (p_buf, win_a, win_b):
                own.did(g.memset(b[:, 0:PAD], 0.0))
            for k in range(len(WINDOWS) - 1):
                for i in range(CB):
                    own.did(g.memset(win_on[:, k, i:i + 1], 1.0 if i > k else 0.0))
            for i, w in enumerate(WINDOWS):
                own.did(g.memset(win_inv[:, i:i + 1], 1.0 / w))
            own.did(g.iota(iota_t[:], pattern=[[1, 16]], base=1, channel_multiplier=0,
                           allow_small_or_imprecise_dtypes=True))
            for i, w in enumerate(WINDOWS):
                own.did(g.tensor_scalar(win_fix[:, i, :], iota_t[:], float(w), 1.0 / w, ALU.min, ALU.mult))
            own.did(g.iota(bit_no[:], pattern=[[-1, 32]], base=BITS - 1, channel_multiplier=0))
            own.did(g.tensor_copy(one_id[:], identity[:]))
            for h in range(BH):
                own.did(g.tensor_scalar(slope_id[:, h, :], identity[:], 2.0 ** (-8.0 * (h + 1) / BH),
                                        None, ALU.mult))
            pool.sem_inc(const_ready, 1)

            pool.wait_ge(rstd_spread, 2)
            for n in range(4 * KT):
                s_, t = divmod(n, KT)
                l, third = divmod(ADA_EARLY + s_, 3)
                if n >= 2:
                    pool.wait_ge(late_used, n - 1)
                pool.dma_start(late_piece[n % 2][:], w_ada_v[l, :, t, third * D:(third + 1) * D])\
                    .then_inc(late_loaded[n % 2], 16)
            pool.wait_ge(late_used, 4 * KT)
            pool.sem_inc(sq_added, 2)
            for l in range(LAYERS):
                for k in range(KT - 1):
                    pool.wait_ge(sq_ready, (2 * l + 1) * KT + k + 1)
                    if k == 0:
                        pool.wait_ge(rstd_spread, 2 * (2 * l + 1))
                        i = g.tensor_copy(sq_sum[:], sqs[0][:])
                    else:
                        pool.wait_ge(sq_added, 2 + l * (KT - 1) + k)
                        i = g.tensor_tensor(sq_sum[:], sq_sum[:], sqs[k % 2][:], ALU.add)
                    i.then_inc(sq_added, 1)
                for k in range(1, KT, 2):
                    pool.wait_ge(y_scaled, (l * KT + k + 1) // 2)
                    g.tensor_tensor(xT[:, k, :], xT[:, k, :], yT[:, k, :], ALU.add).then_inc(x_odd, 1)

            pool.wait_ge(score_added, N_TS * IH)
            pool.wait_ge(relu_done, N_TS * IH + 1)
            g.iota(buf_a[:], pattern=[[-1, T]], base=T - P, channel_multiplier=1,
                   allow_small_or_imprecise_dtypes=True).then_inc(dist_iota, 1)
            pool.wait_ge(dist_signed, 2)
            g.memset(f32(dist_bias[0:CHUNK, T - CHUNK:T]), MASKED).then_inc(dist_ready, 1)

            for n, b in enumerate(Q_BLOCKS):
                pool.wait_ge(p3_copied, 1 + b + 1 + 1)
                g.tensor_scalar(proj[:, b, :], proj[:, b, :], BQK ** -0.5, None, ALU.mult).then_inc(q_scaled, 1)

            for q in range(2):
                for k in range(KT - 1):
                    if q == 0:
                        pool.wait_ge(z_ready, 1 + k + 2)
                    else:
                        pool.wait_ge(acc_added, 1 + (len(GROUPS) - 1) * KT + k + 2)
                    if k == 0:
                        if q:
                            pool.wait_ge(var_mm, q)
                        i = g.tensor_copy(sum2[:], z[:, k, :])
                    else:
                        pool.wait_ge(z_added, q * (KT - 1) + k)
                        i = g.tensor_tensor(sum2[:], sum2[:], z[:, k, :], ALU.add)
                    i.then_inc(z_added, 1)
                for k in range(2, KT, 2):
                    pool.wait_ge(sq2_ready, q * KT + k + 1)
                    if k > 2:
                        pool.wait_ge(sq2_added, q * (KT // 2 - 1) + k // 2 - 1)
                    g.tensor_tensor(sum2[:], sum2[:], sq2[:], ALU.add).then_inc(sq2_added, 1)

        @block.scalar
        def _(act):
            own = Tally(act, act_own)
            for s_ in (gate_done, p_copied, gp_done, g_act):
                act.sem_inc(s_, 1)
            A = nc.scalar.activation
            act.wait_ge(par_loaded, 16 * 11)
            A(c_col[:], c_col[:], ACT.Silu).then_inc(silu_c, 1)

            def square(n, k, src):
                if k >= 2:
                    act.wait_ge(sq_taken, n * KT + k - 1)
                A(sqs[k % 2][:], src, ACT.Square).then_inc(sq_ready, 1)

            def x_updated(l, k):
                act.wait_ge(x_odd if k % 2 else x_even, (l * KT + k) // 2 + 1)

            def root(ready, count, done):
                own.did(A(table[:], ones[:, 0:1], ACT.Sqrt))
                act.wait_ge(ready, count)
                A(rstd_col[:], rstd_col[:], ACT.Sqrt).then_inc(done, 1)

            act.sem_inc(hi_ready, 2)
            act.sem_inc(o_copied, 2)
            act.wait_ge(const_ready, 1)
            for k in range(KT):
                act.wait_ge(xT_ready, k + 1)
                square(0, k, xT[:, k, :])
            root(var_ready, 1, rstd_ready)
            act.wait_ge(par_ready, 1)
            A(lam[:], lam[:], ACT.Exp).then_inc(lam_exp, 1)

            def hi_first(l):
                for r in range(2):
                    u = l * UL + r
                    act.wait_ge(raw_loaded[r], 16 * (u // 2 + 1))
                    act.wait_ge(unit_done, 1 + u)
                    A(w_hi[r][:], w_raw[r][:], ACT.Copy).then_inc(hi_ready, 1)

            def hi_next(base, j, per, r):
                act.wait_ge(unit_done, 1 + base + per * j + r + 2)
                s_ = (base + r) % 2
                act.wait_ge(raw_loaded[s_], j * (8 * per) + 16 * ((base + r) // 2 + 2))
                A(w_hi[s_][:], w_raw[s_][:], ACT.Copy).then_inc(hi_ready, 1)

            act.wait_ge(small_loaded, 16)
            hi_first(0)
            for l in range(LAYERS):
                base = l * UL
                for k in range(KT):
                    act.wait_ge(t_ready, l * KT + k + 1)
                    A(act_hi[:, k, :], yT[:, k, :], ACT.Identity, bias=mod[:, l, k:k + 1])\
                        .then_inc(s_hi, 1)
                with loop(act, CB) as j:
                    n = 4 * l + j
                    for r in range(P1_ROLES):
                        hi_next(base, j, P1_ROLES, r)
                        if r == 0:
                            act.wait_ge(c_used, 1 + n)
                            A(u_buf[:], bank[0][:], ACT.Copy).then_inc(u_copied, 1)
                        if r == 3:
                            act.wait_ge(y_conv, 1 + n)
                            A(gate_buf[:], bank[3][:], ACT.Silu).then_inc(gate_done, 1)
                        if r == 4:
                            act.wait_ge(mixed, 1 + n)
                            A(wpool_now[:], wpool_sb[:, bass.ds(4 * l + j, 1), :].rearrange("p a d -> p (a d)"),
                              ACT.Copy).then_inc(wpool_ready, 1)
                            act.wait_ge(pooled, 1 + n)
                            A(p_buf[:, PAD:], bank[0][:], ACT.Copy).then_inc(p_copied, 1)
                        if r == 5:
                            act.wait_ge(y_pool, 1 + n)
                            A(gp_buf[:], bank[1][:], ACT.Silu).then_inc(gp_done, 1)
                act.wait_ge(y_pool, 1 + 4 * l + 4)
                act.wait_ge(y_conv, 1 + 4 * l + 4)
                act.wait_ge(unit_done, 1 + base + P1_UNITS + 1)
                for k in range(KT):
                    A(act_hi[:, k, :], yT[:, k, :], ACT.Copy).then_inc(s_hi, 1)
                act.wait_ge(s_lo, (2 * l + 2) * KT)
                if l == 0:
                    act.wait_ge(late_used, 4 * KT)
                    act.wait_ge(late_col, 1 + CB)
                with loop(act, KT // 2) as j:
                    for r in range(2):
                        hi_next(base + P1_UNITS, j, 2, r)
                        act.wait_ge(sq_added, 1 + l * (KT - 1) + 2 * j + r)
                        A(sqs[r][:], bank[r][:], ACT.Square).then_inc(sq_ready, 1)
                        act.wait_ge(sq_ready, (2 * l + 1) * KT + 2 * j + r + 1)
                        A(yT[:, bass.ds(2 * j + r, 1), :], bank[r][:].rearrange("p (a t) -> p a t", a=1), ACT.Copy)\
                            .then_inc(o_copied, 1)
                root(var_ready, 2 * l + 2, rstd_ready)
                if l < LAYERS - 1:
                    for k in range(KT):
                        x_updated(l, k)
                        square(l + 1, k, xT[:, k, :])
                    root(var_ready, 2 * l + 3, rstd_ready)

            for k in range(KT):
                x_updated(LAYERS - 1, k)
                A(act_hi[:, k, :], xT[:, k, :], ACT.Copy).then_inc(s_hi, 1)
            act.wait_ge(x_kept, 16)
            act.wait_ge(s_lo, SP_X + KT)
            for r in range(2):
                hi_next(U_IDX, 0, 2, r)
                A(proj[:, N_PROJ - 2 + r, :], bank[r][:], ACT.Copy).then_inc(iq_copied, 1)
            act.wait_ge(unit_done, 1 + U_IDX + 2 + 2)
            act.wait_ge(raw_loaded[U_PROJ % 2 ^ 1], 16 * ((U_PROJ + 1) // 2 + 1))
            A(w_hi[(U_PROJ + 1) % 2][:], w_raw[(U_PROJ + 1) % 2][:], ACT.Copy).then_inc(hi_ready, 1)
            A(index_tmp, bank[2][0:64, :], ACT.Copy).then_inc(ik_copied, 1)
            for g in range(4):
                A(proj[32 * g:32 * g + 32, N_PROJ - 3, :], bank[2][0:32, :], ACT.Copy).then_inc(ik_copied, 1)
            act.sem_inc(relu_done, 1)
            m = 0
            for i in range(SEL0, TT):
                for h in range(IH):
                    act.wait_ge(score_mm, m + 1)
                    act.wait_ge(score_added, max(m - 1, 0))
                    if m == 1:
                        act.wait_ge(iwT_done, 1)
                    A(relu_buf[m % 2][:, 0:keys(i)], bank[m % 2][:, 0:keys(i)], ACT.Relu).then_inc(relu_done, 1)
                    m += 1
            act.sem_inc(p3_copied, 2)
            act.wait_ge(dist_iota, 1)
            A(buf_a[:], buf_a[:], ACT.Abs).then_inc(dist_signed, 1)
            act.wait_ge(dist_signed, 1)
            A(dist_bias[:], buf_a[:], ACT.Copy, scale=-1.0).then_inc(dist_signed, 1)
            with loop(act, N_PROJ // 2 - 1) as j:
                for r in range(2):
                    hi_next(U_PROJ, j, 2, r)
                    A(proj[:, bass.ds(2 * j + r, 1), :], bank[r][:].rearrange("p (a t) -> p a t", a=1), ACT.Copy)\
                        .then_inc(p3_copied, 1)
            act.wait_ge(p3_copied, 1 + 4 + 1)
            for b in (2, 3, 0, 1):
                A(proj[:, b, :], proj[:, b, :], ACT.Gelu_apprx_tanh).then_inc(gelu_done, 1)

            def natural(n):
                b = NATURAL[n]
                act.wait_ge(nat_done, n + 1)
                A(v_nat[:, b - 2, :] if b in (2, 3) else proj[:, b, :], bank[2 + n % 2][:], ACT.Copy)\
                    .then_inc(nat_copied, 1)

            for n in range(N_EARLY):
                natural(n)
            for r in range(2):
                act.wait_ge(unit_done, 1 + U_OUT2 - 2 + r + 2)
                if r:
                    act.wait_ge(bits_done, 1)
                A(proj[:, N_PROJ - 2 + r, :], bank[r][:], ACT.Copy).then_inc(p3_copied, 1)
            for n in range(N_EARLY, len(NATURAL)):
                natural(n)
            act.wait_ge(wsT_done, 1)
            A(wsT, bank[2][:, 0:AG * P].rearrange("p (g t) -> p g t", g=AG), ACT.Copy).then_inc(wsT_copied, 1)

            def exps(item, m):
                n = keys(item // ITEMS)
                act.wait_ge(max_ready, 2 * item + m + 1)
                A(prob[2 * (item % 2) + m][:, 0:n], bank[m][:, 0:n], ACT.Exp, bias=neg_max[:, item % 2, m:m + 1],
                  accum_out=den[:, item % 2, m:m + 1]).then_inc(exp_done, 1)

            def turned(item, k):
                g = group(item, k)
                n = keys(item // ITEMS)
                act.wait_ge(pT_done, g + 1)
                if g >= 2:
                    act.wait_ge(pv_done, g - 1)
                A(probT[g % 2][:, 0:n], bank[2][:, 0:n], ACT.Copy).then_inc(pT_copied, 1)

            for m in range(2):
                exps(0, m)
            for k in range(N_ITEMS + 1):
                for m in range(2):
                    if k and m < groups_of(k - 1):
                        turned(k - 1, m)
                    if k + 1 < N_ITEMS:
                        exps(k + 1, m)
                if k and k % ITEMS == 0:
                    i = k // ITEMS - 1
                    act.wait_ge(pv_done, group(k - 1, 1) + 1)
                    for h in range(BH):
                        A(junk[:, h * P:(h + 1) * P], bank[3][:, h * P:(h + 1) * P], ACT.Square,
                          accum_out=o_ss[:, i, h:h + 1]).then_inc(ob_sq, 1)
                    A(o_nat(i), bank[3][:, 0:HALF], ACT.Copy).then_inc(o_taken, 1)
                    A(c_nat, bank[3][:, HALF:HALF + CH * CD], ACT.Copy).then_inc(o_taken, 1)
                if k > ITEMS and k % ITEMS == 1:
                    i = k // ITEMS - 1
                    act.wait_ge(cT_done, i + 1)
                    A(act_hi[:, 6:8, i * P:(i + 1) * P], cT_bank, ACT.Copy).then_inc(c_hi, 1)
                if k == MIX_AT + 4:
                    act.wait_ge(ln_var, 1)
                    A(ln_stat[:, 1], ln_stat[:, 1], ACT.Sqrt).then_inc(ln_rstd, 1)
                if 0 <= k - MIX_AT - 11 < MIX_CHUNKS:
                    b, a = divmod(k - MIX_AT - 11, 2)
                    act.wait_ge(mix_ready, 2 * b + a + 1)
                    A(act_hi[:, b, a * HALF:(a + 1) * HALF], gm_tmp[:, b, a * HALF:(a + 1) * HALF], ACT.Copy)\
                        .then_inc(s_hi, 1)
            act.wait_ge(cT_done, TT)
            A(act_hi[:, 6:8, T - P:T], cT_bank, ACT.Copy).then_inc(c_hi, 1)

            def hi_plain(u):
                act.wait_ge(raw_loaded[u % 2], 16 * (u // 2 + 1))
                act.wait_ge(unit_done, 1 + u)
                A(w_hi[u % 2][:], w_raw[u % 2][:], ACT.Copy).then_inc(hi_ready, 1)

            own.did(A(table[:], ones[:, 0:1], ACT.Sqrt))
            act.wait_ge(ob_var, 1)
            A(o_ss[:], o_ss[:], ACT.Sqrt).then_inc(ob_rstd, 1)
            hi_plain(U_OUT2)
            hi_plain(U_OUT2 + 1)
            for h in range(BH):
                act.wait_ge(obT_done, h + 1)
                A(act_hi[:, 2 + h, :], bank[2 + h % 2][:], ACT.Identity, scale=sub_gain[:]).then_inc(s_hi, 1)

            with loop(act, KT // 2) as j:
                for r in range(2):
                    hi_next(U_OUT2, j, 2, r)

            def layer_norm_act(q):
                for k in range(KT):
                    act.wait_ge(xc_ready, q * KT + k + 1)
                    if k >= 3 and k % 2:
                        act.wait_ge(sq2_taken, q * (KT // 2) + k // 2)
                    if k >= 4 and k % 2 == 0:
                        act.wait_ge(sq2_added, q * (KT // 2 - 1) + k // 2 - 1)
                    A((sqs2[k % 2] if k else sum2)[:], z[:, k, :], ACT.Square).then_inc(sq2_ready, 1)
                root(ln2_var, q + 1, ln2_rstd)

            layer_norm_act(0)
            for k in range(KT):
                act.wait_ge(ln_t, k + 1)
                A(act_hi[:, k, :], z[:, k, :], ACT.Identity, bias=params2[:, KT + k:KT + k + 1]).then_inc(s_hi, 1)

            for g, n in enumerate(GROUPS):
                act.wait_ge(unit_done, 1 + U_GROUP[g] + 1)
                with loop(act, n) as j:
                    f = FG * g + j
                    hi_next(U_GROUP[g], j, 2, 0)
                    act.wait_ge(f_mul, 1 + f)
                    A(silu_buf[:], bank[0][:], ACT.Silu).then_inc(g_act, 1)
                    hi_next(U_GROUP[g], j, 2, 1)
                    act.wait_ge(f_mul, 1 + f + 1)
                    A(f_hi[:, bass.ds(j, 1), :], f_buf[:].rearrange("p (a t) -> p a t", a=1), ACT.Copy)\
                        .then_inc(f_hi_done, 1)
                last = g == len(GROUPS) - 1
                with loop(act, KT // 2 - last) as j:
                    for r in range(2):
                        hi_next(U_GROUP[g] + 2 * n, j, 2, r)
            layer_norm_act(1)

            def shift(a):
                for k in range(KT):
                    act.wait_ge(ln_t, (1 + a) * KT + k + 1)
                    zz = z[:, k, a * HALF:(a + 1) * HALF]
                    A(zz, zz, ACT.Identity, bias=params2[:, 3 * KT + k:3 * KT + k + 1]).then_inc(x_final, 1)

            shift(0)
            for t in range(TT // 2):
                act.wait_ge(outT_done, t + 1)
                A(x_res[:, t, :], bank[OUT_PAIR[t % 3]][:], ACT.Copy).then_inc(out_copied, 1)
            shift(1)

        @block.vector
        def _(dve):
            v = nc.vector
            own = Tally(dve, dve_own)
            for s_ in (c_used, y_conv, pooled, y_pool, f_mul, late_taken):
                dve.sem_inc(s_, 1)
            dve.sem_inc(lo_ready, 2)
            dve.wait_ge(par_T, 1)
            own.did(v.tensor_copy(params[:, 0:N_ROWS], bank[0][:, 0:N_ROWS]))
            own.did(v.tensor_copy(params2[:, 0:N_ROWS2], bank[0][:, HALF:HALF + N_ROWS2]))
            dve.wait_ge(lam_loaded, 16 * 4)
            for m in range(2):
                own.did(v.tensor_tensor(lam_rows[:, 2 * m, :], lam_rows[:, 2 * m, :], lam_rows[:, 2 * m + 1, :],
                                        ALU.mult))
                own.did(v.tensor_reduce(lam[:, m:m + 1], lam_rows[:, 2 * m, :], AX.X, ALU.add))
            dve.sem_inc(par_ready, 1)
            for k in range(KT):
                dve.wait_ge(xT_done, k + 1)
                v.tensor_copy(xT[:, k, :], bank[1 + k % 2][:]).then_inc(xT_ready, 1)
            dve.wait_ge(silu_c, 1)
            dve.wait_ge(const_ready, 1)
            own.did(v.reciprocal(win_fix[:], win_fix[:]))

            def ada_add(acc, piece, t, used):
                if t == 0:
                    i = v.tensor_scalar(acc[:], piece, c_col[:, t:t + 1], None, ALU.mult)
                else:
                    i = v.scalar_tensor_tensor(acc[:], piece, c_col[:, t:t + 1], acc[:], ALU.mult, ALU.add)
                i.then_inc(used, 1)

            def spread(sums, eps, var_done, root_done, diag, diag_done, count):
                blocks = diag[:].rearrange("p (t c) -> p t c", c=P)
                own.did(v.tensor_tensor(blocks, sums[:].rearrange("p (t c) -> p t c", c=P),
                                        identity[:].unsqueeze(1).broadcast_to([P, TT, P]), ALU.mult))
                own.did(v.tensor_reduce(rstd_col[:], blocks, AX.X, ALU.add))
                own.did(v.tensor_scalar(rstd_col[:], rstd_col[:], 1.0 / D, eps, ALU.mult, ALU.add))
                v.reciprocal(rstd_col[:], rstd_col[:]).then_inc(var_done, 1)
                dve.wait_ge(root_done, count)
                for h in range(2):
                    t = slice(h * TT // 2, (h + 1) * TT // 2)
                    v.tensor_tensor(blocks[:, t, :], identity[:].unsqueeze(1).broadcast_to([P, TT // 2, P]),
                                    rstd_col[:, t].unsqueeze(2).broadcast_to([P, TT // 2, P]),
                                    ALU.mult).then_inc(diag_done, 1)

            def variance(n):
                dve.wait_ge(stat_done, n + 1)
                spread(bank[3], RMS_EPS, var_ready, rstd_ready, rstd_diag, diag_ready, n + 1)
                if n:
                    dve.wait_ge(rstd_spread, 2 * n + 2)

            for n in range(ADA_EARLY * KT):
                if n == ADA_EARLY * KT - 4:
                    variance(0)
                dve.wait_ge(ada_loaded[n % 4], 16 * (n // 4 + 1))
                ada_add(ada_sum[n // KT], ada_piece[n % 4], n % KT, ada_used)
                dve.wait_ge(ada_used, n + 1)
            mod_all = mod[:].rearrange("p l n -> p (l n)")
            dve.wait_ge(ada_col, ADA_EARLY)
            own.did(v.tensor_tensor(mod_all[:, 0:ADA_EARLY * KT], ada_cols,
                                    params[:, ROW_B_ADA:ROW_B_ADA + ADA_EARLY * KT], ALU.add))

            def pre(l):
                own.did(v.scalar_tensor_tensor(pre_gain[:, l], mod[:, l, KT:2 * KT], 1.0,
                                               params[:, ROW_G_PRE + l * KT:ROW_G_PRE + (l + 1) * KT],
                                               ALU.add, ALU.mult))

            def post(l):
                own.did(v.tensor_tensor(post_gain[:, l], mod[:, l, 2 * KT:3 * KT],
                                        params[:, ROW_G_POST + l * KT:ROW_G_POST + (l + 1) * KT], ALU.mult))

            pre(0)

            def late_pieces(j, r):
                for t in range(KT):
                    if LATE_ROLE[t] == r:
                        dve.wait_ge(late_loaded[t % 2], j * (8 * KT) + 16 * (t // 2 + 1))
                        ada_add(late_sum, late_piece[t % 2][:], t, late_used)
                        dve.wait_ge(late_used, j * KT + t + 1)

            def lo_first(l):
                for r in range(2):
                    u = l * UL + r
                    dve.wait_ge(hi_ready, 1 + u + 2)
                    v.tensor_tensor(w_lo[r][:], w_raw[r][:], f32(w_hi[r][:]), ALU.subtract).then_inc(lo_ready, 1)

            def lo_next(base, j, per, r):
                dve.wait_ge(hi_ready, 1 + base + per * j + r + 4)
                s_ = (base + r) % 2
                v.tensor_tensor(w_lo[s_][:], w_raw[s_][:], f32(w_hi[s_][:]), ALU.subtract)\
                    .then_inc(lo_ready, 1)

            dve.wait_ge(rstd_spread, 2)
            for l in range(LAYERS):
                base = l * UL
                for k in range(KT):
                    if l == 0 and k == 1:
                        lo_first(0)
                    v.scalar_tensor_tensor(yT[:, k, :], xT[:, k, :], pre_gain[:, l, k:k + 1], bank[2][:],
                                           ALU.mult, ALU.mult).then_inc(t_ready, 1)
                for k in range(KT):
                    dve.wait_ge(s_hi, 2 * l * KT + k + 1)
                    v.scalar_tensor_tensor(act_lo[:, k, :], yT[:, k, :], mod[:, l, k:k + 1], f32(act_hi[:, k, :]),
                                           ALU.add, ALU.subtract).then_inc(s_lo, 1)
                dve.wait_ge(s_lo, (2 * l + 1) * KT)
                with loop(dve, CB, own, 8) as j:
                    n = 4 * l + j

                    def late(j, r):
                        if l == 0:
                            late_pieces(j, r)

                    def col(row):
                        return params[:, bass.ds(row + j, 1)]

                    lo_next(base, j, P1_ROLES, 0)
                    late(j, 0)
                    lo_next(base, j, P1_ROLES, 1)
                    dve.wait_ge(u_copied, n + 1)
                    v.tensor_tensor(cu[:, TAPS - 1:], bank[1][:], u_buf[:], ALU.mult).then_inc(c_used, 1)
                    dve.wait_ge(c_used, 1 + n + 1)
                    tap = ROW_CONV + l * TAPS * CB
                    own.did(v.tensor_scalar(conv[:], cu[:, 0:T], col(tap), None, ALU.mult))
                    for k in range(1, TAPS):
                        own.did(v.scalar_tensor_tensor(conv[:], cu[:, k:k + T], col(tap + k * CB), conv[:],
                                                       ALU.mult, ALU.add))
                    late(j, 1)
                    lo_next(base, j, P1_ROLES, 2)
                    v.tensor_tensor(conv[:], bank[2][:], conv[:], ALU.mult).then_inc(b_used, 1)
                    dve.wait_ge(b_used, n + 1)
                    late(j, 2)
                    lo_next(base, j, P1_ROLES, 3)
                    dve.wait_ge(gate_done, 1 + n + 1)
                    v.tensor_tensor(yT[:, bass.ds(j, 1), :].rearrange("p a t -> p (a t)"), conv[:], gate_buf[:],
                                    ALU.mult).then_inc(y_conv, 1)
                    late(j, 3)
                    lo_next(base, j, P1_ROLES, 4)
                    dve.wait_ge(p_copied, 1 + n + 1)
                    own.did(v.tensor_tensor(win_a[:, PAD:], p_buf[:, PAD:], p_buf[:, PAD - 1:PAD - 1 + T], ALU.add))
                    src, dst = win_a, win_b
                    for k in range(len(WINDOWS) - 1):
                        s = 2 << k
                        own.did(v.scalar_tensor_tensor(dst[:, PAD:], src[:, PAD - s:PAD - s + T],
                                                       win_on[:, k, bass.ds(j, 1)], src[:, PAD:],
                                                       ALU.mult, ALU.add))
                        src, dst = dst, src
                    own.did(v.tensor_tensor(src[:, PAD:PAD + 16], src[:, PAD:PAD + 16],
                                            win_fix[:, bass.ds(j, 1), :].rearrange("p a t -> p (a t)"), ALU.mult))
                    v.scalar_tensor_tensor(win_a[:, PAD:], src[:, PAD:], win_inv[:, bass.ds(j, 1)], p_buf[:, PAD:],
                                           ALU.mult, ALU.subtract).then_inc(pooled, 1)
                    dve.wait_ge(pooled, 1 + n + 1)
                    lo_next(base, j, P1_ROLES, 5)
                    dve.wait_ge(gp_done, 1 + n + 1)
                    dve.wait_ge(mixed, 1 + n + 1)
                    v.scalar_tensor_tensor(yT[:, bass.ds(CB + j, 1), :].rearrange("p a t -> p (a t)"), bank[2][:],
                                           col(ROW_PSCALE + l * CB), gp_buf[:], ALU.mult, ALU.mult)\
                        .then_inc(y_pool, 1)
                    if l == 0:
                        dve.wait_ge(late_col, j + 2)
                        v.tensor_tensor(mod_all[:, bass.ds((ADA_EARLY + j) * KT, KT)], bank[3][:, 0:KT],
                                        params[:, bass.ds(ROW_B_ADA + (ADA_EARLY + j) * KT, KT)], ALU.add)\
                            .then_inc(late_taken, 1)
                if l == 0:
                    dve.wait_ge(late_taken, 1 + CB)
                    post(0)
                    pre(1)
                    post(1)
                for k in range(KT):
                    dve.wait_ge(s_hi, (2 * l + 1) * KT + k + 1)
                    v.tensor_tensor(act_lo[:, k, :], yT[:, k, :], f32(act_hi[:, k, :]), ALU.subtract)\
                        .then_inc(s_lo, 1)
                with loop(dve, KT // 2) as j:
                    for r in range(2):
                        lo_next(base + P1_UNITS, j, 2, r)
                variance(2 * l + 1)
                dve.wait_ge(o_copied, 1 + KT * (l + 1) + 1)
                for k in range(KT):
                    i = v.scalar_tensor_tensor(yT[:, k, :], yT[:, k, :], post_gain[:, l, k:k + 1], bank[2][:],
                                               ALU.mult, ALU.mult)
                    if k % 2:
                        i.then_inc(y_scaled, 1)
                    else:
                        own.did(i)
                        v.tensor_tensor(xT[:, k, :], xT[:, k, :], yT[:, k, :], ALU.add).then_inc(x_even, 1)
                if l < LAYERS - 1:
                    variance(2 * l + 2)

            dve.wait_ge(lam_exp, 1)
            own.did(v.tensor_tensor(lam[:, 0:1], lam[:, 1:2], lam[:, 0:1], ALU.subtract))
            own.did(v.tensor_scalar(lam[:, 0:1], lam[:, 0:1], LAM_INIT, None, ALU.subtract))
            own.did(v.tensor_scalar(sub_gain[:], params2[:, ROW2_SUB:N_ROWS2], 1.0 - LAM_INIT, None, ALU.mult))
            own.did(v.memset(bit_val[:], 1))
            own.did(v.tensor_tensor(bit_val[:, 0:BITS], bit_val[:, 0:BITS], bit_no[:, 0:BITS],
                                    ALU.logical_shift_left))
            for k in range(KT):
                dve.wait_ge(s_hi, SP_X + k + 1)
                v.tensor_tensor(act_lo[:, k, :], xT[:, k, :], f32(act_hi[:, k, :]), ALU.subtract).then_inc(s_lo, 1)
            for r in range(2):
                lo_next(U_IDX, 0, 2, r)
            dve.wait_ge(hi_ready, 1 + U_PROJ + 3)
            q = (U_PROJ + 1) % 2
            v.tensor_tensor(w_lo[q][:], w_raw[q][:], f32(w_hi[q][:]), ALU.subtract).then_inc(lo_ready, 1)
            dve.wait_ge(iwT_done, 1)
            v.tensor_scalar(index_w[:], bank[3][:, 0:TT * 64].rearrange("p (t c) -> p t c", c=64)[:, :, ID:ID + IH],
                            (IH * ID) ** -0.5, None, ALU.mult).then_inc(iw_ready, 1)
            dve.wait_ge(iw_ready, 1)
            m = 0
            for i in range(SEL0, TT):
                sc = score[:, sel_at(i):sel_at(i) + keys(i)]
                for h in range(IH):
                    dve.wait_ge(relu_done, m + 2)
                    r = relu_buf[m % 2][:, 0:keys(i)]
                    if h == 0:
                        x_ = v.tensor_scalar(sc, r, index_w[:, i, h:h + 1], None, ALU.mult)
                    else:
                        x_ = v.scalar_tensor_tensor(sc, r, index_w[:, i, h:h + 1], sc, ALU.mult, ALU.add)
                    x_.then_inc(score_added, 1)
                    m += 1
                    dve.wait_ge(score_added, m)
                own.did(v.memset(score[0:CHUNK, sel_at(i) + keys(i) - CHUNK:sel_at(i) + keys(i)], -3.0e38))

            def tile(i):
                return score[:, sel_at(i):sel_at(i) + keys(i)]

            for q, i in enumerate(range(SEL0, TT)):
                own.did(v.tensor_scalar(buf_b[:, 0:keys(i)], tile(i), 0.0, 0.0, ALU.is_ge, ALU.add,
                                        accum_out=cnt[:, q:q + 1]))
            own.did(v.tensor_scalar(sign[:], cnt[:], float(TOPK), None, ALU.is_ge))
            for q, i in enumerate(range(SEL0, TT)):
                n = keys(i)
                own.did(v.tensor_scalar(need[:, q:q + 1], sign[:, q:q + 1], float(2 * TOPK - 1 - n),
                                        float(n - TOPK + 1), ALU.mult, ALU.add))
            own.did(v.tensor_scalar(sign[:], sign[:], 2.0, -1.0, ALU.mult, ALU.add))
            for q, i in enumerate(range(SEL0, TT)):
                own.did(v.tensor_scalar(tile(i), tile(i), sign[:, q:q + 1], None, ALU.mult))
            own.did(v.memset(thr[:], 0))

            def bit_try(s_):
                own.did(v.tensor_scalar(cand[:], thr[:], bit_val[:, bass.ds(s_, 1)], None, ALU.bitwise_or))

            def bit_count(tiles, spare=(buf_b, proj[:, N_PROJ - 1, :])):
                for n, i in enumerate(tiles):
                    q = i - SEL0
                    own.did_behind(v.tensor_scalar(spare[n % 2][:, 0:keys(i)], tile(i), f32(cand[:, q:q + 1]), 0.0,
                                            ALU.is_ge, ALU.add, accum_out=cnt[:, q:q + 1]))

            def bit_keep(s_):
                own.catch_up()
                own.did(v.tensor_tensor(flag[:], cnt[:], need[:], ALU.is_ge))
                own.did(v.scalar_tensor_tensor(thr[:], flag[:], bit_no[:, bass.ds(s_, 1)], thr[:],
                                               ALU.logical_shift_left, ALU.bitwise_or))

            sel_tiles = range(SEL0, TT)

            def bit_step(s_):
                bit_try(s_)
                bit_count(sel_tiles)
                bit_keep(s_)

            with loop(dve, N_PROJ // 2 - 1, own, 3 * (3 + N_TS)) as j:
                lo_next(U_PROJ, j, 2, 0)
                bit_step(3 * j)
                bit_try(3 * j + 1)
                bit_count(sel_tiles[0::2])
                own.catch_up()
                lo_next(U_PROJ, j, 2, 1)
                bit_count(sel_tiles[1::2])
                bit_keep(3 * j + 1)
                bit_step(3 * j + 2)
            bit_step(BITS - 1)
            dve.sem_inc(bits_done, 1)
            own.did(v.tensor_tensor(thr_s[:], f32(thr[:]), sign[:], ALU.mult))

            def select(i, step):
                q, n = i - SEL0, keys(i)
                t1, eq = thr_s[:, q:q + 1], buf_b[:, 0:n]
                if step == 0:
                    own.did(v.tensor_scalar(tile(i), tile(i), sign[:, q:q + 1], None, ALU.mult))
                    own.did(v.tensor_scalar(eq, tile(i), t1, 0.0, ALU.is_gt, ALU.add, accum_out=cnt[:, q:q + 1]))
                    own.did(v.tensor_scalar(cnt[:, q:q + 1], cnt[:, q:q + 1], -1.0, float(TOPK), ALU.mult, ALU.add))
                if step == 1:
                    own.did(v.tensor_scalar(eq, tile(i), t1, None, ALU.is_equal))
                    own.did(v.tensor_tensor_scan(eq, eq, eq, 0.0, ALU.bypass, ALU.add))
                if step == 2:
                    own.did(v.tensor_scalar(eq, eq, cnt[:, q:q + 1], None, ALU.is_le))
                    own.did(v.scalar_tensor_tensor(eq, tile(i), t1, eq, ALU.is_equal, ALU.mult))
                if step == 3:
                    own.did(v.scalar_tensor_tensor(eq, tile(i), t1, eq, ALU.is_gt, ALU.add))
                    v.tensor_scalar(sel_bias[:, sel_at(i):sel_at(i) + n], eq, -1.0, -MASKED, ALU.add, ALU.mult)\
                        .then_inc(sel_done, 1)
                    dve.wait_ge(sel_done, q + 1)

            vv = v_nat.rearrange("p b (n c) -> p (b n) c", c=AD)
            G = vv.shape[1]
            tmp = gm_tmp.rearrange("p b (n c) -> p (b n) c", c=AD)
            mean, var = ln_stat[:, 0], ln_stat[:, 1]

            def mixer_step(k):
                if k == 0:
                    dve.wait_ge(nat_copied, len(NATURAL))
                    own.did(v.tensor_reduce(mean, vv, AX.X, ALU.add))
                    own.did(v.tensor_scalar(mean, mean, 1.0 / AD, None, ALU.mult))
                if k == 1:
                    own.did(v.tensor_tensor(vv, vv, mean.unsqueeze(2).broadcast_to([P, G, AD]), ALU.subtract))
                if k == 2:
                    own.did(v.tensor_tensor(tmp, vv, vv, ALU.mult))
                if k == 3:
                    own.did(v.tensor_reduce(var, tmp, AX.X, ALU.add))
                    own.did(v.tensor_scalar(var, var, 1.0 / AD, LN_EPS, ALU.mult, ALU.add))
                    v.reciprocal(var, var).then_inc(ln_var, 1)
                if k == 5:
                    dve.wait_ge(ln_rstd, 1)
                    own.did(v.tensor_tensor(vv, vv, var.unsqueeze(2).broadcast_to([P, G, AD]), ALU.mult))
                if k in (6, 7):
                    b = k - 6
                    dve.wait_ge(gm_loaded, 16 * 7)
                    w = v_nat[:, b, :].rearrange("p (t c) -> p t c", c=P)
                    for row, op in ((ln_g_row, ALU.mult), (ln_b_row, ALU.add)):
                        own.did(v.tensor_tensor(w, w, row[:, b * P:(b + 1) * P].unsqueeze(1).broadcast_to([P, TT, P]),
                                                op))
                if k == 7:
                    dve.wait_ge(wsT_copied, 1)
                    v.memset(wsT[CHUNK:P, :, 0:CHUNK], 0.0).then_inc(v_normed, 1)
                if 0 <= k - 9 < MIX_CHUNKS:
                    c_ = k - 9
                    b, a = divmod(c_, 2)
                    dve.wait_ge(gm_done, c_ + 1)
                    t_ = gm_tmp[:, b, a * HALF:(a + 1) * HALF]
                    own.did(v.tensor_tensor(t_.rearrange("p (t c) -> p t c", c=P),
                                            bank[a][:, HALF:T].rearrange("p (t c) -> p t c", c=P),
                                            bs_tab[:, b, :].unsqueeze(1).broadcast_to([P, HALF // P, P]), ALU.add))
                    v.tensor_tensor(t_, t_, proj[:, b, a * HALF:(a + 1) * HALF], ALU.mult).then_inc(mix_ready, 1)
                if 0 <= k - 12 < MIX_CHUNKS:
                    b, a = divmod(k - 12, 2)
                    dve.wait_ge(s_hi, SP_MIX + k - 12 + 1)
                    v.tensor_tensor(act_lo[:, b, a * HALF:(a + 1) * HALF], gm_tmp[:, b, a * HALF:(a + 1) * HALF],
                                    f32(act_hi[:, b, a * HALF:(a + 1) * HALF]), ALU.subtract).then_inc(s_lo, 1)

            def softmax(item, meanwhile=None):
                i, it = divmod(item, ITEMS)
                n, par = keys(i), item % 2
                for m in range(2):
                    dve.wait_ge(logits_done, 2 * item + m + 1)
                    v.tensor_reduce(neg_max[:, par, m:m + 1], bank[m][:, 0:n], AX.X, ALU.max, negate=True)\
                        .then_inc(max_ready, 1)
                if meanwhile is not None:
                    beside(meanwhile)
                dve.wait_ge(exp_done, 2 * item + 2)
                p0, p1 = (prob[2 * par + m][:, 0:n] for m in range(2))
                own.did(v.reciprocal(den_r[:], den[:, par]))
                if it < BH:
                    own.did(v.tensor_tensor(den_r[:, 1:2], den_r[:, 1:2], lam[:, 0:1], ALU.mult))
                    own.did(v.tensor_scalar(p1, p1, den_r[:, 1:2], None, ALU.mult))
                    v.scalar_tensor_tensor(p0, p0, den_r[:, 0:1], p1, ALU.mult, ALU.add).then_inc(attn_ready, 1)
                else:
                    for m, p_ in enumerate((p0, p1)):
                        v.tensor_scalar(p_, p_, den_r[:, m:m + 1], None, ALU.mult).then_inc(attn_ready, 1)

            def beside(k):
                if k >= MIX_AT:
                    mixer_step(k - MIX_AT)
                i, it = divmod(k, ITEMS)
                if it < 4 and SEL0 <= i + 1 < TT:
                    select(i + 1, it)
                if k > ITEMS and k % ITEMS == 2:
                    i = k // ITEMS - 1
                    dve.wait_ge(c_hi, i + 1)
                    v.tensor_tensor(act_lo[:, 6:8, i * P:(i + 1) * P], cT_bank, f32(act_hi[:, 6:8, i * P:(i + 1) * P]),
                                    ALU.subtract).then_inc(c_lo, 1)

            softmax(0)
            for k in range(N_ITEMS - 1):
                softmax(k + 1, k)
            for k in range(N_ITEMS - 1, N_ITEMS + 1):
                beside(k)
            dve.wait_ge(ob_sq, TT * BH)
            own.did(v.tensor_scalar(o_ss[:], o_ss[:], 1.0 / BV, LN_EPS, ALU.mult, ALU.add))
            v.reciprocal(o_ss[:], o_ss[:]).then_inc(ob_var, 1)
            dve.wait_ge(c_hi, TT)
            v.tensor_tensor(act_lo[:, 6:8, T - P:T], cT_bank, f32(act_hi[:, 6:8, T - P:T]), ALU.subtract)\
                .then_inc(c_lo, 1)
            dve.wait_ge(o_taken, 2 * TT)
            dve.wait_ge(ob_rstd, 1)
            for a in range(2):
                o4 = proj[:, 2 - 2 * a:4 - 2 * a, :].rearrange("p b (n e) -> p (b n) e", e=BV)
                r4 = o_ss[:, 4 * a:4 * a + 4, :].rearrange("p i h -> p (i h)")
                v.tensor_tensor(o4, o4, r4.unsqueeze(2).broadcast_to([P, 16, BV]), ALU.mult).then_inc(ob_normed, 1)

            def lo_plain(u):
                dve.wait_ge(hi_ready, 1 + u + 2)
                v.tensor_tensor(w_lo[u % 2][:], w_raw[u % 2][:], f32(w_hi[u % 2][:]), ALU.subtract)\
                    .then_inc(lo_ready, 1)

            lo_plain(U_OUT2)
            lo_plain(U_OUT2 + 1)
            for h in range(BH):
                dve.wait_ge(s_hi, SP_MIX + MIX_CHUNKS + h + 1)
                v.scalar_tensor_tensor(act_lo[:, 2 + h, :], bank[2 + h % 2][:], sub_gain[:], f32(act_hi[:, 2 + h, :]),
                                       ALU.mult, ALU.subtract).then_inc(s_lo, 1)

            dve.wait_ge(x_back, 16)
            dve.sem_inc(z_ready, 2)
            with loop(dve, KT // 2) as j:
                for r in range(2):
                    lo_next(U_OUT2, j, 2, r)
                    v.scalar_tensor_tensor(z[:, bass.ds(2 * j + r, 1), :].rearrange("p a t -> p (a t)"),
                                           x_res[:, bass.ds(2 * j + r, 1), :].rearrange("p a t -> p (a t)"),
                                           ALPHA, bank[r][:], ALU.mult, ALU.add).then_inc(z_ready, 1)

            def layer_norm_dve(q):
                pair = bank[2 - 2 * q]
                dve.wait_ge(mean_mm, q + 1)
                for k in range(KT):
                    v.scalar_tensor_tensor(z[:, k, :], pair[:], -1.0 / D, z[:, k, :], ALU.mult, ALU.add)\
                        .then_inc(xc_ready, 1)
                dve.wait_ge(xc_ready, (q + 1) * KT)
                dve.wait_ge(var_mm, q + 1)
                spread(bank[3 - 2 * q], LN_EPS, ln2_var, ln2_rstd, rstd2_diag, diag2_ready, q + 1)
                dve.wait_ge(rstd2_spread, 2 * q + 2)
                parts = [(0, T)] if q == 0 else [(0, HALF), (HALF, HALF)]
                for a, w in parts:
                    for k in range(KT):
                        v.scalar_tensor_tensor(z[:, k, a:a + w], z[:, k, a:a + w],
                                               params2[:, ROW2_LN[q] + k:ROW2_LN[q] + k + 1],
                                               pair[:, a:a + w], ALU.mult, ALU.mult).then_inc(ln_t, 1)

            dve.wait_ge(z_ready, 1 + KT + 1)
            layer_norm_dve(0)
            for k in range(KT):
                shift = params2[:, KT + k:KT + k + 1]
                dve.wait_ge(s_hi, SP_X1 + k + 1)
                v.scalar_tensor_tensor(act_lo[:, k, :], z[:, k, :], shift, f32(act_hi[:, k, :]),
                                       ALU.add, ALU.subtract).then_inc(s_lo, 1)
            dve.wait_ge(s_lo, SP_X1 + KT)
            for k in range(KT):
                shift = params2[:, KT + k:KT + k + 1]
                v.tensor_scalar(z[:, k, :], z[:, k, :], shift, ALPHA, ALU.add, ALU.mult).then_inc(acc_init, 1)
            dve.wait_ge(acc_init, KT)
            dve.sem_inc(acc_added, 2)
            for g, n in enumerate(GROUPS):
                last = g == len(GROUPS) - 1
                dve.wait_ge(unit_done, 1 + U_GROUP[g] + 1)
                with loop(dve, n) as j:
                    f = FG * g + j
                    lo_next(U_GROUP[g], j, 2, 0)
                    lo_next(U_GROUP[g], j, 2, 1)
                    dve.wait_ge(g_act, 1 + f + 1)
                    v.tensor_tensor(f_buf[:], silu_buf[:], bank[1][:], ALU.mult).then_inc(f_mul, 1)
                    dve.wait_ge(f_hi_done, f + 1)
                    v.tensor_tensor(f_lo[:, bass.ds(j, 1), :].rearrange("p a t -> p (a t)"), f_buf[:],
                                    f32(f_hi[:, bass.ds(j, 1), :].rearrange("p a t -> p (a t)")), ALU.subtract)\
                        .then_inc(f_lo_done, 1)
                    dve.wait_ge(f_lo_done, f + 1)

                def accumulate(d, r):
                    zz = z[:, bass.ds(d, 1), :].rearrange("p a t -> p (a t)")
                    v.tensor_tensor(zz, bank[2 + r][:], zz, ALU.add).then_inc(acc_added, 1)

                base = U_GROUP[g] + 2 * n
                if last:
                    with loop(dve, KT // 2 - 1) as j:
                        for r in range(2):
                            lo_next(base, j, 2, r)
                            accumulate(2 * j + r, r)
                    for r in range(2):
                        dve.wait_ge(unit_done, 1 + U_END + r)
                        accumulate(KT - 2 + r, r)
                else:
                    with loop(dve, KT // 2) as j:
                        for r in range(2):
                            lo_next(base, j, 2, r)
                            accumulate(2 * j + r, r)
                dve.wait_ge(acc_added, 1 + (g + 1) * KT + 1)
            layer_norm_dve(1)
            for t in range(TT // 2, TT):
                dve.wait_ge(outT_done, t + 1)
                v.tensor_copy(x_res[:, t, :], bank[OUT_PAIR[t % 3]][:]).then_inc(out_copied, 1)

        @block.tensor
        def _(pe):
            mm = nc.tensor.matmul
            pe.sem_inc(mixed, 1)
            pe.wait_ge(const_ready, 1)
            pe.wait_ge(par_loaded, 16 * 11)
            nc.tensor.transpose(bank[0][:, 0:N_ROWS], params_raw[0:N_ROWS, :], identity[0:N_ROWS, 0:N_ROWS])
            nc.tensor.transpose(bank[0][:, HALF:HALF + N_ROWS2], params2_raw[0:N_ROWS2, :],
                                identity[0:N_ROWS2, 0:N_ROWS2]).then_inc(par_T, 1)
            pe.wait_ge(x_loaded, 16)
            for k in range(KT):
                if k >= 2:
                    pe.wait_ge(xT_ready, k - 1)
                for t in range(TT):
                    i = nc.tensor.transpose(bank[1 + k % 2][:, t * P:(t + 1) * P], yT[:, t, k * P:(k + 1) * P],
                                            identity[:])
                i.then_inc(xT_done, 1)

            def feature_sums(src, out, first, last):
                for h in range(2):
                    i = mm(out[:, h * HALF:(h + 1) * HALF], ones[:], src[:, h * HALF:(h + 1) * HALF],
                           start=first, stop=last)
                return i

            def columns(src, out):
                for k in range(KT):
                    i = mm(out[:, k:k + 1], src[:, k * P:(k + 1) * P], ones[:, 0:1], start=True, stop=True)
                return i

            def spread(diag, out, ready, n, done):
                for h in range(2):
                    pe.wait_ge(ready, 2 * n + h + 1)
                    mm(out[:, h * HALF:(h + 1) * HALF], ones[:], diag[:, h * HALF:(h + 1) * HALF],
                       start=True, stop=True).then_inc(done, 1)

            def spread_rstd(n):
                spread(rstd_diag, bank[2], diag_ready, n, rstd_spread)

            def x_squares(n):
                for k in range(KT):
                    pe.wait_ge(sq_ready, 2 * n * KT + k + 1)
                    feature_sums(sqs[k % 2], bank[3], k == 0, k == KT - 1).then_inc(sq_taken, 1)
                pe.wait_ge(sq_taken, (n + 1) * KT)
                pe.sem_inc(stat_done, 1)

            x_squares(0)
            for s in range(ADA_EARLY):
                if s == ADA_EARLY - 1:
                    spread_rstd(0)
                pe.wait_ge(ada_used, (s + 1) * KT)
                columns(ada_sum[s], ada_cols[:, s * KT:(s + 1) * KT]).then_inc(ada_col, 1)
            pe.sem_inc(unit_done, 2)
            pe.sem_inc(late_col, 1)

            def product_two(u, split, order=range(KT), split_blocks=range(KT)):
                for r in range(2):
                    slot = (u + r) % 2
                    pe.wait_ge(hi_ready, 1 + u + r + 2)
                    pe.wait_ge(lo_ready, 1 + u + r + 2)
                    for k in order:
                        if r == 0 and k in split_blocks:
                            pe.wait_ge(s_hi, split + k + 1)
                        for w in (w_hi, w_lo):
                            for h in range(2):
                                mm(bank[r][:, h * HALF:(h + 1) * HALF], w[slot][:, k, :],
                                   act_hi[:, k, h * HALF:(h + 1) * HALF], start=(k == order[0] and w is w_hi), stop=False)
                for r in range(2):
                    slot = (u + r) % 2
                    for k in order:
                        if r == 0 and k in split_blocks:
                            pe.wait_ge(s_lo, split + k + 1)
                        for h in range(2):
                            i = mm(bank[r][:, h * HALF:(h + 1) * HALF], w_hi[slot][:, k, :],
                                   act_lo[:, k, h * HALF:(h + 1) * HALF], start=False, stop=(k == order[-1]))
                    i.then_inc(unit_done, 1)

            def product(u, slot, pair, split=None, kt=KT, hi=act_hi, lo=act_lo, sems=(s_hi, s_lo)):
                pe.wait_ge(hi_ready, 1 + u + 2)
                pe.wait_ge(lo_ready, 1 + u + 2)
                for k in range(kt):
                    if split is not None:
                        pe.wait_ge(sems[0], split + k + 1)
                        pe.wait_ge(sems[1], split + k + 1)
                    for w, a in ((w_hi, hi), (w_hi, lo), (w_lo, hi)):
                        for h in range(2):
                            i = mm(bank[pair][:, h * HALF:(h + 1) * HALF], w[slot][:, k, :],
                                   a[:, k, h * HALF:(h + 1) * HALF],
                                   start=(k == 0 and w is w_hi and a is hi), stop=(k == kt - 1 and w is w_lo))
                i.then_inc(unit_done, 1)

            def input_turn(l, j, first):
                n = CB * l + j
                u = l * UL + P1_ROLES * j
                pe.wait_ge(p_copied, 1 + n)
                pe.wait_ge(gp_done, 1 + n)
                if first:
                    product_two(u, 2 * l * KT)
                else:
                    product(u, 0, 0)
                    product(u + 1, 1, 1)
                pe.wait_ge(y_pool, 1 + n)
                product(u + 2, 0, 2)
                pe.wait_ge(gate_done, 1 + n)
                if l == 0:
                    pe.wait_ge(late_taken, 1 + j)
                product(u + 3, 1, 3)
                pe.wait_ge(u_copied, n + 1)
                product(u + 4, 0, 0)
                pe.wait_ge(c_used, 1 + n + 1)
                product(u + 5, 1, 1)
                pe.wait_ge(pooled, 1 + n + 1)
                pe.wait_ge(wpool_ready, n + 1)
                for h in range(2):
                    i = mm(bank[2][:, h * HALF:(h + 1) * HALF], wpool_now[:],
                           win_a[:, PAD + h * HALF:PAD + (h + 1) * HALF], start=True, stop=True)
                i.then_inc(mixed, 1)
                if l == 0:
                    pe.wait_ge(late_used, (j + 1) * KT)
                    pe.wait_ge(gate_done, 1 + n + 1)
                    columns(late_sum, bank[3]).then_inc(late_col, 1)

            for l in range(LAYERS):
                base = l * UL
                input_turn(l, 0, True)
                with loop(pe, CB - 1) as j:
                    input_turn(l, j + 1, False)
                pe.wait_ge(gp_done, 1 + CB * l + CB)
                pe.wait_ge(o_copied, 1 + KT * l + 1)
                product_two(base + P1_UNITS, (2 * l + 1) * KT)
                with loop(pe, KT // 2 - 1) as j:
                    for r in range(2):
                        pe.wait_ge(o_copied, 1 + KT * l + 2 * j + 2 + r)
                        product(base + P1_UNITS + 2 * j + 2 + r, r, r)
                pe.wait_ge(sq_added, 2 + (l + 1) * (KT - 1))
                pe.wait_ge(gate_done, 1 + CB * l + CB)
                if l == 0:
                    pe.wait_ge(late_taken, 1 + CB)
                feature_sums(sq_sum, bank[3], True, False)
                pe.wait_ge(sq_ready, (2 * l + 2) * KT)
                feature_sums(sqs[1], bank[3], False, True).then_inc(stat_done, 1)
                pe.wait_ge(y_pool, 1 + CB * l + CB)
                spread_rstd(2 * l + 1)
                if l < LAYERS - 1:
                    x_squares(l + 1)
                    spread_rstd(2 * l + 2)

            tr = nc.tensor.transpose
            pe.wait_ge(o_copied, 1 + KT * LAYERS + 1)
            pe.wait_ge(var_ready, 2 * LAYERS)
            product_two(U_IDX, SP_X)
            product(U_IDX + 2, 0, 2)
            pe.wait_ge(ik_copied, 1)
            for t in range(TT):
                i_ = tr(bank[3][:, t * 64:(t + 1) * 64], index_tmp[:, t * P:(t + 1) * P], identity[0:64, 0:64])
            i_.then_inc(iwT_done, 1)
            pe.wait_ge(iq_copied, 2)
            m = 0
            for i in range(SEL0, TT):
                for h in range(IH):
                    pe.wait_ge(relu_done, m)
                    if m < 4:
                        pe.wait_ge(ik_copied, m + 2)
                    at = slice(32 * (h % 4), 32 * (h % 4) + 32)
                    for a, w in pieces(keys(i)):
                        i_ = mm(bank[m % 2][:, a:a + w], proj[at, N_PROJ - 2 + h // 4, i * P:(i + 1) * P],
                                proj[at, N_PROJ - 3, a:a + w], start=True, stop=True)
                    i_.then_inc(score_mm, 1)
                    m += 1
            pe.wait_ge(relu_done, m + 1)
            def natural(n):
                b = NATURAL[n]
                if n >= 2:
                    pe.wait_ge(nat_copied, n - 1)
                for t in range(TT):
                    i_ = tr(bank[2 + n % 2][:, t * P:(t + 1) * P], proj[:, b, t * P:(t + 1) * P], identity[:])
                i_.then_inc(nat_done, 1)

            with loop(pe, N_PROJ // 2 - 1) as j:
                for r in range(2):
                    pe.wait_ge(p3_copied, 1 + 2 * j + r)
                    product(U_PROJ + 2 * j + r, (U_PROJ + r) % 2, r)
            pe.wait_ge(p3_copied, 1 + N_PROJ - 2 + 1)
            for n in range(N_EARLY):
                natural(n)
            for r in range(2):
                product(U_OUT2 - 2 + r, (U_OUT2 + r) % 2, r)
            pe.wait_ge(p3_copied, 1 + N_PROJ + 1)
            pe.wait_ge(gelu_done, 2)
            for n in range(N_EARLY, len(NATURAL)):
                natural(n)
            pe.wait_ge(dist_ready, 1)
            pe.wait_ge(q_scaled, len(Q_BLOCKS))

            def logits(item, m):
                i, it = divmod(item, ITEMS)
                if item:
                    pe.wait_ge(exp_done, 2 * item + m - 1)
                at = slice(64 * m, 64 * m + 64)
                if it < BH:
                    q, k, slope = PB_BQ + it, PB_BK + it, it
                else:
                    q, k, slope = PB_CQ + it - BH, PB_CK + it - BH, 2 * (it - BH) + m
                    if i >= SEL0:
                        pe.wait_ge(sel_done, i - SEL0 + 1)
                for a, w in pieces(keys(i)):
                    o = bank[m][:, a:a + w]
                    mm(o, slope_id[:, slope, :], dist_bias[:, (TT - 1 - i) * P + a:(TT - 1 - i) * P + a + w],
                       start=True, stop=False)
                    if it >= BH and i >= SEL0:
                        mm(o, one_id[:], sel_bias[:, sel_at(i) + a:sel_at(i) + a + w], start=False, stop=False)
                    i_ = mm(o, proj[at, q, i * P:(i + 1) * P], proj[at, k, a:a + w], start=False, stop=True)
                i_.then_inc(logits_done, 1)

            def turn(item, k):
                g, i = group(item, k), item // ITEMS
                pe.wait_ge(attn_ready, g + 1)
                if g:
                    pe.wait_ge(pT_copied, g)
                for t in range(i + 1):
                    i_ = tr(bank[2][:, t * P:(t + 1) * P], prob[2 * (item % 2) + k][:, t * P:(t + 1) * P],
                            identity[:])
                i_.then_inc(pT_done, 1)

            def values(item, k):
                g = group(item, k)
                i, it = divmod(item, ITEMS)
                pe.wait_ge(pT_copied, g + 1)
                if i:
                    pe.wait_ge(o_taken, 2 * i)
                for t in range(i + 1):
                    if it < BH:
                        o, w = bank[3][:, it * P:(it + 1) * P], proj[:, PB_BV + it, t * P:(t + 1) * P]
                    else:
                        c_ = (2 * (it - BH) + k) * CD
                        o = bank[3][:, HALF + c_:HALF + c_ + CD]
                        w = proj[:, PB_CV + it - BH, t * P + k * CD:t * P + (k + 1) * CD]
                    i_ = mm(o, probT[g % 2][:, t * P:(t + 1) * P], w, start=(t == 0), stop=(t == i))
                i_.then_inc(pv_done, 1)

            for m in range(2):
                logits(0, m)
            pe.wait_ge(gm_loaded, 16 * 7)
            pe.wait_ge(nat_copied, len(NATURAL))
            for g in range(AG):
                i_ = tr(bank[2][:, g * P:(g + 1) * P], ws_raw[:, g, :], identity[:])
            i_.then_inc(wsT_done, 1)
            pe.wait_ge(wsT_copied, 1)
            for k in range(N_ITEMS + 1):
                for m in range(2):
                    if k and m < groups_of(k - 1):
                        turn(k - 1, m)
                    if k + 1 < N_ITEMS:
                        logits(k + 1, m)
                    if k and m < groups_of(k - 1):
                        values(k - 1, m)
                if k > ITEMS and k % ITEMS == 1 or k == N_ITEMS:
                    i = TT - 1 if k == N_ITEMS else k // ITEMS - 1
                    pe.wait_ge(o_taken, 2 * i + 2)
                    if i:
                        pe.wait_ge(c_lo, i)
                    for b in range(2):
                        i_ = tr(cT_bank[:, b, :], c_nat[:, b * P:(b + 1) * P], identity[:])
                    i_.then_inc(cT_done, 1)
                if 0 <= k - MIX_AT - 8 < MIX_CHUNKS:
                    c_ = k - MIX_AT - 8
                    b, a = divmod(c_, 2)
                    pe.wait_ge(v_normed, 1)
                    if c_ >= 2:
                        pe.wait_ge(mix_ready, c_ - 1)
                    for gg in range(2):
                        for t in range(HALF // P):
                            tt = a * (HALF // P) + t
                            i_ = mm(bank[a][AD * gg:AD * (gg + 1), HALF + t * P:HALF + (t + 1) * P],
                                    v_nat[:, b, tt * P + AD * gg:tt * P + AD * (gg + 1)], wsT[:, 2 * b + gg, :],
                                    start=True, stop=True)
                    i_.then_inc(gm_done, 1)

            pe.wait_ge(ob_normed, 2)
            pe.wait_ge(c_lo, TT)
            for h in range(BH):
                if h >= 2:
                    pe.wait_ge(s_lo, SP_MIX + MIX_CHUNKS + h - 1)
                for i in range(TT):
                    i_ = tr(bank[2 + h % 2][:, i * P:(i + 1) * P], o_nat(i)[:, h * P:(h + 1) * P], identity[:])
                i_.then_inc(obT_done, 1)
            ob_at = SP_MIX + MIX_CHUNKS - 2
            product_two(U_OUT2, ob_at, order=(0, 1, 6, 7, 2, 3, 4, 5), split_blocks=range(2, 2 + BH))
            with loop(pe, KT // 2 - 1) as j:
                for r in range(2):
                    pe.wait_ge(z_ready, 1 + 2 * j + 2 + r)
                    product(U_OUT2 + 2 * j + 2 + r, (U_OUT2 + r) % 2, r)

            def layer_norm_pe(q):
                pair = bank[2 - 2 * q]
                pe.wait_ge(z_added, (q + 1) * (KT - 1))
                for a in range(2):
                    mm(pair[:, a * HALF:(a + 1) * HALF], ones[:], sum2[:, a * HALF:(a + 1) * HALF],
                       start=True, stop=False)
                if q == 0:
                    pe.wait_ge(z_ready, 2 + KT)
                else:
                    pe.wait_ge(acc_added, 2 + len(GROUPS) * KT)
                for a in range(2):
                    i_ = mm(pair[:, a * HALF:(a + 1) * HALF], ones[:], z[:, KT - 1, a * HALF:(a + 1) * HALF],
                            start=False, stop=True)
                i_.then_inc(mean_mm, 1)
                squares = bank[3 - 2 * q]
                for k in range(1, KT, 2):
                    pe.wait_ge(sq2_ready, q * KT + k + 1)
                    feature_sums(sqs2[1], squares, k == 1, False).then_inc(sq2_taken, 1)
                pe.wait_ge(sq2_added, (q + 1) * (KT // 2 - 1))
                feature_sums(sum2, squares, False, True).then_inc(var_mm, 1)
                spread(rstd2_diag, pair, diag2_ready, q, rstd2_spread)

            layer_norm_pe(0)
            pe.wait_ge(ln_t, 1)
            product_two(U_FFN, SP_X1)
            for g, n in enumerate(GROUPS):
                peeled = 1 if g == 0 else 0
                with loop(pe, n - peeled) as j:
                    f = FG * g + j + peeled
                    for r, pair_used in ((0, g_act), (1, f_mul)):
                        pe.wait_ge(pair_used, 1 + f)
                        product(U_GROUP[g] + 2 * (j + peeled) + r, (U_GROUP[g] + r) % 2, r)
                with loop(pe, KT // 2) as j:
                    for r in range(2):
                        pe.wait_ge(acc_added, 1 + g * KT + 2 * j + r)
                        product(U_GROUP[g] + 2 * n + 2 * j + r, (U_GROUP[g] + r) % 2, 2 + r,
                                split=FG * g if r == 0 else None, kt=n, hi=f_hi, lo=f_lo,
                                sems=(f_hi_done, f_lo_done))
            layer_norm_pe(1)
            for t in range(TT):
                pe.wait_ge(x_final, (1 + t // (TT // 2)) * KT)
                if t >= 3:
                    pe.wait_ge(out_copied, t - 2)
                for k in range(KT):
                    i_ = tr(bank[OUT_PAIR[t % 3]][:, k * P:(k + 1) * P], z[:, k, t * P:(t + 1) * P], identity[:])
                i_.then_inc(outT_done, 1)



_INS = ['x', 'c', 'w_ada', 'b_ada', 'g_pre', 'w_in', 'w_conv', 'w_pool', 'pool_scale', 'w_out', 'g_post', 'w_in_2',
        'gmlp_w_s_2', 'gmlp_b_s_2', 'gmlp_ln_g_2', 'gmlp_ln_b_2', 'lam_q1_2', 'lam_k1_2', 'lam_q2_2', 'lam_k2_2',
        'diff_subln_g_2', 'w_out_2', 'ln1_g_2', 'ln1_b_2', 'w_gu_2', 'w_down_2', 'ln2_g_2', 'ln2_b_2']


def kernel(**inputs):
    import numpy as np
    import concourse.bacc as bacc
    from concourse.bass_utils import run_bass_kernel_spmd

    nc = bacc.Bacc("TRN2", target_bir_lowering=False, num_devices=1)
    arrays, args = {}, []
    for name in _INS:
        a = np.ascontiguousarray(inputs[name])
        arrays[name] = a
        args.append(nc.dram_tensor(name, a.shape, mybir.dt.from_np(a.dtype), kind="ExternalInput").ap())
    out = nc.dram_tensor("out", (1, T, D), FP32, kind="ExternalOutput").ap()
    build(nc, *args, out)
    return run_bass_kernel_spmd(nc, [arrays], core_ids=[0]).results[0]["out"]
```
